# Optimizing a Trainium2 kernel written in Bass

```python
import math
import jax, jax.numpy as jnp
from jax import lax
import numpy as np

D_MODEL = 1024
BATCH = 1
SEQ = 256
DEPTH = 2

MLA_HEADS = 8
MLA_NOPE_DIM = 128
MLA_ROPE_DIM = 64
MLA_V_DIM = 128
MLA_Q_RANK = 384
MLA_KV_RANK = 256
ROPE_THETA = 10000.0
SWA_Q_HEADS = 16
SWA_KV_HEADS = 4
SWA_HEAD_DIM = 64
WINDOW = 128
REL_BUCKETS = 32
REL_MAX_DIST = 128
D_FF = 4 * D_MODEL
BLOCK = 128
LN_EPS = 1e-5
RMS_EPS = 1e-6


def _layernorm(x, g, b):
    xf = x.astype(jnp.float32)
    mu = xf.mean(-1, keepdims=True)
    var = jnp.square(xf - mu).mean(-1, keepdims=True)
    return ((xf - mu) * lax.rsqrt(var + LN_EPS) * g + b).astype(x.dtype)

def _rmsnorm(x, g):
    xf = x.astype(jnp.float32)
    return (xf * lax.rsqrt(jnp.mean(xf * xf, -1, keepdims=True) + RMS_EPS) * g).astype(x.dtype)

def _rope(x, pos):
    half = x.shape[-1] // 2
    inv = ROPE_THETA ** (-jnp.arange(half, dtype=jnp.float32) / half)
    ang = pos.astype(jnp.float32)[:, None] * inv[None, :]
    ang = ang.reshape(ang.shape[:1] + (1,) * (x.ndim - 3) + ang.shape[1:])
    cos, sin = jnp.cos(ang), jnp.sin(ang)
    xf = x.astype(jnp.float32)
    x1, x2 = xf[..., :half], xf[..., half:]
    return jnp.concatenate([x1 * cos - x2 * sin, x1 * sin + x2 * cos], -1).astype(x.dtype)

def _t5_bucket(dist):
    n = jnp.maximum(dist, 0)
    max_exact = REL_BUCKETS // 2
    nf = jnp.maximum(n, 1).astype(jnp.float32)
    large = max_exact + (jnp.log(nf / max_exact) / math.log(REL_MAX_DIST / max_exact)
                         * (REL_BUCKETS - max_exact)).astype(jnp.int32)
    large = jnp.minimum(large, REL_BUCKETS - 1)
    return jnp.where(n < max_exact, n, large)

def _to_blocks(t, nb):
    return t.reshape((t.shape[0], nb, BLOCK) + t.shape[2:]).swapaxes(0, 1)

def _mla(x, w_in, g_q, g_kv, w_uq, w_uk, w_uv, w_o, pos):
    B, S, _ = x.shape
    nb = S // BLOCK
    h = x @ w_in
    c_q = _rmsnorm(h[..., :MLA_Q_RANK], g_q)
    c_kv = _rmsnorm(h[..., MLA_Q_RANK:MLA_Q_RANK + MLA_KV_RANK], g_kv)
    k_r = _rope(h[..., MLA_Q_RANK + MLA_KV_RANK:], pos)
    q = jnp.einsum('bsr,rhd->bshd', c_q, w_uq)
    q_n = q[..., :MLA_NOPE_DIM]
    q_r = _rope(q[..., MLA_NOPE_DIM:], pos)
    q_lat = jnp.einsum('bshn,chn->bshc', q_n, w_uk)
    scale = (MLA_NOPE_DIM + MLA_ROPE_DIM) ** -0.5
    kpos = jnp.arange(S)

    def block(args):
        ql, qr, i = args
        s = (jnp.einsum('bqhc,bkc->bhqk', ql, c_kv)
             + jnp.einsum('bqhr,bkr->bhqk', qr, k_r)).astype(jnp.float32) * scale
        qpos = i * BLOCK + jnp.arange(BLOCK)
        s = jnp.where(kpos[None, :] <= qpos[:, None], s, -jnp.inf)
        p = jax.nn.softmax(s, axis=-1).astype(x.dtype)
        return jnp.einsum('bhqk,bkc->bqhc', p, c_kv)

    o_lat = lax.map(block, (_to_blocks(q_lat, nb), _to_blocks(q_r, nb), jnp.arange(nb)))
    o_lat = o_lat.swapaxes(0, 1).reshape(B, S, MLA_HEADS, MLA_KV_RANK)
    o = jnp.einsum('bshc,chv->bshv', o_lat, w_uv).reshape(B, S, MLA_HEADS * MLA_V_DIM)
    return o @ w_o

def _shared_kv(x, w_kv):
    B, S, _ = x.shape
    nb = S // BLOCK
    kv = (x @ w_kv).reshape(B, nb, BLOCK, 2, SWA_KV_HEADS, SWA_HEAD_DIM)
    k, v = kv[:, :, :, 0], kv[:, :, :, 1]

    def band(t):
        prev = jnp.pad(t, ((0, 0), (1, 0), (0, 0), (0, 0), (0, 0)))[:, :-1]
        return jnp.concatenate([prev, t], axis=2)

    return band(k), band(v)

def _swa(x, w_q, sinks, w_o, k_band, v_band, rel_bias):
    B, S, _ = x.shape
    nb = S // BLOCK
    G = SWA_Q_HEADS // SWA_KV_HEADS
    q = (x @ w_q).reshape(B, nb, BLOCK, SWA_KV_HEADS, G, SWA_HEAD_DIM)
    s = jnp.einsum('bnqkgd,bnjkd->bnkgqj', q, k_band).astype(jnp.float32) * SWA_HEAD_DIM ** -0.5
    i = jnp.arange(BLOCK)
    j = jnp.arange(2 * BLOCK)
    dist = i[:, None] + BLOCK - j[None, :]
    bias = rel_bias[_t5_bucket(dist)].astype(jnp.float32)
    bias = bias.transpose(2, 0, 1).reshape(SWA_KV_HEADS, G, BLOCK, 2 * BLOCK)
    kpos = jnp.arange(nb)[:, None] * BLOCK - BLOCK + j[None, :]
    valid = (dist >= 0) & (dist < WINDOW)
    mask = valid[None] & (kpos >= 0)[:, None, :]
    s = jnp.where(mask[None, :, None, None], s + bias, -jnp.inf)
    sink = sinks.astype(jnp.float32).reshape(SWA_KV_HEADS, G)[..., None]
    m = jnp.maximum(s.max(-1), sink)
    p = jnp.exp(s - m[..., None])
    denom = p.sum(-1) + jnp.exp(sink - m)
    p = (p / denom[..., None]).astype(x.dtype)
    o = jnp.einsum('bnkgqj,bnjkd->bnqkgd', p, v_band).reshape(B, S, SWA_Q_HEADS * SWA_HEAD_DIM)
    return o @ w_o

def _mlp(x, w_up, w_down):
    h = jax.nn.relu(x @ w_up)
    return (h * h) @ w_down

def first_inputs(seed: int = 0) -> dict:
    key = jax.random.key(seed)
    ks = jax.random.split(key, 20)
    n_a = DEPTH // 2
    n_b = DEPTH - n_a
    beta = (8 * DEPTH) ** -0.25
    f32 = jnp.float32

    def nrm(k, shape, fan_in, gain=1.0):
        return jax.random.normal(k, shape, f32) * (gain * fan_in ** -0.5)

    in_w = MLA_Q_RANK + MLA_KV_RANK + MLA_ROPE_DIM
    kv_k = nrm(ks[8], (D_MODEL, 1, SWA_KV_HEADS * SWA_HEAD_DIM), D_MODEL)
    kv_v = nrm(ks[9], (D_MODEL, 1, SWA_KV_HEADS * SWA_HEAD_DIM), D_MODEL, beta)
    return {
        'x': jax.random.normal(ks[0], (BATCH, SEQ, D_MODEL), f32),
        'mla_w_in': nrm(ks[1], (n_a, D_MODEL, in_w), D_MODEL),
        'mla_g_q': 1.0 + 0.05 * jax.random.normal(ks[2], (n_a, MLA_Q_RANK), f32),
        'mla_g_kv': 1.0 + 0.05 * jax.random.normal(ks[3], (n_a, MLA_KV_RANK), f32),
        'mla_w_uq': nrm(ks[4], (n_a, MLA_Q_RANK, MLA_HEADS, MLA_NOPE_DIM + MLA_ROPE_DIM), MLA_Q_RANK),
        'mla_w_uk': nrm(ks[5], (n_a, MLA_KV_RANK, MLA_HEADS, MLA_NOPE_DIM), MLA_KV_RANK),
        'mla_w_uv': nrm(ks[6], (n_a, MLA_KV_RANK, MLA_HEADS, MLA_V_DIM), MLA_KV_RANK, beta),
        'mla_w_o': nrm(ks[7], (n_a, MLA_HEADS * MLA_V_DIM, D_MODEL), MLA_HEADS * MLA_V_DIM, beta),
        'kv_w_shared': jnp.concatenate([kv_k, kv_v], axis=1).reshape(D_MODEL, 2 * SWA_KV_HEADS * SWA_HEAD_DIM),
        'swa_w_q': nrm(ks[10], (n_b, D_MODEL, SWA_Q_HEADS * SWA_HEAD_DIM), D_MODEL),
        'swa_sinks': 0.5 * jax.random.normal(ks[11], (n_b, SWA_Q_HEADS), f32),
        'swa_w_o': nrm(ks[12], (n_b, SWA_Q_HEADS * SWA_HEAD_DIM, D_MODEL), SWA_Q_HEADS * SWA_HEAD_DIM, beta),
        'rel_bias': 0.5 * jax.random.normal(ks[13], (REL_BUCKETS, SWA_Q_HEADS), f32),
        'mlp_w_up': nrm(ks[14], (DEPTH, D_MODEL, D_FF), D_MODEL),
        'mlp_w_down': nrm(ks[15], (DEPTH, D_FF, D_MODEL), D_FF, beta),
        'ln_mix_g': 1.0 + 0.05 * jax.random.normal(ks[16], (DEPTH, D_MODEL), f32),
        'ln_mix_b': 0.02 * jax.random.normal(ks[17], (DEPTH, D_MODEL), f32),
        'ln_mlp_g': 1.0 + 0.05 * jax.random.normal(ks[18], (DEPTH, D_MODEL), f32),
        'ln_mlp_b': 0.02 * jax.random.normal(ks[19], (DEPTH, D_MODEL), f32),
    }

def first_block(x, mla_w_in, mla_g_q, mla_g_kv, mla_w_uq, mla_w_uk, mla_w_uv, mla_w_o,
              kv_w_shared, swa_w_q, swa_sinks, swa_w_o, rel_bias,
              mlp_w_up, mlp_w_down, ln_mix_g, ln_mix_b, ln_mlp_g, ln_mlp_b):
    alpha = (2 * DEPTH) ** 0.25
    n_a = DEPTH // 2
    pos = jnp.arange(x.shape[1])
    k_band = v_band = None
    for l in range(DEPTH):
        if l < n_a:
            y = _mla(x, mla_w_in[l], mla_g_q[l], mla_g_kv[l], mla_w_uq[l], mla_w_uk[l],
                     mla_w_uv[l], mla_w_o[l], pos)
        else:
            if l == n_a:
                k_band, v_band = _shared_kv(x, kv_w_shared)
            b = l - n_a
            y = _swa(x, swa_w_q[b], swa_sinks[b], swa_w_o[b], k_band, v_band, rel_bias)
        x = _layernorm(alpha * x + y, ln_mix_g[l], ln_mix_b[l])
        x = _layernorm(alpha * x + _mlp(x, mlp_w_up[l], mlp_w_down[l]), ln_mlp_g[l], ln_mlp_b[l])
    return x


DEPTH_2 = 1

RWKV_HEADS = 8
RWKV_HD = 64
RWKV_W = RWKV_HEADS * RWKV_HD
DECAY_LORA = 64
ICLR_LORA = 64
VRES_LORA = 32
GATE_LORA = 128
LNX_EPS = 64e-5
SB_HEADS = 8
SB_HD = 64
SB_W = SB_HEADS * SB_HD
SB_BLOCK = 128
MEM_LEN = 256
MEM_HEADS = 4
MEM_HD = 128
MEM_W = MEM_HEADS * MEM_HD
N_BRANCH = 3
BRANCH_W = 512
D_FF_2 = 2816
CONV_W = 3
NORM_EPS = 1e-6

RWKV_SPLITS = (RWKV_W, RWKV_W, RWKV_W, DECAY_LORA, ICLR_LORA, GATE_LORA)
RWKV_COLS = sum(RWKV_SPLITS)
IN_COLS = RWKV_COLS + 3 * SB_W + MEM_W + N_BRANCH * D_MODEL


def rms_norm(x, g, eps=NORM_EPS):
    xf = x.astype(jnp.float32)
    y = xf * lax.rsqrt(jnp.mean(xf * xf, axis=-1, keepdims=True) + eps)
    return (y * g.astype(jnp.float32)).astype(x.dtype)

def split_heads(t, h, d):
    return t.reshape(t.shape[:-1] + (h, d))

def token_shift(p, mu):
    prev = jnp.pad(p, ((0, 0), (1, 0), (0, 0)))[:, :-1]
    return p + (prev - p) * mu

def rwkv7_recurrence(r, decay, k, v, kk, a):
    b, t, h, n = r.shape
    xs = tuple(jnp.moveaxis(z, 1, 0) for z in (r, decay, k, v, kk, a))

    def step(S, inp):
        r_t, w_t, k_t, v_t, kk_t, a_t = inp
        sa = jnp.einsum('bhij,bhj->bhi', S, -kk_t)
        S = (S * w_t[:, :, None, :]
             + sa[..., None] * (kk_t * a_t)[:, :, None, :]
             + v_t[..., None] * k_t[:, :, None, :])
        y_t = jnp.einsum('bhij,bhj->bhi', S, r_t)
        return S, y_t

    S0 = jnp.zeros((b, h, n, n), jnp.float32)
    _, ys = lax.scan(step, S0, xs)
    return jnp.moveaxis(ys, 0, 1)

def rwkv7_branch(p, mu, w0, w2, a0, a2, g2, k_k, k_a, r_k, lnx_g, lnx_b, v_first, vres):
    dt = p.dtype
    p = token_shift(p, mu)
    idx = list(np.cumsum(RWKV_SPLITS)[:-1])
    r, k, v, wl, al, gl = jnp.split(p, idx, axis=-1)
    f32 = jnp.float32
    w = -jax.nn.softplus(-(w0 + jnp.tanh(wl) @ w2).astype(f32)) - 0.5
    decay = jnp.exp(-jnp.exp(w))
    a = jax.nn.sigmoid((a0 + al @ a2).astype(f32))
    g = jax.nn.sigmoid(gl) @ g2
    if vres is None:
        v_first = v
    else:
        v0, v1, v2 = vres
        v = v + (v_first - v) * jax.nn.sigmoid(v0 + (v @ v1) @ v2)
    kk = split_heads((k * k_k).astype(f32), RWKV_HEADS, RWKV_HD)
    kk = kk / jnp.maximum(jnp.sqrt(jnp.sum(kk * kk, axis=-1, keepdims=True)), 1e-12)
    k = k.astype(f32) * (1.0 + (a - 1.0) * k_a.astype(f32))
    rh = split_heads(r.astype(f32), RWKV_HEADS, RWKV_HD)
    kh = split_heads(k, RWKV_HEADS, RWKV_HD)
    vh = split_heads(v.astype(f32), RWKV_HEADS, RWKV_HD)
    ah = split_heads(a, RWKV_HEADS, RWKV_HD)
    dh = split_heads(decay, RWKV_HEADS, RWKV_HD)
    y = rwkv7_recurrence(rh, dh, kh, vh, kk, ah)
    mean = jnp.mean(y, axis=-1, keepdims=True)
    var = jnp.mean(jnp.square(y - mean), axis=-1, keepdims=True)
    y = (y - mean) * lax.rsqrt(var + LNX_EPS)
    y = y.reshape(y.shape[:2] + (RWKV_W,)) * lnx_g.astype(f32) + lnx_b.astype(f32)
    bonus = jnp.sum(rh * kh * r_k.astype(f32), axis=-1, keepdims=True) * vh
    y = (y + bonus.reshape(y.shape)) * g.astype(f32)
    return y.astype(dt), v_first

def stick_breaking_attention(q, k, v):
    t_len = q.shape[2]
    scale = SB_HD ** -0.5
    outs = []
    for blk in range(t_len // SB_BLOCK):
        start = blk * SB_BLOCK
        end = start + SB_BLOCK
        qb = q[:, :, start:end]
        kb = k[:, :, :end]
        vb = v[:, :, :end]
        z = jnp.einsum('bhqd,bhkd->bhqk', qb, kb).astype(jnp.float32) * scale
        t_idx = start + jnp.arange(SB_BLOCK)
        s_idx = jnp.arange(end)
        mask = s_idx[None, :] < t_idx[:, None]
        log_1mb = jnp.where(mask, jax.nn.log_sigmoid(-z), 0.0)
        log_between = lax.cumsum(log_1mb, axis=3, reverse=True) - log_1mb
        attn = jnp.where(mask, jnp.exp(jax.nn.log_sigmoid(z) + log_between), 0.0)
        outs.append(jnp.einsum('bhqk,bhkd->bhqd', attn.astype(v.dtype), vb))
    return jnp.concatenate(outs, axis=2)

def stick_breaking_branch(p, q_g, k_g):
    b, t, _ = p.shape
    q, k, v = jnp.split(p, 3, axis=-1)
    q = rms_norm(split_heads(q, SB_HEADS, SB_HD), q_g).transpose(0, 2, 1, 3)
    k = rms_norm(split_heads(k, SB_HEADS, SB_HD), k_g).transpose(0, 2, 1, 3)
    v = split_heads(v, SB_HEADS, SB_HD).transpose(0, 2, 1, 3)
    o = stick_breaking_attention(q, k, v)
    return o.transpose(0, 2, 1, 3).reshape(b, t, SB_W)

def memory_branch(q, mem, mem_g, w_kv, q_g, k_g):
    b, t, _ = q.shape
    kv = rms_norm(mem, mem_g) @ w_kv
    mk, mv = jnp.split(kv, 2, axis=-1)
    qh = rms_norm(split_heads(q, MEM_HEADS, MEM_HD), q_g)
    kh = rms_norm(split_heads(mk, MEM_HEADS, MEM_HD), k_g)
    vh = split_heads(mv, MEM_HEADS, MEM_HD)
    s = jnp.einsum('bthd,bmhd->bhtm', qh, kh).astype(jnp.float32) * (MEM_HD ** -0.5)
    pr = jax.nn.softmax(s, axis=-1).astype(vh.dtype)
    o = jnp.einsum('bhtm,bmhd->bthd', pr, vh)
    return o.reshape(b, t, MEM_W)

def conv_ffn(x, g, w_up, conv_w, conv_b, w_down):
    h = rms_norm(x, g) @ w_up
    t = h.shape[1]
    hp = jnp.pad(h, ((0, 0), (CONV_W - 1, 0), (0, 0)))
    acc = conv_b + hp[:, 0:t] * conv_w[0]
    for i in range(1, CONV_W):
        acc = acc + hp[:, i:i + t] * conv_w[i]
    gate, val = jnp.split(acc, 2, axis=-1)
    return (jax.nn.silu(gate) * val) @ w_down

def second_inputs(seed: int = 0) -> dict:
    key = jax.random.key(seed)
    ks = jax.random.split(key, 40)
    f32 = jnp.float32
    nrm = lambda k, s, sc: jax.random.normal(k, s, f32) * sc
    gain = lambda k, s: 1.0 + 0.05 * jax.random.normal(k, s, f32)
    L = DEPTH_2
    return {
        "x": nrm(ks[0], (BATCH, SEQ, D_MODEL), 1.0),
        "mem": nrm(ks[1], (BATCH, MEM_LEN, D_MODEL), 1.0),
        "norm1_g": gain(ks[2], (L, D_MODEL)),
        "w_in": nrm(ks[3], (L, D_MODEL, IN_COLS), D_MODEL ** -0.5),
        "shift_mu": jax.random.uniform(ks[4], (L, RWKV_COLS), f32, 0.0, 1.0),
        "decay_w0": jax.random.uniform(ks[5], (L, RWKV_W), f32, -6.0, 1.0),
        "decay_w2": nrm(ks[6], (L, DECAY_LORA, RWKV_W), 0.5 * DECAY_LORA ** -0.5),
        "iclr_a0": nrm(ks[7], (L, RWKV_W), 0.1),
        "iclr_a2": nrm(ks[8], (L, ICLR_LORA, RWKV_W), ICLR_LORA ** -0.5),
        "gate_g2": nrm(ks[9], (L, GATE_LORA, RWKV_W), GATE_LORA ** -0.5),
        "k_k": 0.85 + 0.05 * jax.random.normal(ks[10], (L, RWKV_W), f32),
        "k_a": gain(ks[11], (L, RWKV_W)),
        "r_k": nrm(ks[12], (L, RWKV_HEADS, RWKV_HD), 0.1),
        "lnx_g": gain(ks[13], (L, RWKV_W)),
        "lnx_b": nrm(ks[14], (L, RWKV_W), 0.02),
        "vres_v0": 1.0 + 0.1 * jax.random.normal(ks[15], (L - 1, RWKV_W), f32),
        "vres_v1": nrm(ks[16], (L - 1, RWKV_W, VRES_LORA), RWKV_W ** -0.5),
        "vres_v2": nrm(ks[17], (L - 1, VRES_LORA, RWKV_W), VRES_LORA ** -0.5),
        "sb_q_norm_g": gain(ks[18], (L, SB_HD)),
        "sb_k_norm_g": gain(ks[19], (L, SB_HD)),
        "mem_norm_g": gain(ks[20], (L, D_MODEL)),
        "w_mem_kv": nrm(ks[21], (L, D_MODEL, 2 * MEM_W), D_MODEL ** -0.5),
        "mem_q_norm_g": gain(ks[22], (L, MEM_HD)),
        "mem_k_norm_g": gain(ks[23], (L, MEM_HD)),
        "w_branch": nrm(ks[24], (L, N_BRANCH, BRANCH_W, D_MODEL), BRANCH_W ** -0.5),
        "w_out": nrm(ks[25], (L, D_MODEL, D_MODEL), D_MODEL ** -0.5),
        "norm2_g": gain(ks[26], (L, D_MODEL)),
        "w_up": nrm(ks[27], (L, D_MODEL, 2 * D_FF_2), D_MODEL ** -0.5),
        "conv_w": nrm(ks[28], (L, CONV_W, 2 * D_FF_2), CONV_W ** -0.5),
        "conv_b": nrm(ks[29], (L, 2 * D_FF_2), 0.02),
        "w_down": nrm(ks[30], (L, D_FF_2, D_MODEL), D_FF_2 ** -0.5),
    }

def second_block(x, mem, norm1_g, w_in, shift_mu, decay_w0, decay_w2, iclr_a0, iclr_a2, gate_g2,
              k_k, k_a, r_k, lnx_g, lnx_b, vres_v0, vres_v1, vres_v2, sb_q_norm_g, sb_k_norm_g,
              mem_norm_g, w_mem_kv, mem_q_norm_g, mem_k_norm_g, w_branch, w_out, norm2_g,
              w_up, conv_w, conv_b, w_down):
    b, t, _ = x.shape
    cut = [RWKV_COLS, RWKV_COLS + 3 * SB_W, RWKV_COLS + 3 * SB_W + MEM_W]
    v_first = None
    for l in range(DEPTH_2):
        h = rms_norm(x, norm1_g[l])
        proj = h @ w_in[l]
        p_rwkv, p_sb, q_mem, gate_logits = jnp.split(proj, cut, axis=-1)
        vres = None if l == 0 else (vres_v0[l - 1], vres_v1[l - 1], vres_v2[l - 1])
        y_a, v_first = rwkv7_branch(p_rwkv, shift_mu[l], decay_w0[l], decay_w2[l], iclr_a0[l],
                                    iclr_a2[l], gate_g2[l], k_k[l], k_a[l], r_k[l], lnx_g[l],
                                    lnx_b[l], v_first, vres)
        y_b = stick_breaking_branch(p_sb, sb_q_norm_g[l], sb_k_norm_g[l])
        y_m = memory_branch(q_mem, mem, mem_norm_g[l], w_mem_kv[l], mem_q_norm_g[l], mem_k_norm_g[l])
        ys = jnp.stack([y_a, y_b.astype(y_a.dtype), y_m.astype(y_a.dtype)], axis=2)
        branch_out = jnp.einsum('btnc,ncd->btnd', ys, w_branch[l])
        gates = jax.nn.sigmoid(gate_logits.reshape(b, t, N_BRANCH, D_MODEL))
        merged = jnp.sum(gates * branch_out, axis=2)
        x = x + merged @ w_out[l]
        x = x + conv_ffn(x, norm2_g[l], w_up[l], conv_w[l], conv_b[l], w_down[l])
    return x


def setup_inputs(seed=0):
    out = dict(first_inputs(seed))
    for name, value in second_inputs(seed + 1).items():
        if name != "x":
            out[name + "_2"] = value
    return out


def reference(
    x, mla_w_in, mla_g_q, mla_g_kv, mla_w_uq, mla_w_uk, mla_w_uv, mla_w_o, kv_w_shared, swa_w_q,
    swa_sinks, swa_w_o, rel_bias, mlp_w_up, mlp_w_down, ln_mix_g, ln_mix_b, ln_mlp_g, ln_mlp_b,
    mem_2, norm1_g_2, w_in_2, shift_mu_2, decay_w0_2, decay_w2_2, iclr_a0_2, iclr_a2_2,
    gate_g2_2, k_k_2, k_a_2, r_k_2, lnx_g_2, lnx_b_2, vres_v0_2, vres_v1_2, vres_v2_2,
    sb_q_norm_g_2, sb_k_norm_g_2, mem_norm_g_2, w_mem_kv_2, mem_q_norm_g_2, mem_k_norm_g_2,
    w_branch_2, w_out_2, norm2_g_2, w_up_2, conv_w_2, conv_b_2, w_down_2,
):
    x = first_block(
        x, mla_w_in, mla_g_q, mla_g_kv, mla_w_uq, mla_w_uk, mla_w_uv, mla_w_o, kv_w_shared,
        swa_w_q, swa_sinks, swa_w_o, rel_bias, mlp_w_up, mlp_w_down, ln_mix_g, ln_mix_b,
        ln_mlp_g, ln_mlp_b,
    )
    return second_block(
        x, mem_2, norm1_g_2, w_in_2, shift_mu_2, decay_w0_2, decay_w2_2, iclr_a0_2, iclr_a2_2,
        gate_g2_2, k_k_2, k_a_2, r_k_2, lnx_g_2, lnx_b_2, vres_v0_2, vres_v1_2, vres_v2_2,
        sb_q_norm_g_2, sb_k_norm_g_2, mem_norm_g_2, w_mem_kv_2, mem_q_norm_g_2, mem_k_norm_g_2,
        w_branch_2, w_out_2, norm2_g_2, w_up_2, conv_w_2, conv_b_2, w_down_2,
    )


_drawn_inputs = setup_inputs


def setup_inputs(seed=0):
    import zlib

    import numpy as np

    out = dict(_drawn_inputs(seed))
    spreads = {}
    factors = {'mla_g_q': 8.0,
     'mla_g_kv': 8.0,
     'swa_sinks': 8.0,
     'rel_bias': 2.961,
     'decay_w2_2': 5.208,
     'iclr_a0_2': 5.442,
     'k_k_2': 29.912,
     'k_a_2': 2.762,
     'lnx_g_2': 17.054,
     'lnx_b_2': 43.788,
     'sb_q_norm_g_2': 17.772,
     'sb_k_norm_g_2': 30.365,
     'mem_norm_g_2': 8.0,
     'mem_q_norm_g_2': 8.0,
     'mem_k_norm_g_2': 8.0,
     'conv_b_2': 14.636,
     'r_k_2': 2.697,
     'norm2_g_2': 5.653}
    for name, (base, spread) in spreads.items():
        noise = np.random.default_rng([zlib.crc32(name.encode()), seed]).standard_normal(out[name].shape)
        drawn = base * np.exp(spread * noise) if base else spread * noise
        out[name] = __import__('jax').numpy.asarray(drawn.astype(out[name].dtype))
    for name, factor in factors.items():
        out[name] = (out[name] * factor).astype(out[name].dtype)
    return out
```

```python
import math
from contextlib import ExitStack, contextmanager

import numpy as np
import concourse.bass as bass
from concourse import mybir

F32 = mybir.dt.float32
F32R = mybir.dt.float32r
BF16 = mybir.dt.bfloat16
ACT = mybir.ActivationFunctionType
ALU = mybir.AluOpType
AX = mybir.AxisListType

P = 128
T = 256
D = 1024
DC = D // P
NEG = -1.0e30

MLA_H, Q_RANK, KV_RANK, NOPE, ROPE, VD = 8, 384, 256, 128, 64, 128
SWA_H, SWA_KV, SWA_D = 16, 4, 64
DFF = 4096
FC = DFF // P
RW_W, RW_H, RW_D = 512, 8, 64
DFF2 = 2816
FC2 = DFF2 // P
LN_EPS, RMS_EPS, LNX_EPS = 1e-5, 1e-6, 64e-5
ALPHA = (2 * 2) ** 0.25
RING = 4
AHEAD = 3

STREAM = [("in", 7), ("memk", 4), ("q", 6), ("uk", 2), ("uv", 2), ("wo", 8), ("memv", 4), ("mlp0", 2 * FC),
          ("swaq", 8), ("swak", 2), ("swav", 2), ("swao", 8), ("mlp1", 2 * FC), ("rwkv", 14), ("sbqk", 8),
          ("sbv", 4), ("memq", 4), ("gate", 24), ("branch", 12), ("out", 8), ("ffn", 3 * FC2)]
SLOT = {}
NSLOT = 0
for _name, _n in STREAM:
    SLOT[_name] = NSLOT
    NSLOT += _n

PARAMS = [("g_q", 3), ("g_kv", 2), ("ln_mix_g", 16), ("ln_mix_b", 16), ("ln_mlp_g", 16), ("ln_mlp_b", 16),
          ("norm1", 8), ("mu", 14), ("w0", 4), ("a0", 4), ("k_k", 4), ("k_a", 4), ("r_k", 4), ("lnx_g", 4),
          ("lnx_b", 4), ("sbq_g", 1), ("sbk_g", 1), ("mem_g", 8), ("memq_g", 1), ("memk_g", 1), ("norm2", 8),
          ("conv0", 44), ("conv1", 44), ("conv2", 44), ("conv_b", 44), ("sinks", 16)]
PCOL = {}
NPAR = 0
for _name, _n in PARAMS:
    PCOL[_name] = NPAR
    NPAR += _n

CONSTS = [("ident", 128), ("ones", 128), ("blockones", 128), ("later", 128), ("causal", 384), ("cos", 256),
          ("sin", 256), ("before", 128), ("upto", 128), ("level", 7 * 128), ("level0t", 128)]
CCOL = {}
NCON = 0
for _name, _n in CONSTS:
    CCOL[_name] = NCON
    NCON += _n


def constants():
    i = np.arange(P)
    row, col = i[:, None], i[None, :]
    c = {"ident": np.eye(P), "ones": np.ones((P, P)), "blockones": (row // 64 == col // 64)}
    c["later"] = row > col
    future = np.where(col > row, NEG, 0.0)
    c["causal"] = np.concatenate([future, np.zeros((P, P)), future], 1)
    half = ROPE // 2
    inv = np.float32(10000.0) ** (-np.arange(half, dtype=np.float32) / np.float32(half))
    ang = (np.arange(T, dtype=np.float32)[None, :] * inv[:, None]).astype(np.float32)
    c["cos"] = np.tile(np.cos(ang), (4, 1))
    c["sin"] = np.tile(np.concatenate([-np.sin(ang), np.sin(ang)], 0), (2, 1))
    c["before"] = row < col
    c["upto"] = row <= col
    levels = []
    for l in range(7):
        b = 1 << l
        levels.append((row // (2 * b) == col // (2 * b)) & (row // b % 2 == 0) & (col // b % 2 == 1))
    c["level"] = np.concatenate(levels, 1)
    c["level0t"] = levels[0].T
    dist = np.arange(384) - 127
    ok = (dist >= 0) & (dist < 128)
    n = np.maximum(dist, 0)
    nf = np.maximum(n, 1).astype(np.float32)
    large = 16 + (np.log(nf / np.float32(16)) / np.float32(math.log(8)) * np.float32(16)).astype(np.int32)
    bucket = np.where(n < 16, n, np.minimum(large, 31))
    onehot = np.zeros((P, 384))
    onehot[:32] = (bucket[None, :] == np.arange(32)[:, None]) & ok[None, :]
    out = np.zeros((P, NCON), np.float32)
    for name, n_ in CONSTS:
        out[:, CCOL[name]:CCOL[name] + n_] = c[name]
    band = np.zeros((32, 2, 384), np.float32)
    band[:, 0] = onehot[:32]
    band[:, 1] = np.where(ok, 0.0, NEG)[None, :]
    return out, band


class Tally:

    def __init__(self, engine, sem):
        self.engine, self.sem, self.n, self.i, self.per = engine, sem, 0, None, 0

    def value(self, n):
        return n if self.i is None else self.i * self.per + n

    def link(self, ins):
        ins.then_inc(self.sem, 1)
        self.n += 1
        self.engine.wait_ge(self.sem, self.value(self.n))

    def enter(self, i, per):
        self.i, self.per, self.at = i, per, self.n

    def leave(self, times):
        assert self.n - self.at == self.per, (self.n - self.at, self.per)
        self.n = self.at + self.per * times
        self.i = None



def pipeline(steps):
    kinds, heads = steps
    return [(kind, t - lag) for t in range(heads + kinds[-1][1] + 1) for kind, lag in kinds
            if 0 <= t - lag < heads and (kind != "opair" or (t - lag) % 2)]


MLA_STEPS = ([("s", 0), ("t", 2), ("o", 3), ("u", 4)], MLA_H)
SWA_STEPS = ([("s", 0), ("t", 2), ("opair", 3)], SWA_H)
MEM_STEPS = ([("s", 0), ("t", 2), ("o", 3)], 4)

RESULTS = []
KAPPA = math.exp(-0.5)
SWA_ORDER = [h for a in (0, 8) for c in range(4) for h in (a + c, a + 4 + c)]


def _results(stage, names):
    RESULTS.extend((stage, n) for n in names)


_results("brow", [0])
_results("in", range(4))
_results("memstat", [0])
_results("in", range(4, 7))
_results("mlastat", [0])
_results("memk", range(4))
_results("ckvt", [0])
_results("q", range(16))
_results("qlat", range(8))
_results("mla", pipeline(MLA_STEPS))
_results("wo", range(8))
_results("ln0", range(2))
_results("memv", range(2))
_results("mlp0", range(FC))
_results("ln1", range(2))
_results("swaq", range(8))
_results("swak", range(2))
_results("swav", range(2))
_results("swa", pipeline(SWA_STEPS))
_results("swao", range(8))
_results("ln2", range(2))
_results("mlp1", range(FC))
_results("ln3", range(2))
_results("rms1", [0])
_results("rwkv", range(14))
_results("loraw", range(2))
_results("loraa", range(2))
_results("kknorm", range(2))
_results("bonus", range(2))
_results("vtok", range(2))
_results("btok", range(2))
for _tc in range(2):
    _results(f"mat{_tc}", [(m, g) for g in range(2) for m in ("at", "a0", "kk", "rb", "rk")])
    _results(f"inv{_tc}", [(l, m, g) for l in range(1, 7) for m in ("h", "d") for g in range(2)
                           for m in ((m,) if m == "h" else (("d", "dt") if l < 6 else ("dt",)))])
    _results(f"end{_tc}", ["rhs0", "rhs1", "sa", "y"] + (["state"] if _tc == 0 else []))
_results("lorag", range(2))
_results("ynorm", range(4))
_results("sbqk", range(8))
_results("sbnorm", range(4))
_results("sbv", range(2))
_results("sbz", range(8))
_results("sbo", [("b", 0), ("b", 1)] + [(k, h) for h in range(2, 10) for k in ("b", "o")
                                        if (k == "b" and h < 8) or (k == "o" and h % 2)])
_results("memq", range(4))
_results("memnorm", range(4))
_results("mem", pipeline(MEM_STEPS))
_results("gate", range(24))
_results("branch", range(24))
_results("out", range(8))
_results("rms2", [0])
_results("ffn", range(2 * FC2))
RESULT = {key: n for n, key in enumerate(RESULTS)}
assert len(RESULT) == len(RESULTS)


def build(nc, w, xt, memt, consts_in, band_in, params_in, lora_in, gate2_in, relb_in, out):
    ctx = ExitStack()
    with ctx:
        def tensor(stack, name, shape, dt=F32):
            return stack.enter_context(nc.sbuf_tensor(name, shape, dt))

        def flat(ap):
            return ap[:, :, :].rearrange("p a t -> p (a t)")

        raw = tensor(ctx, "raw", [P, RING, 1024])
        whi = tensor(ctx, "whi", [P, RING, 1024], F32R)
        wlo = tensor(ctx, "wlo", [P, RING, 1024], F32R)
        con = tensor(ctx, "con", [P, NCON])
        par = tensor(ctx, "par", [P, NPAR])
        lora = tensor(ctx, "lora", [P, 512])
        gate2 = tensor(ctx, "gate2", [P, 512])
        relb = tensor(ctx, "relb", [32, 16])
        zeros = tensor(ctx, "zeros", [P, 512], BF16)
        x = tensor(ctx, "x", [P, DC, T])
        xh = tensor(ctx, "xh", [P, DC, T], F32R)
        xl = tensor(ctx, "xl", [P, DC, T], F32R)
        res = tensor(ctx, "res", [P, DC, T])
        sqr = tensor(ctx, "sqr", [P, DC, T])
        stat = tensor(ctx, "stat", [P, 4, T])
        km = tensor(ctx, "km", [P, 4, T])
        vm = tensor(ctx, "vm", [P, 2, 512])
        sc = tensor(ctx, "sc", [P, 2, 512])
        pr = tensor(ctx, "pr", [P, 2, 512])
        pT = tensor(ctx, "pT", [P, 4, 512])
        sm = tensor(ctx, "sm", [P, 2, 8])
        hh = tensor(ctx, "hh", [P, 2, T], F32R)
        hl = tensor(ctx, "hl", [P, 2, T], F32R)
        ha = tensor(ctx, "ha", [P, 2, T])
        hb = tensor(ctx, "hb", [P, 2, T])
        with ExitStack() as first:
            oh = tensor(first, "oh", [P, 8, T], F32R)
            ol = tensor(first, "ol", [P, 8, T], F32R)
            with ExitStack() as inner:
                memh = tensor(inner, "memh", [P, DC, T], F32R)
                meml = tensor(inner, "meml", [P, DC, T], F32R)
            bias = tensor(first, "bias", [P, 16, T])
            cqh = tensor(first, "cqh", [P, 3, T], F32R)
            cql = tensor(first, "cql", [P, 3, T], F32R)
            ckv = tensor(first, "ckv", [P, 2, T])
            ckvt = tensor(first, "ckvt", [P, 2, T])
            kr = tensor(first, "kr", [P, T])
            qr = tensor(first, "qr", [P, 4, T])
            nsink = tensor(first, "nsink", [P, 16])
            qlat = tensor(first, "qlat", [P, 8, 2 * T])
            qnh, qnl = oh, ol
            olh, oll = flat(hh), flat(hl)
            qs = qlat[:, 0:4, :].rearrange("p a (b t) -> p (a b) t", t=T)
            ks = qlat[:, 4, :].rearrange("p (b t) -> p b t", t=T)
            vs = qlat[:, 5, :].rearrange("p (b t) -> p b t", t=T)
            bandt = qlat[0:32, 6:8, 0:384]
            brow = qlat[0:16, 5, 0:384]
            hraw = sqr[:, 0:5, :]
        with ExitStack() as second:
            yh = tensor(second, "yh", [P, 12, T], F32R)
            yl = tensor(second, "yl", [P, 12, T], F32R)
            with ExitStack() as inner:
                rkv = tensor(inner, "rkv", [P, 14, T])
                kk = tensor(inner, "kk", [P, 4, T])
                aa = tensor(inner, "aa", [P, 4, T])
                bon = tensor(inner, "bon", [P, 4, T])
                vtok = tensor(inner, "vtok", [P, 2, 512])
                btok = tensor(inner, "btok", [P, 2, 512])
                gg = kk
                yy = rkv[:, 8:12, :]
                rhs, sa = flat(ha), flat(hb)
                st = stat[:, 0, :].rearrange("p (c i) -> p c i", c=4)
                mid = stat[:, 1, 0:24].rearrange("p (a c) -> p a c", a=3)
                fac = stat[:, 2, 0:4]
                pb = sc[:, :, 0:T + 1]
                em = pr[:, :, :].rearrange("p a (b t) -> p (a b) t", t=128)
                ep = pT[:, :, :].rearrange("p a b -> p (a b)")[:, 0:8 * 129].rearrange("p (a b) -> p a b", b=129)
                with ExitStack() as innermost:
                    cum = tensor(innermost, "cum", [P, 8, 129])
                rb = tensor(inner, "rb", [P, 2, 512])
                rk = tensor(inner, "rk", [P, 2, 512])
            with ExitStack() as inner:
                sbt = tensor(inner, "sbt", [P, 12, T])
                vsb = tensor(inner, "vsb", [P, 2, 512])
                z8 = tensor(inner, "z8", [P, 8, 384])
                e8 = tensor(inner, "e8", [P, 8, 384])
            with ExitStack() as inner:
                gates = tensor(inner, "gates", [P, 24, T])
                cg = tensor(inner, "cg", [P, 2, T + 2])
                cv = tensor(inner, "cv", [P, 2, T + 2])
                fa = tensor(inner, "fa", [P, 2, T])
                fb = tensor(inner, "fb", [P, 2, T])
                fs = tensor(inner, "fs", [P, 2, T])
        acc = [ctx.enter_context(nc.psum_tensor(f"acc{b}", [P, 512], F32)) for b in range(4)]
        work = [ctx.enter_context(nc.psum_tensor(f"work{b}", [P, 512], F32)) for b in range(4)]
        scratch = nc.dram_tensor("bias_scratch", [16, 384], F32, kind="Internal").ap()

        def spc(h):
            at_, h_ = (sqr, h) if h < 5 else (res, h - 5)
            return flat(at_)[:, h_ * 384:(h_ + 1) * 384]

        mst = hb[:, 0, :]
        at = res[:, 0:4, :].rearrange("p (g a) t -> p g (a t)", g=2)
        kkm = res[:, 4:8, :].rearrange("p (g a) t -> p g (a t)", g=2)
        tinv = sqr[:, 0:4, :].rearrange("p (g a) t -> p g (a t)", g=2)
        uinv = sqr[:, 4:8, :].rearrange("p (g a) t -> p g (a t)", g=2)

        def memc(c):
            return qlat[:, c // 2, c % 2 * T:c % 2 * T + T]

        def mem2(c):
            return qlat[:, c, :].rearrange("p (a t) -> p a t", a=2)

        def hsq(j):
            return pT[:, j // 2, j % 2 * T:j % 2 * T + T]

        memraw = qlat[:, 0:4, :]

        def C(name, width=P, col=0):
            return con[:, CCOL[name] + col:CCOL[name] + col + width]

        def G(name, col=0):
            return par[:, PCOL[name] + col:PCOL[name] + col + 1]

        def half(t):
            return slice(t * P, (t + 1) * P)

        def four(ap):
            return ap.rearrange("p (a b) -> p a b", b=P)

        def mask4(ap):
            return ap.rearrange("p (a b) -> p a b", a=1).broadcast_to([P, 4, P])

        def sem(name):
            return ctx.enter_context(nc.semaphore(name))

        filled = [sem(f"filled{b}") for b in range(4)]
        drained = [sem(f"drained{b}") for b in range(4)]
        raw_loaded = [sem(f"raw_loaded{r}") for r in range(RING)]
        cut_hi = sem("cut_hi")
        cut_lo = sem("cut_lo")
        slots_used = sem("slots_used")
        named = {}

        def sig(name):
            if name not in named:
                named[name] = sem(name)
            return named[name]

        def wait_filled(eng, key, it=None, per=0):
            n = RESULT[key]
            eng.wait_ge(filled[n % 4], n // 4 + 1 if it is None else it * (per // 4) + (n // 4 + 1))
            return work[n % 4]

        def wait_drained(eng, key, it=None, per=0):
            n = RESULT[key]
            eng.wait_ge(drained[n % 4], n // 4 + 1 if it is None else it * (per // 4) + (n // 4 + 1))

        def drain(ins, key):
            ins.then_inc(drained[RESULT[key] % 4], 1)

        block = ctx.enter_context(nc.Block())

        @block.sync
        def _(sp):
            for n in range(RING):
                sp.dma_start(raw[:, n, :], w[n]).then_inc(raw_loaded[n], 16)
            rounds = NSLOT // RING
            with sp.Fori(1, rounds) as i:
                for r in range(RING):
                    sp.wait_ge(cut_lo, i * RING + (r + 1 - RING))
                    sp.dma_start(raw[:, r, :], w[bass.ds(i * RING + r, 1), :, :].rearrange("a p n -> p (a n)"))\
                        .then_inc(raw_loaded[r], 16)
            for n in range(rounds * RING, NSLOT):
                sp.wait_ge(cut_lo, n + 1 - RING)
                sp.dma_start(raw[:, n % RING, :], w[n]).then_inc(raw_loaded[n % RING], 16)
            sp.wait_ge(sig("final"), 4)
            sp.dma_start(out, res[:, :, :]).then_inc(sig("stored"), 16)
            sp.wait_ge(sig("stored"), 16)

        @block.gpsimd
        def _(pool):
            nc.gpsimd.memset(zeros[:, :], 0.0).then_inc(sig("zeros_set"), 1)
            pool.dma_start(relb[:, :], relb_in).then_inc(sig("band_loaded"), 16)
            pool.dma_start(bandt, band_in).then_inc(sig("band_loaded"), 16)
            wait_drained(pool, ("brow", 0))
            pool.dma_start(scratch, brow).then_inc(sig("brow_stored"), 16)
            pool.wait_ge(sig("brow_stored"), 16)
            wait_drained(pool, ("memv", 0))
            wait_drained(pool, ("memv", 1))
            pool.dma_start(bias[:, :, :], bass.AP(scratch.tensor, 0, [[1, P], [384, 16], [1, T]]))\
                .then_inc(sig("bias_loaded"), 16)
            pool.wait_ge(sig("rinv"), 5)
            nc.gpsimd.memset(pb[:, :, 0:1], 0.0).then_inc(sig("pb_zero"), 1)
            nc.gpsimd.memset(cum[:, :, 0:1], 0.0).then_inc(sig("pb_zero"), 1)
            wait_drained(pool, ("mem", ("o", 3)))
            nc.gpsimd.memset(cg[:, :, 0:2], 0.0).then_inc(sig("cg_zero"), 1)
            nc.gpsimd.memset(cv[:, :, 0:2], 0.0).then_inc(sig("cg_zero"), 1)

        @block.tensor
        def _(pe):
            mm = nc.tensor.matmul

            def slot_start(n, it=None, per=0):
                pe.wait_ge(cut_lo, n + 1 if it is None else it * per + (n + 1))

            def open_result(key, it=None, per=0):
                n = RESULT[key]
                if n >= 4:
                    pe.wait_ge(drained[n % 4], n // 4 if it is None else it * (per // 4) + (n // 4))
                return work[n % 4]

            def close_result(ins, key):
                ins.then_inc(filled[RESULT[key] % 4], 1)

            def cut_product(dst, n, tile, hi, lo, start, stop, first=False, shared=False):
                col = slice(tile * P, tile * P + P)
                a = mm(dst, whi[:, n % RING, col], hi, start=start, stop=False, skip_group_check=shared)
                if first and n > 0:
                    a.then_inc(slots_used, 1)
                mm(dst, whi[:, n % RING, col], lo, start=False, stop=False, skip_group_check=shared)
                return mm(dst, wlo[:, n % RING, col], hi, start=False, stop=stop, skip_group_check=shared)

            def chunk(stage, j, key, hi, lo, waits=None):
                n = SLOT[stage] + j
                bank = open_result(key)
                slot_start(n)
                for k in range(DC):
                    if waits is not None:
                        waits(k)
                    last = cut_product(bank[:, 0:T], n, k, hi[:, k, :], lo[:, k, :], k == 0, k == DC - 1, k == 0)
                close_result(last, key)

            def token_major(stage, slots, width, hi, lo):
                rows = 1024 // width
                banks = [open_result((stage, t)) for t in range(2)]
                for j in range(slots):
                    n = SLOT[stage] + j
                    slot_start(n)
                    for r in range(rows):
                        k = j * rows + r
                        col = slice(r * width, (r + 1) * width)
                        for t in range(2):
                            dst = banks[t][:, 0:width]
                            a = mm(dst, hi[:, k, half(t)], whi[:, n % RING, col], start=k == 0, stop=False)
                            if r == 0 and t == 0:
                                a.then_inc(slots_used, 1)
                            mm(dst, hi[:, k, half(t)], wlo[:, n % RING, col], start=False, stop=False)
                            last = mm(dst, lo[:, k, half(t)], whi[:, n % RING, col], start=False, stop=k == DC - 1)
                            if k == DC - 1:
                                close_result(last, (stage, t))

            def sums(keys, srcs, weights, chunks, waits):
                banks = [open_result(k) for k in keys]
                for c in range(chunks):
                    for a, (bank, src) in enumerate(zip(banks, srcs)):
                        waits(c, a)
                        last = mm(bank[:, 0:T], weights, src[:, c, :], start=c == 0, stop=c == chunks - 1)
                        if c == chunks - 1:
                            close_result(last, keys[a])

            def group_sums(stage, first, srcs, weights):
                for j, src in enumerate(srcs):
                    key = (stage, first + j)
                    close_result(mm(open_result(key)[:, :], weights, flat(src), start=True, stop=True), key)

            pe.wait_ge(sig("band_loaded"), 32)
            close_result(mm(open_result(("brow", 0))[0:16, 0:384], relb[:, :], bandt[:, 0, :], start=True, stop=True), ("brow", 0))
            pe.wait_ge(sig("con_loaded"), 16)
            pe.wait_ge(sig("x_cut"), 1)
            for j in range(4):
                chunk("in", j, ("in", j), xh, xl)
            sums([("memstat", 0)], [res], C("ones"), DC, lambda c, a: pe.wait_ge(sig("mem_sq"), 1))
            for j in range(4, 7):
                chunk("in", j, ("in", j), xh, xl)
            bank = open_result(("mlastat", 0))
            pe.wait_ge(sig("in_sq"), 5)
            for j in range(5):
                dst = bank[:, 0:T] if j < 3 else bank[:, T:2 * T]
                last = mm(dst, C("ones"), hsq(j), start=j in (0, 3), stop=j in (2, 4))
            close_result(last, ("mlastat", 0))
            pe.wait_ge(sig("mem_cut"), 4)
            for j in range(4):
                chunk("memk", j, ("memk", j), memh, meml)
            bank = open_result(("ckvt", 0))
            pe.wait_ge(sig("ckv_ready"), 2)
            for t in range(2):
                for c in range(2):
                    last = nc.tensor.transpose(bank[:, t * T + c * P:t * T + c * P + P], ckv[:, c, half(t)], C("ident"))
            close_result(last, ("ckvt", 0))
            pe.wait_ge(sig("cq_cut"), 1)
            for j in range(16):
                bank = open_result(("q", j))
                for k in range(3):
                    s, tile = divmod(3 * j + k, 8)
                    if tile == 0:
                        slot_start(SLOT["q"] + s)
                    last = cut_product(bank[:, 0:T], SLOT["q"] + s, tile, cqh[:, k, :], cql[:, k, :], k == 0, k == 2, tile == 0)
                close_result(last, ("q", j))
            for h in range(MLA_H):
                bank = open_result(("qlat", h))
                wait_drained(pe, ("q", h))
                for c in range(2):
                    s, tile = divmod(2 * h + c, 8)
                    if tile == 0:
                        slot_start(SLOT["uk"] + s)
                    last = cut_product(bank[:, c * T:(c + 1) * T], SLOT["uk"] + s, tile, qnh[:, h, :], qnl[:, h, :], True, True, tile == 0)
                close_result(last, ("qlat", h))

            def transposes(stage, h, blocks):
                bank = open_result((stage, ("t", h)))
                pe.wait_ge(sig(f"{stage}_norm"), h + 1)
                for a, b in blocks:
                    last = nc.tensor.transpose(bank[:, b * P:b * P + P], pr[:, h % 2, a * P:a * P + P], C("ident"))
                close_result(last, (stage, ("t", h)))

            pe.wait_ge(sig("kr_ready"), 1)
            pe.wait_ge(sig("qr_ready"), 4)
            wait_drained(pe, ("ckvt", 0))
            for kind, h in pipeline(MLA_STEPS):
                key = ("mla", (kind, h))
                if kind == "s":
                    bank = open_result(key)
                    wait_drained(pe, ("qlat", h))
                    off = slice(64 * (h % 2), 64 * (h % 2) + 64)
                    for dst, q, keys in ((bank[:, 0:P], 0, P), (bank[:, P:3 * P], P, T)):
                        for c in range(2):
                            mm(dst, qlat[:, h, c * T + q:c * T + q + P], ckv[:, c, 0:keys], start=c == 0, stop=False)
                        last = mm(dst, qr[off, h // 2, q:q + P], kr[off, 0:keys], start=False, stop=True)
                    close_result(last, key)
                elif kind == "t":
                    transposes("mla", h, [(0, 0), (1, 1), (2, 2)])
                elif kind == "o":
                    bank = open_result(key)
                    wait_drained(pe, ("mla", ("t", h)))
                    for c in range(2):
                        mm(bank[:, c * T:(c + 1) * T], ckvt[:, 0, half(c)], pT[:, h % 4, 0:T], start=True, stop=False)
                        last = mm(bank[:, c * T + P:(c + 1) * T], ckvt[:, 1, half(c)], pT[:, h % 4, T:3 * P], start=False, stop=True)
                    close_result(last, key)
                else:
                    bank = open_result(key)
                    wait_drained(pe, ("mla", ("o", h)))
                    for c in range(2):
                        s, tile = divmod(2 * h + c, 8)
                        if tile == 0:
                            slot_start(SLOT["uv"] + s)
                        last = cut_product(bank[:, 0:T], SLOT["uv"] + s, tile, olh[:, c * T:(c + 1) * T],
                                           oll[:, c * T:(c + 1) * T], c == 0, c == 1, tile == 0)
                    close_result(last, key)
            for j in range(DC):
                chunk("wo", j, ("wo", j), oh, ol, (lambda k: wait_drained(pe, ("mla", ("u", k)))) if j == 0 else None)

            def norm_sums(name, source, squares_before):
                def waits(c, a):
                    if a == 0 and source is not None:
                        wait_drained(pe, (source, c))
                    elif a == 0:
                        pe.wait_ge(sig(f"{name}_sum"), c // 2 + 1)
                    else:
                        pe.wait_ge(sig("squared"), squares_before + c + 1)
                sums([(name, 0), (name, 1)], [res, sqr], C("ones"), DC, waits)

            def mlp(stage, normed):
                base = SLOT[stage]
                pe.wait_ge(sig("zeros_set"), 1)
                for b in range(4):
                    mm(acc[b][:, :], zeros[:, 0:P], zeros[:, :], start=True, stop=False, skip_group_check=True)
                chunk(stage, 0, (stage, 0), xh, xl, lambda k: pe.wait_ge(sig("x_normed"), normed + k // 2 + 1))

                def step(f, it=None):
                    key = (stage, f + 1)
                    bank = open_result(key, it, 4)
                    n = base + 2 * f + 1
                    slot_start(n, it, 8)
                    for k in range(DC):
                        last = cut_product(bank[:, 0:T], n, k, xh[:, k, :], xl[:, k, :], k == 0, k == DC - 1, k == 0)
                    close_result(last, key)
                    down(f, n + 1, it)

                def down(f, n, it=None):
                    slot_start(n, it, 8)
                    wait_drained(pe, (stage, f), it, 4)
                    for c in range(DC):
                        last = cut_product(acc[c // 2][:, (c % 2) * T:(c % 2 + 1) * T], n, c, hh[:, f % 2, :], hl[:, f % 2, :],
                                           False, c == DC - 1, c == 0, True)
                    return last

                rounds = (FC - 1) // 4
                with pe.Fori(0, rounds) as it:
                    for f in range(4):
                        step(f, it)
                for f in range(4 * rounds, FC - 1):
                    step(f)
                down(FC - 1, base + 2 * FC - 1).then_inc(sig("acc_full"), 1)

            norm_sums("ln0", "wo", 0)
            token_major("memv", 4, 512, memh, meml)
            mlp("mlp0", 0)
            norm_sums("ln1", None, 8)

            for j in range(8):
                chunk("swaq", j, ("swaq", j), xh, xl, (lambda k: pe.wait_ge(sig("x_normed"), 4 + k // 2 + 1)) if j == 0 else None)
            for j in range(2):
                chunk("swak", j, ("swak", j), xh, xl)
            token_major("swav", 2, T, xh, xl)
            for kind, h in pipeline(SWA_STEPS):
                key = ("swa", (kind, h))
                chunk_, off = h // 2, slice(64 * (h % 2), 64 * (h % 2) + 64)
                if kind == "s":
                    bank = open_result(key)
                    wait_drained(pe, ("swaq", chunk_))
                    wait_drained(pe, ("swak", chunk_ // 4))
                    for dst, q, keys in ((bank[:, 0:P], 0, P), (bank[:, P:3 * P], P, T)):
                        last = mm(dst, qs[off, chunk_, q:q + P], ks[off, chunk_ // 4, 0:keys], start=True, stop=True)
                    close_result(last, key)
                elif kind == "t":
                    transposes("swa", h, [(0, 0), (1, 1), (2, 2)])
                else:
                    bank = open_result(key)
                    for t in range(2):
                        wait_drained(pe, ("swav", t))
                    for g in (h - 1, h):
                        wait_drained(pe, ("swa", ("t", g)))
                        o = slice(64 * (g % 2), 64 * (g % 2) + 64)
                        kv = 2 * (g // 8) + g % 2
                        mm(bank[o, 0:T], vs[:, 0, kv * 64:kv * 64 + 64], pT[:, g % 4, 0:T], start=True, stop=False)
                        last = mm(bank[o, P:T], vs[:, 1, kv * 64:kv * 64 + 64], pT[:, g % 4, T:3 * P], start=False, stop=True)
                    close_result(last, key)
            for j in range(DC):
                chunk("swao", j, ("swao", j), oh, ol, (lambda k: wait_drained(pe, ("swa", ("opair", 2 * k + 1)))) if j == 0 else None)
            norm_sums("ln2", "swao", 16)
            mlp("mlp1", 8)
            norm_sums("ln3", None, 24)

            sums([("rms1", 0)], [sqr], C("ones"), DC, lambda c, a: pe.wait_ge(sig("squared"), 32 + c + 1))
            for j in range(14):
                chunk("rwkv", j, ("rwkv", j), xh, xl, (lambda k: pe.wait_ge(sig("x_normed"), 12 + k // 2 + 1)) if j == 0 else None)
            pe.wait_ge(sig("lora_loaded"), 32)
            pe.wait_ge(sig("lora_act"), 2)
            wait_drained(pe, ("rwkv", 12))

            def lora_out(name, weights, src):
                for j in range(2):
                    bank = open_result((name, j))
                    for c in range(2):
                        last = mm(bank[:, c * T:(c + 1) * T], weights[:, (2 * j + c) * P:(2 * j + c + 1) * P], src, start=True, stop=True)
                    close_result(last, (name, j))

            lora_out("loraw", lora[0:64, :], rkv[0:64, 12, :])
            lora_out("loraa", lora[64:P, :], rkv[64:P, 12, :])
            pe.wait_ge(sig("kk_sq"), 1)
            group_sums("kknorm", 0, [sqr[:, 2 * j:2 * j + 2, :] for j in range(2)], C("blockones"))
            pe.wait_ge(sig("rk_prod"), 1)
            group_sums("bonus", 0, [sqr[:, 4 + 2 * j:6 + 2 * j, :] for j in range(2)], C("blockones"))
            for t in range(2):
                bank = open_result(("vtok", t))
                for c in range(4):
                    last = nc.tensor.transpose(bank[:, c * P:c * P + P], rkv[:, 8 + c, half(t)], C("ident"))
                close_result(last, ("vtok", t))
            pe.wait_ge(sig("factors"), 1)
            for j, src in enumerate((aa[:, :, :], rkv[:, 0:4, :])):
                bank = open_result(("btok", j))
                for c in range(4):
                    last = nc.tensor.transpose(bank[:, c * P:c * P + P], src[:, c, 0:P], C("ident"))
                close_result(last, ("btok", j))

            def blk(j):
                return slice(j * P, j * P + P)

            levels = 0
            for tc in range(2):
                mats = {"at": (aa, kk), "a0": (kk, aa), "kk": (rkv[:, 0:4, :], kk), "rb": (aa, rkv[:, 4:8, :]),
                        "rk": (rkv[:, 0:4, :], rkv[:, 4:8, :])}
                for g in range(2):
                    for m, (left, right) in mats.items():
                        key = (f"mat{tc}", (m, g))
                        bank = open_result(key)
                        for j in range(4):
                            off = slice(64 * g, 64 * g + 64)
                            last = mm(bank[:, blk(j)], left[off, j, half(tc)], right[off, j, half(tc)], start=True, stop=True)
                        close_result(last, key)
                for l in range(1, 7):
                    for g in range(2):
                        key = (f"inv{tc}", (l, "h", g))
                        bank = open_result(key)
                        pe.wait_ge(sig("inv_mask"), levels + g + 1)
                        for j in range(4):
                            last = mm(bank[:, blk(j)], sc[:, g, blk(j)], tinv[:, g, blk(j)], start=True, stop=True)
                        close_result(last, key)
                    levels += 2
                    for g in range(2):
                        wait_drained(pe, (f"inv{tc}", (l, "h", g)))
                        for m in ("d", "dt")[l == 6:]:
                            key = (f"inv{tc}", (l, m, g))
                            bank = open_result(key)
                            for j in range(4):
                                left, right = (uinv, pr) if m == "d" else (pr, uinv)
                                last = mm(bank[:, blk(j)], left[:, g, blk(j)], right[:, g, blk(j)], start=True, stop=True)
                            close_result(last, key)
                banks = [open_result((f"end{tc}", f"rhs{g}")) for g in range(2)]
                wait_drained(pe, (f"mat{tc}", ("rk", 1)))
                if tc == 0:
                    wait_drained(pe, ("vtok", 1))
                else:
                    wait_drained(pe, ("end0", "state"))
                for h in range(8):
                    c, off, col = h // 2, slice(64 * (h % 2), 64 * (h % 2) + 64), slice(h * 64, h * 64 + 64)
                    dst = banks[h % 2][:, c * 64:c * 64 + 64]
                    last = mm(dst, kkm[:, h % 2, blk(c)], vtok[:, tc, col], start=True, stop=tc == 0)
                    if tc:
                        last = mm(dst, kk[off, c, half(1)], st[off, c, :], start=False, stop=True)
                    if h >= 6:
                        close_result(last, (f"end{tc}", f"rhs{h % 2}"))
                key = (f"end{tc}", "sa")
                bank = open_result(key)
                for g in range(2):
                    wait_drained(pe, (f"end{tc}", f"rhs{g}"))
                for g in range(2):
                    wait_drained(pe, (f"inv{tc}", (6, "dt", g)))
                for h in range(8):
                    src = rhs[:, h % 2 * T + h // 2 * 64:h % 2 * T + h // 2 * 64 + 64]
                    last = mm(bank[:, h * 64:h * 64 + 64], uinv[:, h % 2, blk(h // 2)], src, start=True, stop=True)
                close_result(last, key)
                key = (f"end{tc}", "y")
                bank = open_result(key)
                wait_drained(pe, (f"end{tc}", "sa"))
                for h in range(8):
                    c, off, col = h // 2, slice(64 * (h % 2), 64 * (h % 2) + 64), slice(h * 64, h * 64 + 64)
                    dst = bank[off, blk(c)]
                    mm(dst, vtok[:, tc, col], rk[:, h % 2, blk(c)], start=True, stop=False)
                    last = mm(dst, sa[:, col], rb[:, h % 2, blk(c)], start=False, stop=tc == 0)
                    if tc:
                        last = mm(dst, st[off, c, :], rkv[off, 4 + c, half(1)], start=False, stop=True)
                close_result(last, key)
                if tc == 0:
                    key = ("end0", "state")
                    bank = open_result(key)
                    for j in range(2):
                        wait_drained(pe, ("btok", j))
                    for h in range(8):
                        c, off, col = h // 2, slice(64 * (h % 2), 64 * (h % 2) + 64), slice(h * 64, h * 64 + 64)
                        dst = bank[off, c * 64:c * 64 + 64]
                        mm(dst, btok[:, 0, col], sa[:, col], start=True, stop=False)
                        last = mm(dst, btok[:, 1, col], vtok[:, 0, col], start=False, stop=True)
                    close_result(last, key)
            lora_out("lorag", gate2[:, :], rkv[:, 13, :])
            wait_drained(pe, ("end1", "y"))
            group_sums("ynorm", 0, [yy[:, 2 * j:2 * j + 2, :] for j in range(2)], C("blockones"))
            pe.wait_ge(sig("y_sq"), 1)
            group_sums("ynorm", 2, [sqr[:, 2 * j:2 * j + 2, :] for j in range(2)], C("blockones"))

            for j in range(8):
                chunk("sbqk", j, ("sbqk", j), xh, xl)
            pe.wait_ge(sig("head_sq"), 1)
            group_sums("sbnorm", 0, [sqr[:, 2 * j:2 * j + 2, :] for j in range(4)], C("blockones"))
            token_major("sbv", 4, 512, xh, xl)
            pe.wait_ge(sig("sb_normed"), 8)
            for h in range(8):
                key = ("sbz", h)
                bank = open_result(key)
                c, off = h // 2, slice(64 * (h % 2), 64 * (h % 2) + 64)
                mm(bank[:, 0:T], sbt[off, 4 + c, 0:P], sbt[off, c, :], start=True, stop=True)
                last = mm(bank[:, T:3 * P], sbt[off, 4 + c, P:T], sbt[off, c, P:T], start=True, stop=True)
                close_result(last, key)
            for kind, h in [k[1] for k in RESULTS if k[0] == "sbo"]:
                key = ("sbo", (kind, h))
                bank = open_result(key)
                if kind == "b":
                    pe.wait_ge(sig("softplus"), h + 1)
                    mm(bank[:, 0:T], C("later"), spc(h)[:, 0:T], start=True, stop=False)
                    mm(bank[:, P:T], C("ones"), spc(h)[:, T:3 * P], start=False, stop=True)
                    last = mm(bank[:, T:3 * P], C("later"), spc(h)[:, T:3 * P], start=True, stop=True)
                else:
                    for t in range(2):
                        wait_drained(pe, ("sbv", t))
                    pe.wait_ge(sig("sb_attn"), h - 1)
                    for g in (h - 3, h - 2):
                        o = slice(64 * (g % 2), 64 * (g % 2) + 64)
                        mm(bank[o, 0:T], vsb[:, 0, g * 64:g * 64 + 64], z8[:, g, 0:T], start=True, stop=False)
                        last = mm(bank[o, P:T], vsb[:, 1, g * 64:g * 64 + 64], z8[:, g, T:3 * P], start=False, stop=True)
                close_result(last, key)

            for j in range(4):
                chunk("memq", j, ("memq", j), xh, xl)
            pe.wait_ge(sig("head_sq"), 2)
            group_sums("memnorm", 0, [sqr[:, 2 * j:2 * j + 2, :] for j in range(4)], C("ones"))
            pe.wait_ge(sig("mem_normed"), 8)
            for kind, h in pipeline(MEM_STEPS):
                key = ("mem", (kind, h))
                if kind == "s":
                    bank = open_result(key)
                    for t in range(2):
                        last = mm(bank[:, t * T:(t + 1) * T], sbt[:, 8 + h, half(t)], km[:, h, :], start=True, stop=True)
                    close_result(last, key)
                elif kind == "t":
                    transposes("mem", h, [(0, 0), (1, 2), (2, 1), (3, 3)])
                else:
                    bank = open_result(key)
                    wait_drained(pe, ("mem", ("t", h)))
                    for t in range(2):
                        wait_drained(pe, ("memv", t))
                    for t in range(2):
                        last = mm(bank[:, 0:T], vm[:, t, h * P:h * P + P], pT[:, h % 4, t * T:(t + 1) * T], start=t == 0, stop=t == 1)
                    close_result(last, key)

            with pe.Fori(0, 6) as it:
                for r in range(4):
                    bank = open_result(("gate", r), it, 4)
                    n = SLOT["gate"] + r
                    slot_start(n, it, 4)
                    for k in range(DC):
                        last = cut_product(bank[:, 0:T], n, k, xh[:, k, :], xl[:, k, :], k == 0, k == DC - 1, k == 0)
                    close_result(last, ("gate", r))
            for c in range(4):
                wait_drained(pe, ("mem", ("o", c)))
            pe.wait_ge(sig("y_cut"), 1)
            with pe.Fori(0, 3) as it:
                for r in range(8):
                    bank = open_result(("branch", r), it, 8)
                    n = SLOT["branch"] + r // 2
                    if r % 2 == 0:
                        slot_start(n, it, 4)
                    for k in range(4):
                        tile = 4 * (r % 2) + k
                        part = bass.ds(it * 4 + k, 1)
                        last = cut_product(bank[:, 0:T], n, tile, flat(yh[:, part, :]), flat(yl[:, part, :]), k == 0, k == 3, tile == 0)
                    close_result(last, ("branch", r))
            for j in range(DC):
                chunk("out", j, ("out", j), xh, xl, (lambda k: pe.wait_ge(sig("x_normed"), 16 + k // 2 + 1)) if j == 0 else None)
            sums([("rms2", 0)], [sqr], C("ones"), DC, lambda c, a: pe.wait_ge(sig("squared"), 40 + c + 1))

            base = SLOT["ffn"]
            for b in range(4):
                mm(acc[b][:, :], zeros[:, 0:P], zeros[:, :], start=True, stop=False, skip_group_check=True)
            for j in range(2):
                chunk("ffn", j, ("ffn", j), xh, xl, (lambda k: pe.wait_ge(sig("x_normed"), 20 + k // 2 + 1)) if j == 0 else None)

            def ffn_down(f, n, it=None):
                slot_start(n, it, 12)
                wait_drained(pe, ("ffn", 2 * f + 1), it, 8)
                for c in range(DC):
                    last = cut_product(acc[c // 2][:, (c % 2) * T:(c % 2 + 1) * T], n, c, hh[:, f % 2, :], hl[:, f % 2, :],
                                       False, c == DC - 1, c == 0, True)
                return last

            def ffn_step(f, it=None):
                for j in range(2):
                    key = ("ffn", 2 * f + 2 + j)
                    bank = open_result(key, it, 8)
                    n = base + 3 * f + 2 + j
                    slot_start(n, it, 12)
                    for k in range(DC):
                        last = cut_product(bank[:, 0:T], n, k, xh[:, k, :], xl[:, k, :], k == 0, k == DC - 1, k == 0)
                    close_result(last, key)
                ffn_down(f, base + 3 * f + 4, it)

            rounds = (FC2 - 1) // 4
            with pe.Fori(0, rounds) as it:
                for f in range(4):
                    ffn_step(f, it)
            for f in range(4 * rounds, FC2 - 1):
                ffn_step(f)
            ffn_down(FC2 - 1, base + 3 * FC2 - 1).then_inc(sig("acc_full"), 1)
        @block.scalar
        def _(act):
            own = Tally(act, sig("act_step"))
            act_fn = nc.scalar.activation
            count = {"norm": 0, "x_ready": 0}

            def cut(n, it=None, per=0):
                if n >= NSLOT:
                    return
                loaded, used = 16 * (n // RING + 1), n - RING + 1
                act.wait_ge(raw_loaded[n % RING], loaded if it is None else it * (16 * per // RING) + loaded)
                if n >= RING:
                    act.wait_ge(slots_used, used if it is None else it * per + used)
                act_fn(whi[:, n % RING, :], raw[:, n % RING, :], ACT.Copy).then_inc(cut_hi, 1)

            def cuts(stage, s, it=None, per=0):
                cut(SLOT[stage] + s + AHEAD, it, per)

            act.dma_start(x[:, :, :], xt).then_inc(sig("x_loaded"), 16)
            act.dma_start(con[:, :], consts_in).then_inc(sig("con_loaded"), 16)
            act.dma_start(par[:, :], params_in).then_inc(sig("par_loaded"), 16)
            act.dma_start(flat(memraw), memt).then_inc(sig("mem_loaded"), 16)
            act.dma_start(lora[:, :], lora_in).then_inc(sig("lora_loaded"), 16)
            act.dma_start(gate2[:, :], gate2_in).then_inc(sig("lora_loaded"), 16)

            def root():
                count["norm"] += 1
                act.wait_ge(sig("rinv"), count["norm"])
                act_fn(stat[:, 3, :], stat[:, 2, :], ACT.Sqrt).then_inc(sig("rstd"), 1)

            def square(src, wait):
                for c in range(DC):
                    wait(c)
                    act_fn(sqr[:, c, :], src[:, c, :], ACT.Square).then_inc(sig("squared"), 1)

            def cut_x(src, hooks=None, merged=False):
                for c in range(4):
                    if merged:
                        act.wait_ge(sig("merged"), 16 + 2 * c + 2)
                    else:
                        count["x_ready"] += 1
                        act.wait_ge(sig("x_ready"), count["x_ready"])
                    act_fn(xh[:, 2 * c:2 * c + 2, :], src[:, 2 * c:2 * c + 2, :], ACT.Copy).then_inc(sig("x_hi"), 1)
                    if hooks:
                        hooks(c)

            act.wait_ge(sig("x_loaded"), 16)
            act_fn(flat(xh), flat(x), ACT.Copy).then_inc(sig("x0_hi"), 1)
            for n in range(AHEAD):
                cut(n)
            act.wait_ge(sig("mem_loaded"), 16)
            act_fn(flat(res), flat(memraw), ACT.Square).then_inc(sig("mem_sq"), 1)
            for j in range(7):
                cuts("in", j)
                if j < 5:
                    bank = wait_filled(act, ("in", j))
                    act_fn(hsq(j), bank[:, 0:T], ACT.Square).then_inc(sig("in_sq"), 1)
                if j == 4:
                    act.wait_ge(sig("mem_inv"), 1)
                    act_fn(mst[:, :], mst[:, :], ACT.Sqrt).then_inc(sig("mem_rstd"), 1)
            for c in range(4):
                act.wait_ge(sig("mem_ready"), c + 1)
                act_fn(memh[:, 2 * c:2 * c + 2, :], mem2(c), ACT.Copy).then_inc(sig("mem_hi"), 1)
            cuts("memk", 0)
            act.wait_ge(sig("mla_inv"), 1)
            act_fn(stat[:, 2:4, :], stat[:, 0:2, :], ACT.Sqrt).then_inc(sig("mla_rstd"), 1)
            act.wait_ge(sig("cq_ready"), 1)
            act_fn(flat(cqh), flat(hraw[:, 0:3, :]), ACT.Copy).then_inc(sig("cq_hi"), 1)
            for j in range(4):
                if j:
                    cuts("memk", j)
                bank = wait_filled(act, ("memk", j))
                drain(act_fn(km[:, j, :], bank[:, 0:T], ACT.Copy), ("memk", j))
            bank = wait_filled(act, ("ckvt", 0))
            drain(act_fn(flat(ckvt), bank[:, :], ACT.Copy), ("ckvt", 0))
            for j in range(16):
                for s in range(6):
                    if 3 * j <= 8 * s < 3 * j + 3:
                        cuts("q", s)
                if j < 8:
                    bank = wait_filled(act, ("q", j))
                    act_fn(qnh[:, j, :], bank[:, 0:T], ACT.Copy).then_inc(sig("qn_hi"), 1)
            act.wait_ge(sig("brow_stored"), 16)
            for h in range(8):
                if h % 4 == 0:
                    cuts("uk", h // 4)
                if h % 2 == 0:
                    bank = wait_filled(act, ("qlat", h))
                    drain(act_fn(qlat[:, h, :], bank[:, :], ACT.Copy), ("qlat", h))

            def probabilities(stage, h, parts, sink=None):
                p = h % 2
                act.wait_ge(sig(f"{stage}_max"), h + 1)
                for b, cols in enumerate(parts):
                    last = act_fn(pr[:, p, cols], sc[:, p, cols], ACT.Exp, bias=sm[:, p, b:b + 1], accum_out=sm[:, p, 2 + b:3 + b])
                    if sink is not None:
                        own.link(last)
                if sink is not None:
                    last = act_fn(sm[:, p, 4:6], sm[:, p, 0:2], ACT.Exp, bias=sink)
                last.then_inc(sig(f"{stage}_exp"), 1)

            def key_major(stage, h, width):
                bank = wait_filled(act, (stage, ("t", h)))
                drain(act_fn(pT[:, h % 4, 0:width], bank[:, 0:width], ACT.Copy), (stage, ("t", h)))

            three = (slice(0, P), slice(P, 3 * P))
            for t in range(MLA_H + 4):
                if 0 <= t - 4:
                    if (t - 4) % 4 == 0:
                        cuts("uv", (t - 4) // 4)
                if 0 <= t - 2 < MLA_H:
                    key_major("mla", t - 2, 384)
                if 0 <= t - 4:
                    bank = wait_filled(act, ("mla", ("u", t - 4)))
                    act_fn(oh[:, t - 4, :], bank[:, 0:T], ACT.Copy).then_inc(sig("oh_hi"), 1)
                if 0 <= t - 3 < MLA_H:
                    bank = wait_filled(act, ("mla", ("o", t - 3)))
                    act_fn(olh[:, :], bank[:, :], ACT.Copy).then_inc(sig("ol_hi"), 1)
                if t < MLA_H:
                    probabilities("mla", t, three)
            for j in range(DC):
                cuts("wo", j)
                wait_drained(act, ("wo", j))
                act_fn(sqr[:, j, :], res[:, j, :], ACT.Square).then_inc(sig("squared"), 1)
            root()
            cut_x(x, lambda c: cuts("memv", c) if c < 2 else None)
            for j in range(2, 4):
                cuts("memv", j)
            for t in range(2):
                bank = wait_filled(act, ("memv", t))
                drain(act_fn(vm[:, t, :], bank[:, :], ACT.Copy), ("memv", t))

            def mlp(stage, units_before):
                def hidden(f, it=None):
                    bank = wait_filled(act, (stage, f), it, 4)
                    act_fn(ha[:, f % 2, :], bank[:, 0:T], ACT.Relu).then_inc(sig("relu"), 1)
                    done = units_before + f + 1
                    act.wait_ge(sig("relu"), done if it is None else it * 4 + done)
                    act_fn(hh[:, f % 2, :], ha[:, f % 2, :], ACT.Square).then_inc(sig("h_hi"), 1)

                cuts(stage, 0)
                hidden(0)

                def step(f, it=None):
                    cuts(stage, 2 * f + 1, it, 8)
                    hidden(f + 1, it)
                    cuts(stage, 2 * f + 2, it, 8)

                rounds = (FC - 1) // 4
                with act.Fori(0, rounds) as it:
                    for f in range(4):
                        step(f, it)
                for f in range(4 * rounds, FC - 1):
                    step(f)
                cuts(stage, 2 * FC - 1)

            mlp("mlp0", 0)
            square(res, lambda c: act.wait_ge(sig("ln1_sum"), c // 2 + 1))
            root()
            cut_x(x)
            for j in range(8):
                cuts("swaq", j)
                bank = wait_filled(act, ("swaq", j))
                drain(act_fn(qs[:, j, :], bank[:, 0:T], ACT.Copy), ("swaq", j))
            for j in range(2):
                cuts("swak", j)
                bank = wait_filled(act, ("swak", j))
                drain(act_fn(ks[:, j, :], bank[:, 0:T], ACT.Copy), ("swak", j))
            for j in range(2):
                cuts("swav", j)
            for t in range(2):
                bank = wait_filled(act, ("swav", t))
                drain(act_fn(vs[:, t, :], bank[:, 0:T], ACT.Copy), ("swav", t))
            for t in range(SWA_H + 3):
                if 0 <= t - 2 < SWA_H:
                    key_major("swa", t - 2, 384)
                if 0 <= t - 3 and (t - 3) % 2:
                    bank = wait_filled(act, ("swa", ("opair", t - 3)))
                    act_fn(oh[:, (t - 3) // 2, :], bank[:, 0:T], ACT.Copy).then_inc(sig("oh_hi"), 1)
                if t < SWA_H:
                    probabilities("swa", t, three, par[:, PCOL["sinks"] + SWA_ORDER[t]:PCOL["sinks"] + SWA_ORDER[t] + 1])
            for j in range(DC):
                cuts("swao", j)
                wait_drained(act, ("swao", j))
                act_fn(sqr[:, j, :], res[:, j, :], ACT.Square).then_inc(sig("squared"), 1)
            root()
            cut_x(x)
            mlp("mlp1", FC)
            square(res, lambda c: act.wait_ge(sig("ln3_sum"), c // 2 + 1))
            root()

            square(x, lambda c: act.wait_ge(sig("x_out"), c // 2 + 1))
            root()
            cut_x(res)
            for j in range(14):
                cuts("rwkv", j)
                bank = wait_filled(act, ("rwkv", j))
                if j == 0:
                    act.wait_ge(sig("pb_zero"), 2)
                if j >= 2:
                    wait_drained(act, ("rwkv", j - 2))
                act_fn(pb[:, j % 2, 1:T + 1], bank[:, 0:T], ACT.Copy).then_inc(sig("pb_full"), 1)
            wait_drained(act, ("rwkv", 12))
            act_fn(rkv[0:64, 12, :], rkv[0:64, 12, :], ACT.Tanh).then_inc(sig("lora_act"), 1)
            wait_drained(act, ("rwkv", 13))
            act_fn(rkv[:, 13, :], rkv[:, 13, :], ACT.Sigmoid).then_inc(sig("lora_act"), 1)
            for name, col in (("loraw", "w0"), ("loraa", "a0")):
                for j in range(2):
                    bank = wait_filled(act, (name, j))
                    for c in range(2):
                        src, chunk_ = bank[:, c * T:(c + 1) * T], 2 * j + c
                        if name == "loraw":
                            last = act_fn(em[:, 2 * chunk_:2 * chunk_ + 2, :], src.rearrange("p (a t) -> p a t", a=2), ACT.Sigmoid, bias=G(col, chunk_))
                        else:
                            last = act_fn(aa[:, chunk_, :], src, ACT.Sigmoid, bias=G(col, chunk_))
                    drain(last, (name, j))
            act.wait_ge(sig("kk_raw"), 1)
            act_fn(sqr[:, 0:4, :], kk[:, :, :], ACT.Square).then_inc(sig("kk_sq"), 1)
            act.wait_ge(sig("cum_ready"), 1)
            for c in range(8):
                last = act_fn(ep[:, c, :], cum[:, c, :], ACT.Exp, scale=-KAPPA, bias=mid[:, 0, c:c + 1])
            for c in range(8):
                last = act_fn(em[:, c, :], cum[:, c, 1:129], ACT.Exp, scale=KAPPA, bias=mid[:, 1, c:c + 1])
            last.then_inc(sig("exps"), 1)
            act.wait_ge(sig("fac_ready"), 1)
            act_fn(fac[:, :], fac[:, :], ACT.Exp, scale=-KAPPA).then_inc(sig("fac_exp"), 1)
            act.wait_ge(sig("kk_inv"), 1)
            act_fn(sqr[:, 0:4, :], sqr[:, 0:4, :], ACT.Sqrt).then_inc(sig("kk_rstd"), 1)
            for t in range(2):
                bank = wait_filled(act, ("vtok", t))
                drain(act_fn(vtok[:, t, :], bank[:, :], ACT.Copy), ("vtok", t))
            for t in range(2):
                bank = wait_filled(act, ("btok", t))
                drain(act_fn(btok[:, t, :], bank[:, :], ACT.Copy), ("btok", t))
            for tc in range(2):
                for l in range(1, 7):
                    for g in range(2):
                        key = (f"inv{tc}", (l, "h", g))
                        bank = wait_filled(act, key)
                        drain(act_fn(pr[:, g, :], bank[:, :], ACT.Copy), key)
                bank = wait_filled(act, (f"end{tc}", "sa"))
                drain(act_fn(sa[:, :], bank[:, :], ACT.Copy), (f"end{tc}", "sa"))
            for j in range(2):
                bank = wait_filled(act, ("lorag", j))
                drain(act_fn(flat(gg[:, 2 * j:2 * j + 2, :]), bank[:, :], ACT.Copy), ("lorag", j))
            wait_drained(act, ("end1", "y"))
            act_fn(sqr[:, 0:4, :], yy[:, :, :], ACT.Square).then_inc(sig("y_sq"), 1)
            act.wait_ge(sig("y_inv"), 1)
            act_fn(res[:, 4:8, :], res[:, 4:8, :], ACT.Sqrt).then_inc(sig("y_rstd"), 1)
            act.wait_ge(sig("y_done"), 1)
            act_fn(yh[:, 0:4, :], yy[:, :, :], ACT.Copy).then_inc(sig("y_hi"), 1)

            for j in range(8):
                cuts("sbqk", j)
                bank = wait_filled(act, ("sbqk", j))
                if j == 0:
                    act.wait_ge(sig("y_cut"), 1)
                drain(act_fn(sbt[:, j, :], bank[:, 0:T], ACT.Copy), ("sbqk", j))
            wait_drained(act, ("sbqk", 7))
            for j in range(4, 8):
                wait_drained(act, ("sbqk", j))
            act_fn(flat(sqr), flat(sbt[:, 0:8, :]), ACT.Square).then_inc(sig("head_sq"), 1)
            act.wait_ge(sig("head_inv"), 1)
            act_fn(flat(res), flat(res), ACT.Sqrt).then_inc(sig("head_rstd"), 1)
            for j in range(4):
                cuts("sbv", j)
            for t in range(2):
                bank = wait_filled(act, ("sbv", t))
                drain(act_fn(vsb[:, t, :], bank[:, :], ACT.Copy), ("sbv", t))
            for h in range(8):
                act.wait_ge(sig("sb_abs"), h + 1)
                own.link(act_fn(e8[:, h, :], e8[:, h, :], ACT.Exp, scale=-1.0))
            for h in range(8):
                act_fn(e8[:, h, :], e8[:, h, :], ACT.Ln, bias=1.0).then_inc(sig("sb_ln"), 1)
            for t in range(10):
                if t < 8:
                    wait_drained(act, ("sbo", ("b", t)))
                    act_fn(z8[:, t, :], z8[:, t, :], ACT.Exp).then_inc(sig("sb_exp"), 1)
                if t >= 2 and (t + 1) % 2 == 0:
                    key = ("sbo", ("o", t))
                    bank = wait_filled(act, key)
                    act_fn(yh[:, 4 + (t - 3) // 2, :], bank[:, 0:T], ACT.Copy).then_inc(sig("sbo_hi"), 1)

            for j in range(4):
                cuts("memq", j)
                bank = wait_filled(act, ("memq", j))
                drain(act_fn(sbt[:, 8 + j, :], bank[:, 0:T], ACT.Copy), ("memq", j))
            for j in range(4):
                wait_drained(act, ("memq", j))
            own.link(act_fn(sqr[:, 0:4, :], sbt[:, 8:12, :], ACT.Square))
            act_fn(sqr[:, 4:8, :], km[:, :, :], ACT.Square).then_inc(sig("head_sq"), 1)
            act.wait_ge(sig("head_inv"), 2)
            act_fn(flat(res), flat(res), ACT.Sqrt).then_inc(sig("head_rstd"), 1)
            for t in range(4 + 3):
                if 0 <= t - 2 < 4:
                    key_major("mem", t - 2, 512)
                if 0 <= t - 3:
                    bank = wait_filled(act, ("mem", ("o", t - 3)))
                    act_fn(yh[:, 8 + t - 3, :], bank[:, 0:T], ACT.Copy).then_inc(sig("memo_hi"), 1)
                if t < 4:
                    probabilities("mem", t, (slice(0, T), slice(T, 2 * T)))

            with act.Fori(0, 6) as it:
                for r in range(4):
                    cuts("gate", r, it, 4)
                    bank = wait_filled(act, ("gate", r), it, 4)
                    drain(act_fn(flat(gates[:, bass.ds(it * 4 + r, 1), :]), bank[:, 0:T], ACT.Sigmoid), ("gate", r))
            with act.Fori(0, 3) as it:
                for r in range(4):
                    cuts("branch", r, it, 4)
            cut_x(res, merged=True)
            for j in range(DC):
                cuts("out", j)
                wait_drained(act, ("out", j))
                act_fn(sqr[:, j, :], x[:, j, :], ACT.Square).then_inc(sig("squared"), 1)
            root()
            cut_x(res)

            act.wait_ge(sig("cg_zero"), 2)

            def ffn_hidden(f, it=None):
                bank = wait_filled(act, ("ffn", 2 * f), it, 8)
                act_fn(cg[:, f % 2, 2:T + 2], bank[:, 0:T], ACT.Copy).then_inc(sig("conv_in"), 1)
                bank = wait_filled(act, ("ffn", 2 * f + 1), it, 8)
                act_fn(cv[:, f % 2, 2:T + 2], bank[:, 0:T], ACT.Copy).then_inc(sig("conv_in"), 1)
                wait_drained(act, ("ffn", 2 * f), it, 8)
                act_fn(fs[:, f % 2, :], fa[:, f % 2, :], ACT.Sigmoid).then_inc(sig("sigm"), 1)
                act.wait_ge(sig("ffn_prod"), f + 1 if it is None else it * 4 + (f + 1))
                act_fn(hh[:, f % 2, :], hb[:, f % 2, :], ACT.Copy).then_inc(sig("ffn_hi"), 1)

            cuts("ffn", 0)
            cuts("ffn", 1)
            ffn_hidden(0)

            def ffn_step(f, it=None):
                cuts("ffn", 3 * f + 2, it, 12)
                cuts("ffn", 3 * f + 3, it, 12)
                ffn_hidden(f + 1, it)
                cuts("ffn", 3 * f + 4, it, 12)

            rounds = (FC2 - 1) // 4
            with act.Fori(0, rounds) as it:
                for f in range(4):
                    ffn_step(f, it)
            for f in range(4 * rounds, FC2 - 1):
                ffn_step(f)
        @block.vector
        def _(dve):
            own = Tally(dve, sig("dve_step"))
            tt, ts, stt = nc.vector.tensor_tensor, nc.vector.tensor_scalar, nc.vector.scalar_tensor_tensor
            count = {"norm": 0, "x_hi": 0}

            def cut(n, it=None, per=0):
                if n >= NSLOT:
                    return
                dve.wait_ge(cut_hi, n + 1 if it is None else it * per + (n + 1))
                tt(wlo[:, n % RING, :], raw[:, n % RING, :], whi[:, n % RING, :].bitcast(F32), ALU.subtract).then_inc(cut_lo, 1)

            def cuts(stage, s, it=None, per=0):
                cut(SLOT[stage] + s + AHEAD, it, per)

            def minus(dst, src, hi):
                return tt(dst, src, hi.bitcast(F32), ALU.subtract)

            def finish(ins, key):
                drain(ins, key)
                wait_drained(dve, key)

            def norm_stats(name, centred=True):
                if centred:
                    bank = wait_filled(dve, (name, 0))
                    finish(ts(stat[:, 0, :], bank[:, 0:T], 1.0 / D, None, ALU.mult), (name, 0))
                    own.link(tt(stat[:, 1, :], stat[:, 0, :], stat[:, 0, :], ALU.mult))
                    bank = wait_filled(dve, (name, 1))
                    finish(stt(stat[:, 2, :], bank[:, 0:T], 1.0 / D, stat[:, 1, :], ALU.mult, ALU.subtract), (name, 1))
                    own.link(ts(stat[:, 2, :], stat[:, 2, :], LN_EPS, None, ALU.add))
                else:
                    bank = wait_filled(dve, (name, 0))
                    finish(ts(stat[:, 2, :], bank[:, 0:T], 1.0 / D, RMS_EPS, ALU.mult, ALU.add), (name, 0))
                count["norm"] += 1
                nc.vector.reciprocal(stat[:, 2, :], stat[:, 2, :]).then_inc(sig("rinv"), 1)
                dve.wait_ge(sig("rstd"), count["norm"])

            def two(ap):
                return ap.broadcast_to([P, 2, T])

            def low_x(src, c):
                count["x_hi"] += 1
                dve.wait_ge(sig("x_hi"), count["x_hi"])
                minus(xl[:, 2 * c:2 * c + 2, :], src[:, 2 * c:2 * c + 2, :], xh[:, 2 * c:2 * c + 2, :]).then_inc(sig("x_normed"), 1)

            def layer_norm(name, g, b, col, cut_after=True, hooks=None):
                norm_stats(name)
                for c in range(5):
                    if c < 4:
                        pair = res[:, 2 * c:2 * c + 2, :]
                        own.link(tt(pair, pair, two(stat[:, 0:1, :]), ALU.subtract))
                        own.link(tt(pair, pair, two(stat[:, 3:4, :]), ALU.mult))
                        own.link(ts(x[:, 2 * c, :], res[:, 2 * c, :], G(g, col + 2 * c), G(b, col + 2 * c), ALU.mult, ALU.add))
                        ts(x[:, 2 * c + 1, :], res[:, 2 * c + 1, :], G(g, col + 2 * c + 1), G(b, col + 2 * c + 1), ALU.mult, ALU.add)\
                            .then_inc(sig("x_ready" if cut_after else "x_out"), 1)
                    if c and cut_after:
                        low_x(x, c - 1)
                        if hooks:
                            hooks(c - 1)

            def rms_norm(name, g):
                norm_stats(name, False)
                for c in range(5):
                    if c < 4:
                        for d in range(2):
                            last = stt(res[:, 2 * c + d, :], x[:, 2 * c + d, :], G(g, 2 * c + d), stat[:, 3, :], ALU.mult, ALU.mult)
                            if d == 0:
                                own.link(last)
                        last.then_inc(sig("x_ready"), 1)
                    if c:
                        low_x(res, c - 1)

            dve.wait_ge(sig("x0_hi"), 1)
            minus(flat(xl), flat(x), flat(xh)).then_inc(sig("x_cut"), 1)
            for n in range(AHEAD):
                cut(n)
            dve.wait_ge(sig("par_loaded"), 16)
            own.link(ts(nsink[:, :], par[:, PCOL["sinks"]:PCOL["sinks"] + 16], -1.0, None, ALU.mult))
            bank = wait_filled(dve, ("brow", 0))
            dve.wait_ge(sig("band_loaded"), 32)
            drain(tt(brow, bank[0:16, 0:384], bandt[0:16, 1, :], ALU.add), ("brow", 0))
            dve.wait_ge(sig("con_loaded"), 16)
            for j in range(7):
                cuts("in", j)
                if j < 5:
                    dve.wait_ge(sig("in_sq"), j + 1)
                    drain(nc.vector.tensor_copy(hraw[:, j, :], work[RESULT[("in", j)] % 4][:, 0:T]), ("in", j))
                elif j == 5:
                    bank = wait_filled(dve, ("in", 5))
                    drain(tt(ha[:, 0, :], bank[:, 0:T], C("cos", T), ALU.mult), ("in", 5))
                else:
                    bank = wait_filled(dve, ("in", 6))
                    finish(tt(ha[:, 1, :], bank[:, 0:T], C("sin", T), ALU.mult), ("in", 6))
                    wait_drained(dve, ("in", 5))
                    tt(kr[:, :], ha[:, 0, :], ha[:, 1, :], ALU.add).then_inc(sig("kr_ready"), 1)
                if j == 3:
                    bank = wait_filled(dve, ("memstat", 0))
                    finish(ts(mst[:, :], bank[:, 0:T], 1.0 / D, RMS_EPS, ALU.mult, ALU.add), ("memstat", 0))
                    nc.vector.reciprocal(mst[:, :], mst[:, :]).then_inc(sig("mem_inv"), 1)
                if j >= 4:
                    dve.wait_ge(sig("mem_rstd"), 1)
                    for c in ((0, 1), (2,), (3,))[j - 4]:
                        own.link(stt(memc(2 * c), memc(2 * c), G("mem_g", 2 * c), mst[:, :], ALU.mult, ALU.mult))
                        stt(memc(2 * c + 1), memc(2 * c + 1), G("mem_g", 2 * c + 1), mst[:, :], ALU.mult, ALU.mult)\
                            .then_inc(sig("mem_ready"), 1)
            for c in range(4):
                dve.wait_ge(sig("mem_hi"), c + 1)
                minus(meml[:, 2 * c:2 * c + 2, :], mem2(c), memh[:, 2 * c:2 * c + 2, :]).then_inc(sig("mem_cut"), 1)
            cuts("memk", 0)
            bank = wait_filled(dve, ("mlastat", 0))
            own.link(ts(stat[:, 0, :], bank[:, 0:T], 1.0 / Q_RANK, RMS_EPS, ALU.mult, ALU.add))
            finish(ts(stat[:, 1, :], bank[:, T:2 * T], 1.0 / KV_RANK, RMS_EPS, ALU.mult, ALU.add), ("mlastat", 0))
            nc.vector.reciprocal(stat[:, 0:2, :], stat[:, 0:2, :]).then_inc(sig("mla_inv"), 1)
            dve.wait_ge(sig("mla_rstd"), 1)
            for j in range(3):
                wait_drained(dve, ("in", j))
                last = stt(hraw[:, j, :], hraw[:, j, :], G("g_q", j), stat[:, 2, :], ALU.mult, ALU.mult)
            last.then_inc(sig("cq_ready"), 1)
            for j in range(2):
                wait_drained(dve, ("in", 3 + j))
                stt(ckv[:, j, :], hraw[:, 3 + j, :], G("g_kv", j), stat[:, 3, :], ALU.mult, ALU.mult).then_inc(sig("ckv_ready"), 1)
            dve.wait_ge(sig("cq_hi"), 1)
            minus(flat(cql), flat(hraw[:, 0:3, :]), flat(cqh)).then_inc(sig("cq_cut"), 1)
            for j in range(1, 4):
                cuts("memk", j)
            for j in range(16):
                for s in range(6):
                    if 3 * j <= 8 * s < 3 * j + 3:
                        cuts("q", s)
                key = ("q", j)
                if j < 8:
                    dve.wait_ge(sig("qn_hi"), j + 1)
                    drain(minus(qnl[:, j, :], work[RESULT[key] % 4][:, 0:T], qnh[:, j, :]), key)
                elif j % 2 == 0:
                    bank = wait_filled(dve, key)
                    finish(tt(ha[:, 0, :], bank[:, 0:T], C("cos", T), ALU.mult), key)
                else:
                    bank = wait_filled(dve, key)
                    finish(tt(ha[:, 1, :], bank[:, 0:T], C("sin", T), ALU.mult), key)
                    tt(qr[:, j // 2 - 4, :], ha[:, 0, :], ha[:, 1, :], ALU.add).then_inc(sig("qr_ready"), 1)
                    dve.wait_ge(sig("qr_ready"), j // 2 - 3)
            dve.wait_ge(sig("brow_stored"), 16)
            for h in range(8):
                if h % 4 == 0:
                    cuts("uk", h // 4)
                if h % 2:
                    bank = wait_filled(dve, ("qlat", h))
                    drain(nc.vector.tensor_copy(qlat[:, h, :], bank[:, :]), ("qlat", h))

            def scores(stage, h, parts, scale, added, sink=None):
                p = h % 2
                bank = wait_filled(dve, (stage, ("s", h)))
                n = len(added)
                for a, (cols, extra) in enumerate(added):
                    if extra is None:
                        ins = ts(sc[:, p, cols], bank[:, cols], scale, None, ALU.mult)
                    else:
                        ins = stt(sc[:, p, cols], bank[:, cols], scale, extra, ALU.mult, ALU.add)
                    if a == n - 1:
                        finish(ins, (stage, ("s", h)))
                    else:
                        own.link(ins)
                for b, cols in enumerate(parts):
                    last = nc.vector.tensor_reduce(sm[:, p, b:b + 1], sc[:, p, cols], AX.X, ALU.max, negate=True)
                    if b == 0 or sink is not None:
                        own.link(last)
                if sink is not None:
                    last = ts(sm[:, p, 0:2], sm[:, p, 0:2], sink, None, ALU.min)
                last.then_inc(sig(f"{stage}_max"), 1)

            def normalise(stage, h, parts, sink=False):
                p = h % 2
                dve.wait_ge(sig(f"{stage}_exp"), h + 1)
                if sink:
                    own.link(tt(sm[:, p, 2:4], sm[:, p, 2:4], sm[:, p, 4:6], ALU.add))
                own.link(nc.vector.reciprocal(sm[:, p, 6:8], sm[:, p, 2:4]))
                for b, cols in enumerate(parts):
                    last = ts(pr[:, p, cols], pr[:, p, cols], sm[:, p, 6 + b:7 + b], None, ALU.mult)
                    if b == 0:
                        own.link(last)
                last.then_inc(sig(f"{stage}_norm"), 1)

            three = (slice(0, P), slice(P, 3 * P))
            for t in range(MLA_H + 4):
                if t >= 4 and (t - 4) % 4 == 0:
                    cuts("uv", (t - 4) // 4)
                if t < MLA_H:
                    scores("mla", t, three, (NOPE + ROPE) ** -0.5, [(slice(0, 384), C("causal", 384))])
                if 0 <= t - 1 < MLA_H:
                    normalise("mla", t - 1, three)
                if t >= 4:
                    key = ("mla", ("u", t - 4))
                    dve.wait_ge(sig("oh_hi"), t - 3)
                    drain(minus(ol[:, t - 4, :], work[RESULT[key] % 4][:, 0:T], oh[:, t - 4, :]), key)
                if 0 <= t - 3 < MLA_H:
                    key = ("mla", ("o", t - 3))
                    dve.wait_ge(sig("ol_hi"), t - 2)
                    drain(minus(oll[:, :], work[RESULT[key] % 4][:, :], olh[:, :]), key)

            def residual(stage):
                for j in range(DC):
                    cuts(stage, j)
                    bank = wait_filled(dve, (stage, j))
                    drain(stt(res[:, j, :], x[:, j, :], ALPHA, bank[:, 0:T], ALU.mult, ALU.add), (stage, j))

            def mlp(stage, units_before, name):
                def hidden(f, it=None):
                    done = units_before + f + 1
                    n = RESULT[(stage, f)]
                    dve.wait_ge(sig("relu"), done if it is None else it * 4 + done)
                    tt(hb[:, f % 2, :], ha[:, f % 2, :], ha[:, f % 2, :], ALU.mult).then_inc(sig("h_squared"), 1)
                    dve.wait_ge(sig("h_squared"), done if it is None else it * 4 + done)
                    dve.wait_ge(sig("h_hi"), done if it is None else it * 4 + done)
                    drain(minus(hl[:, f % 2, :], hb[:, f % 2, :], hh[:, f % 2, :]), (stage, f))

                cuts(stage, 0)
                hidden(0)

                def step(f, it=None):
                    cuts(stage, 2 * f + 1, it, 8)
                    hidden(f + 1, it)
                    cuts(stage, 2 * f + 2, it, 8)

                rounds = (FC - 1) // 4
                with dve.Fori(0, rounds) as it:
                    for f in range(4):
                        step(f, it)
                for f in range(4 * rounds, FC - 1):
                    step(f)
                cuts(stage, 2 * FC - 1)
                dve.wait_ge(sig("acc_full"), units_before // FC + 1)
                for b in range(4):
                    stt(res[:, 2 * b:2 * b + 2, :], x[:, 2 * b:2 * b + 2, :], ALPHA, acc[b][:, :].rearrange("p (a t) -> p a t", a=2),
                        ALU.mult, ALU.add).then_inc(sig(f"{name}_sum"), 1)
                dve.wait_ge(sig(f"{name}_sum"), 4)

            residual("wo")
            layer_norm("ln0", "ln_mix_g", "ln_mix_b", 0, True, lambda c: cuts("memv", c) if c < 2 else None)
            for j in range(2, 4):
                cuts("memv", j)
            mlp("mlp0", 0, "ln1")
            layer_norm("ln1", "ln_mlp_g", "ln_mlp_b", 0)
            for j in range(8):
                cuts("swaq", j)
            for j in range(2):
                cuts("swak", j)
            for j in range(2):
                cuts("swav", j)
            dve.wait_ge(sig("bias_loaded"), 16)
            for t in range(SWA_H + 3):
                if t < SWA_H:
                    h = SWA_ORDER[t]
                    scores("swa", t, three, SWA_D ** -0.5, [(slice(0, P), bias[:, h, P - 1::-1]), (slice(P, 384), bias[:, h, ::-1])],
                           nsink[:, h:h + 1])
                if 0 <= t - 1 < SWA_H:
                    normalise("swa", t - 1, three, True)
                if 0 <= t - 3 and (t - 3) % 2:
                    key = ("swa", ("opair", t - 3))
                    dve.wait_ge(sig("oh_hi"), 8 + (t - 3) // 2 + 1)
                    drain(minus(ol[:, (t - 3) // 2, :], work[RESULT[key] % 4][:, 0:T], oh[:, (t - 3) // 2, :]), key)
            residual("swao")
            layer_norm("ln2", "ln_mix_g", "ln_mix_b", 8)
            mlp("mlp1", FC, "ln3")
            layer_norm("ln3", "ln_mlp_g", "ln_mlp_b", 8, False)
            dve.wait_ge(sig("x_out"), 4)

            rms_norm("rms1", "norm1")
            dve.wait_ge(sig("pb_zero"), 2)
            for j in range(14):
                cuts("rwkv", j)
                dve.wait_ge(sig("pb_full"), j + 1)
                own.link(tt(ha[:, j % 2, :], pb[:, j % 2, 0:T], pb[:, j % 2, 1:T + 1], ALU.subtract))
                drain(stt(rkv[:, j, :], ha[:, j % 2, :], G("mu", j), pb[:, j % 2, 1:T + 1], ALU.mult, ALU.add), ("rwkv", j))
            for j in range(12):
                wait_drained(dve, ("rwkv", j))
            k_, r_, v_ = rkv[:, 0:4, :], rkv[:, 4:8, :], rkv[:, 8:12, :]
            for c in range(4):
                last = ts(kk[:, c, :], k_[:, c, :], G("k_k", c), None, ALU.mult)
                if c < 3:
                    own.link(last)
            last.then_inc(sig("kk_raw"), 1)
            for j in range(2):
                wait_drained(dve, ("loraw", j))
            for c in range(8):
                own.link(nc.vector.tensor_tensor_scan(out=cum[:, c, 1:129], data0=C("ones"), data1=em[:, c, :], initial=0.0,
                                                      op0=ALU.mult, op1=ALU.add))
            own.link(ts(mid[:, 0, :], cum[:, :, 64], KAPPA, None, ALU.mult))
            own.link(ts(mid[:, 1, :], cum[:, :, 64], -KAPPA, None, ALU.mult))
            ts(mid[:, 2, :], cum[:, :, 64], 1.0, None, ALU.mult).then_inc(sig("cum_ready"), 1)
            dve.wait_ge(sig("cum_ready"), 1)
            halves = cum[:, :, :].rearrange("p (c a) t -> p c a t", a=2)
            own.link(tt(fac[:, :], halves[:, :, 0, 128], halves[:, :, 0, 64], ALU.subtract))
            tt(fac[:, :], fac[:, :], halves[:, :, 1, 64], ALU.add).then_inc(sig("fac_ready"), 1)
            for j in range(2):
                wait_drained(dve, ("loraa", j))
            for c in range(4):
                own.link(ts(sqr[:, 4 + c, :], aa[:, c, :], -1.0, G("k_a", c), ALU.add, ALU.mult))
            own.link(stt(k_, sqr[:, 4:8, :], 1.0, k_, ALU.add, ALU.mult))
            for c in range(4):
                last = stt(sqr[:, 4 + c, :], r_[:, c, :], G("r_k", c), k_[:, c, :], ALU.mult, ALU.mult)
                if c < 3:
                    own.link(last)
            last.then_inc(sig("rk_prod"), 1)
            dve.wait_ge(sig("kk_sq"), 1)
            for j in range(2):
                bank = wait_filled(dve, ("kknorm", j))
                finish(ts(sqr[:, 2 * j:2 * j + 2, :], bank[:, :].rearrange("p (a t) -> p a t", a=2), 1e-24, None, ALU.max), ("kknorm", j))
            nc.vector.reciprocal(sqr[:, 0:4, :], sqr[:, 0:4, :]).then_inc(sig("kk_inv"), 1)
            for j in range(2):
                bank = wait_filled(dve, ("bonus", j))
                drain(tt(bon[:, 2 * j:2 * j + 2, :], v_[:, 2 * j:2 * j + 2, :], bank[:, :].rearrange("p (a t) -> p a t", a=2), ALU.mult), ("bonus", j))
            dve.wait_ge(sig("kk_rstd"), 1)
            own.link(tt(kk[:, :, :], kk[:, :, :], sqr[:, 0:4, :], ALU.mult))
            own.link(tt(aa[:, :, :], aa[:, :, :], kk[:, :, :], ALU.mult))
            dve.wait_ge(sig("exps"), 1)

            def eight(ap):
                return ap.rearrange("p c (a t) -> p (c a) t", a=2)

            own.link(tt(eight(kk[:, :, :]), eight(kk[:, :, :]), ep[:, :, 0:128], ALU.mult))
            own.link(tt(eight(r_), eight(r_), ep[:, :, 1:129], ALU.mult))
            own.link(tt(eight(aa[:, :, :]), eight(aa[:, :, :]), em[:, :, :], ALU.mult))
            tt(eight(k_), eight(k_), em[:, :, :], ALU.mult).then_inc(sig("factors"), 1)
            dve.wait_ge(sig("fac_exp"), 1)
            dve.wait_ge(sig("factors"), 1)

            for tc in range(2):
                for g in range(2):
                    def masked(m, dst, mask, *_):
                        key = (f"mat{tc}", (m, g))
                        bank = wait_filled(dve, key)
                        finish(tt(four(dst), four(bank[:, :]), mask4(mask), ALU.mult), key)
                    masked("at", at[:, g, :], C("before"))
                    own.link(tt(four(uinv[:, g, :]), four(at[:, g, :]), mask4(C("level")), ALU.mult))
                    own.link(tt(four(uinv[:, g, :]), mask4(C("ident")), four(uinv[:, g, :]), ALU.subtract))
                    masked("a0", tinv[:, g, :], C("level0t"))
                    own.link(tt(four(tinv[:, g, :]), mask4(C("ident")), four(tinv[:, g, :]), ALU.subtract))
                    masked("kk", kkm[:, g, :], C("before"))
                    masked("rb", rb[:, g, :], C("upto"))
                    masked("rk", rk[:, g, :], C("upto"))
                for l in range(1, 7):
                    for g in range(2):
                        tt(four(sc[:, g, :]), four(at[:, g, :]), mask4(C("level", P, l * P)), ALU.mult).then_inc(sig("inv_mask"), 1)
                        count["mask"] = count.get("mask", 0) + 1
                        dve.wait_ge(sig("inv_mask"), count["mask"])
                    for g in range(2):
                        if l < 6:
                            key = (f"inv{tc}", (l, "d", g))
                            bank = wait_filled(dve, key)
                            finish(tt(tinv[:, g, :], tinv[:, g, :], bank[:, :], ALU.subtract), key)
                        key = (f"inv{tc}", (l, "dt", g))
                        bank = wait_filled(dve, key)
                        finish(tt(uinv[:, g, :], uinv[:, g, :], bank[:, :], ALU.subtract), key)
                for g in range(2):
                    key = (f"end{tc}", f"rhs{g}")
                    bank = wait_filled(dve, key)
                    drain(ts(rhs[:, g * T:(g + 1) * T], bank[:, 0:T], -1.0, None, ALU.mult), key)
                key = (f"end{tc}", "y")
                bank = wait_filled(dve, key)
                finish(nc.vector.tensor_copy(yy[:, :, half(tc)], four(bank[:, :])), key)
                if tc == 0:
                    key = ("end0", "state")
                    bank = wait_filled(dve, key)
                    for c in range(4):
                        last = ts(st[:, c, :], bank[:, c * 64:c * 64 + 64], fac[:, c:c + 1], None, ALU.mult)
                    drain(last, key)

            mean, inv = res[:, 0:4, :], res[:, 4:8, :]
            for j in range(2):
                bank = wait_filled(dve, ("ynorm", j))
                finish(ts(mean[:, 2 * j:2 * j + 2, :], bank[:, :].rearrange("p (a t) -> p a t", a=2), 1.0 / RW_D, None, ALU.mult), ("ynorm", j))
            own.link(tt(sqr[:, 4:8, :], mean, mean, ALU.mult))
            for j in range(2):
                bank = wait_filled(dve, ("ynorm", 2 + j))
                finish(stt(inv[:, 2 * j:2 * j + 2, :], bank[:, :].rearrange("p (a t) -> p a t", a=2), 1.0 / RW_D,
                           sqr[:, 4 + 2 * j:6 + 2 * j, :], ALU.mult, ALU.subtract), ("ynorm", 2 + j))
            own.link(ts(inv, inv, LNX_EPS, None, ALU.add))
            nc.vector.reciprocal(inv, inv).then_inc(sig("y_inv"), 1)
            own.link(tt(yy[:, :, :], yy[:, :, :], mean, ALU.subtract))
            dve.wait_ge(sig("y_rstd"), 1)
            own.link(tt(yy[:, :, :], yy[:, :, :], inv, ALU.mult))
            for c in range(4):
                own.link(ts(yy[:, c, :], yy[:, c, :], G("lnx_g", c), G("lnx_b", c), ALU.mult, ALU.add))
            own.link(tt(yy[:, :, :], yy[:, :, :], bon[:, :, :], ALU.add))
            for j in range(2):
                wait_drained(dve, ("bonus", j))
                wait_drained(dve, ("lorag", j))
            tt(yy[:, :, :], yy[:, :, :], gg[:, :, :], ALU.mult).then_inc(sig("y_done"), 1)
            dve.wait_ge(sig("y_done"), 1)
            dve.wait_ge(sig("y_hi"), 1)
            minus(yl[:, 0:4, :], yy[:, :, :], yh[:, 0:4, :]).then_inc(sig("y_cut"), 1)

            def head_norm(stage, width, pieces, units):
                for j in range(4):
                    key = (stage, j)
                    bank = wait_filled(dve, key)
                    finish(ts(res[:, 2 * j:2 * j + 2, :], bank[:, :].rearrange("p (a t) -> p a t", a=2), 1.0 / width, RMS_EPS, ALU.mult, ALU.add), key)
                nc.vector.reciprocal(res[:, :, :], res[:, :, :]).then_inc(sig("head_inv"), 1)
                dve.wait_ge(sig("head_rstd"), units)
                for j, (ap, g) in enumerate(pieces):
                    stt(ap, ap, G(g), res[:, j, :], ALU.mult, ALU.mult).then_inc(sig("sb_normed" if stage == "sbnorm" else "mem_normed"), 1)

            for j in range(8):
                cuts("sbqk", j)
            head_norm("sbnorm", RW_D, [(sbt[:, j, :], "sbq_g" if j < 4 else "sbk_g") for j in range(8)], 1)
            for j in range(4):
                cuts("sbv", j)
            for h in range(8):
                bank = wait_filled(dve, ("sbz", h))
                finish(ts(z8[:, h, :], bank[:, 0:384], RW_D ** -0.5, None, ALU.mult), ("sbz", h))
                stt(e8[:, h, :], z8[:, h, :], -1.0, z8[:, h, :], ALU.mult, ALU.max).then_inc(sig("sb_abs"), 1)

            def diagonals(ap):
                b = ap.rearrange("p (a t) -> p a t", t=P)
                return b[:, 0:3:2, :]

            def masked_diagonals(ap):
                return tt(diagonals(ap), diagonals(ap), C("before").rearrange("p (a t) -> p a t", a=1).broadcast_to([P, 2, P]), ALU.mult)

            for h in range(8):
                dve.wait_ge(sig("sb_ln"), h + 1)
                own.link(stt(spc(h), z8[:, h, :], 0.0, e8[:, h, :], ALU.max, ALU.add))
                own.link(stt(z8[:, h, :], z8[:, h, :], 0.0, e8[:, h, :], ALU.min, ALU.subtract))
                masked_diagonals(spc(h)).then_inc(sig("softplus"), 1)
            for t in range(10):
                if t < 8:
                    key = ("sbo", ("b", t))
                    bank = wait_filled(dve, key)
                    finish(tt(z8[:, t, :], z8[:, t, :], bank[:, 0:384], ALU.subtract), key)
                if 0 <= t - 1 < 8:
                    dve.wait_ge(sig("sb_exp"), t)
                    masked_diagonals(z8[:, t - 1, :]).then_inc(sig("sb_attn"), 1)
                if t >= 3 and t % 2:
                    key = ("sbo", ("o", t))
                    dve.wait_ge(sig("sbo_hi"), (t - 3) // 2 + 1)
                    c = 4 + (t - 3) // 2
                    drain(minus(yl[:, c, :], work[RESULT[key] % 4][:, 0:T], yh[:, c, :]), key)

            for j in range(4):
                cuts("memq", j)
            head_norm("memnorm", P, [(sbt[:, 8 + j, :], "memq_g") for j in range(4)] + [(km[:, j, :], "memk_g") for j in range(4)], 2)
            wide = (slice(0, T), slice(T, 2 * T))
            for t in range(4 + 3):
                if t < 4:
                    scores("mem", t, wide, P ** -0.5, [(slice(0, 512), None)])
                if 0 <= t - 1 < 4:
                    normalise("mem", t - 1, wide)
                if t >= 3:
                    key = ("mem", ("o", t - 3))
                    dve.wait_ge(sig("memo_hi"), t - 2)
                    drain(minus(yl[:, 8 + t - 3, :], work[RESULT[key] % 4][:, 0:T], yh[:, 8 + t - 3, :]), key)

            with dve.Fori(0, 6) as it:
                for r in range(4):
                    cuts("gate", r, it, 4)
            own.link(nc.vector.memset(res[:, :, :], 0.0))
            for r in range(4):
                wait_drained(dve, ("gate", 20 + r))
            with dve.Fori(0, 3) as it:
                for r in range(8):
                    if r % 2 == 0:
                        cuts("branch", r // 2, it, 4)
                    bank = wait_filled(dve, ("branch", r), it, 8)
                    drain(tt(hb[:, r % 2, :], flat(gates[:, bass.ds(it * 8 + r, 1), :]), bank[:, 0:T], ALU.mult), ("branch", r))
                    wait_drained(dve, ("branch", r), it, 8)
                    tt(res[:, r, :], res[:, r, :], hb[:, r % 2, :], ALU.add).then_inc(sig("merged"), 1)
                    dve.wait_ge(sig("merged"), it * 8 + (r + 1))
            for c in range(4):
                low_x(res, c)
            for j in range(DC):
                cuts("out", j)
                bank = wait_filled(dve, ("out", j))
                finish(tt(x[:, j, :], x[:, j, :], bank[:, 0:T], ALU.add), ("out", j))
            rms_norm("rms2", "norm2")

            dve.wait_ge(sig("cg_zero"), 2)

            def conv(dst, src, chunk_, it, f, is_value):
                def tap(name):
                    col = PCOL[name] + f + (FC2 if is_value else 0)
                    if it is None:
                        return par[:, col:col + 1]
                    return par[:, bass.ds(it * 4 + col, 1)]
                own.link(ts(dst, src[:, 2:T + 2], tap("conv2"), tap("conv_b"), ALU.mult, ALU.add))
                own.link(stt(dst, src[:, 1:T + 1], tap("conv1"), dst, ALU.mult, ALU.add))
                return stt(dst, src[:, 0:T], tap("conv0"), dst, ALU.mult, ALU.add)

            def ffn_hidden(f, it=None):
                def upto(n, per):
                    return n if it is None else it * per + n
                p = f % 2
                dve.wait_ge(sig("conv_in"), upto(2 * f + 1, 8))
                drain(conv(fa[:, p, :], cg[:, p, :], f, it, f, False), ("ffn", 2 * f))
                wait_drained(dve, ("ffn", 2 * f), it, 8)
                dve.wait_ge(sig("conv_in"), upto(2 * f + 2, 8))
                own.link(conv(fb[:, p, :], cv[:, p, :], f, it, f, True))
                own.link(tt(fb[:, p, :], fb[:, p, :], fa[:, p, :], ALU.mult))
                dve.wait_ge(sig("sigm"), upto(f + 1, 4))
                tt(hb[:, p, :], fb[:, p, :], fs[:, p, :], ALU.mult).then_inc(sig("ffn_prod"), 1)
                dve.wait_ge(sig("ffn_hi"), upto(f + 1, 4))
                drain(minus(hl[:, p, :], hb[:, p, :], hh[:, p, :]), ("ffn", 2 * f + 1))

            cuts("ffn", 0)
            cuts("ffn", 1)
            ffn_hidden(0)

            def ffn_step(f, it=None):
                cuts("ffn", 3 * f + 2, it, 12)
                cuts("ffn", 3 * f + 3, it, 12)
                ffn_hidden(f + 1, it)
                cuts("ffn", 3 * f + 4, it, 12)

            rounds = (FC2 - 1) // 4
            with dve.Fori(0, rounds) as it:
                own.enter(it, 4 * 6)
                for f in range(4):
                    ffn_step(f, it)
                own.leave(rounds)
            for f in range(4 * rounds, FC2 - 1):
                ffn_step(f)
            dve.wait_ge(sig("acc_full"), 3)
            for b in range(4):
                tt(res[:, 2 * b:2 * b + 2, :], x[:, 2 * b:2 * b + 2, :], acc[b][:, :].rearrange("p (a t) -> p a t", a=2), ALU.add)\
                    .then_inc(sig("final"), 1)


def _tiles(m):
    return m.reshape(m.shape[0] // P, P, m.shape[1] // P, P)


def _columns(m):
    t = _tiles(m).transpose(2, 1, 0, 3)
    return t.reshape(-1, P, 1024)


def _rows(m):
    t = m.reshape(m.shape[0] // P, P, m.shape[1]).transpose(1, 0, 2).reshape(P, -1, 1024)
    return t.transpose(1, 0, 2)


def _packed(tiles):
    t = np.stack(tiles).reshape(-1, 8, P, P).transpose(0, 2, 1, 3)
    return t.reshape(-1, P, 1024)


def _stream(i):
    swap = np.r_[32:64, 0:32]
    w_in = i["mla_w_in"][0]
    kr = w_in[:, Q_RANK + KV_RANK:]
    parts = {"in": _columns(np.concatenate([w_in[:, :Q_RANK + KV_RANK], kr, kr, kr[:, swap], kr[:, swap]], 1))}
    mem = i["w_mem_kv_2"][0]
    parts["memk"] = _columns(mem[:, :512])
    parts["memv"] = _rows(mem[:, 512:])
    uq = i["mla_w_uq"][0]
    nope = [uq[:, h, :NOPE] for h in range(MLA_H)]
    rope = uq[:, :, NOPE:]
    pairs = []
    for c in range(4):
        for r in (rope, rope[:, :, swap]):
            pairs.append(r[:, 2 * c:2 * c + 2].reshape(Q_RANK, P))
    parts["q"] = _packed([m[k * P:(k + 1) * P] for m in nope + pairs for k in range(3)])
    uk = i["mla_w_uk"][0].transpose(1, 2, 0)
    parts["uk"] = _packed([uk[h, :, c * P:(c + 1) * P] for h in range(MLA_H) for c in range(2)])
    uv = i["mla_w_uv"][0]
    parts["uv"] = _packed([uv[c * P:(c + 1) * P, h, :] for h in range(MLA_H) for c in range(2)])
    parts["wo"] = _columns(i["mla_w_o"][0])
    for l in range(2):
        up, down = _columns(i["mlp_w_up"][l]), _rows(i["mlp_w_down"][l])
        order = [up[0]]
        for f in range(FC - 1):
            order += [up[f + 1], down[f]]
        parts[f"mlp{l}"] = np.stack(order + [down[-1]])
    q = i["swa_w_q"][0].reshape(D, SWA_H, SWA_D)[:, SWA_ORDER].reshape(D, D)
    parts["swaq"] = _columns(q)
    parts["swak"] = _columns(i["kv_w_shared"][:, :256])
    parts["swav"] = _rows(i["kv_w_shared"][:, 256:])
    parts["swao"] = _columns(i["swa_w_o"][0].reshape(SWA_H, SWA_D, D)[SWA_ORDER].reshape(D, D))
    w = i["w_in_2"][0]
    cols = [w[:, 512:1024], w[:, 0:512], w[:, 1024:1792]]
    parts["rwkv"] = _columns(np.concatenate(cols, 1))
    parts["sbqk"] = _columns(w[:, 1792:2816])
    parts["sbv"] = _rows(w[:, 2816:3328])
    parts["memq"] = _columns(w[:, 3328:3840])
    parts["gate"] = _columns(w[:, 3840:])
    br = i["w_branch_2"][0]
    parts["branch"] = _packed([br[n, k * P:(k + 1) * P, c * P:(c + 1) * P] for n in range(3) for c in range(DC) for k in range(4)])
    parts["out"] = _columns(i["w_out_2"][0])
    up, down = _columns(i["w_up_2"][0]), _rows(i["w_down_2"][0])
    order = [up[0], up[FC2]]
    for f in range(FC2 - 1):
        order += [up[f + 1], up[FC2 + f + 1], down[f]]
    parts["ffn"] = np.stack(order + [down[-1]])
    for name, n in STREAM:
        assert parts[name].shape[0] == n, name
    return np.ascontiguousarray(np.concatenate([parts[name] for name, _ in STREAM]))


def _params(i):
    mu = i["shift_mu_2"][0]
    mu = np.concatenate([mu[512:1024], mu[0:512], mu[1024:]])
    conv = i["conv_w_2"][0]
    rows = {"g_q": i["mla_g_q"], "g_kv": i["mla_g_kv"], "ln_mix_g": i["ln_mix_g"], "ln_mix_b": i["ln_mix_b"],
            "ln_mlp_g": i["ln_mlp_g"], "ln_mlp_b": i["ln_mlp_b"], "norm1": i["norm1_g_2"], "mu": mu,
            "w0": i["decay_w0_2"], "a0": i["iclr_a0_2"], "k_k": i["k_k_2"], "k_a": i["k_a_2"], "r_k": i["r_k_2"],
            "lnx_g": i["lnx_g_2"], "lnx_b": i["lnx_b_2"], "sbq_g": np.tile(i["sb_q_norm_g_2"], (1, 2)),
            "sbk_g": np.tile(i["sb_k_norm_g_2"], (1, 2)), "mem_g": i["mem_norm_g_2"], "memq_g": i["mem_q_norm_g_2"],
            "memk_g": i["mem_k_norm_g_2"], "norm2": i["norm2_g_2"], "conv0": conv[0], "conv1": conv[1],
            "conv2": conv[2], "conv_b": i["conv_b_2"]}
    cols = [rows[name].reshape(-1, P).T if name in rows else np.tile(i["swa_sinks"][0], (P, 1)) for name, _ in PARAMS]
    return np.ascontiguousarray(np.concatenate(cols, 1))


def kernel(**inputs):
    import concourse.bacc as bacc
    from concourse.bass_utils import run_bass_kernel_spmd

    i = {name: np.asarray(a) for name, a in inputs.items()}

    def feature_major(a):
        return np.ascontiguousarray(a.reshape(T, DC, P).transpose(2, 1, 0))

    table, band = constants()
    arrays = {
        "weights": _stream(i),
        "x_t": feature_major(i["x"][0]),
        "mem_t": feature_major(i["mem_2"][0]).reshape(P, DC * T),
        "table": table,
        "band_rows": band,
        "params": _params(i),
        "lora_w": np.ascontiguousarray(np.concatenate([i["decay_w2_2"][0], i["iclr_a2_2"][0]], 0)),
        "gate_w": np.ascontiguousarray(i["gate_g2_2"][0]),
        "rel_bias_w": np.ascontiguousarray(i["rel_bias"]),
    }
    nc = bacc.Bacc("TRN2", target_bir_lowering=False, num_devices=1)
    args = [nc.dram_tensor(name, a.shape, F32, kind="ExternalInput").ap() for name, a in arrays.items()]
    out = nc.dram_tensor("out_t", (P, DC, T), F32, kind="ExternalOutput").ap()
    build(nc, *args, out)
    result = run_bass_kernel_spmd(nc, [arrays], core_ids=[0]).results[0]["out_t"]
    return np.ascontiguousarray(np.asarray(result).transpose(2, 1, 0).reshape(1, T, D))
```

```python
import math
from contextlib import ExitStack, contextmanager

import numpy as np
import concourse.bass as bass
from concourse import mybir

F32 = mybir.dt.float32
F32R = mybir.dt.float32r
BF16 = mybir.dt.bfloat16
ACT = mybir.ActivationFunctionType
ALU = mybir.AluOpType
AX = mybir.AxisListType

P = 128
T = 256
D = 1024
DC = D // P
NEG = -1.0e30

MLA_H, Q_RANK, KV_RANK, NOPE, ROPE, VD = 8, 384, 256, 128, 64, 128
SWA_H, SWA_KV, SWA_D = 16, 4, 64
DFF = 4096
FC = DFF // P
RW_W, RW_H, RW_D = 512, 8, 64
DFF2 = 2816
FC2 = DFF2 // P
LN_EPS, RMS_EPS, LNX_EPS = 1e-5, 1e-6, 64e-5
ALPHA = (2 * 2) ** 0.25
RING = 4
AHEAD = 3

STREAM = [("in", 7), ("memk", 4), ("q", 6), ("uk", 2), ("uv", 2), ("wo", 8), ("memva", 2), ("mlp0", 2 * FC), ("memvb", 2),
          ("swaq", 8), ("swak", 2), ("swav", 2), ("swao", 8), ("mlp1", 2 * FC), ("rwkv", 14), ("sbqk", 8),
          ("sbv", 4), ("memq", 4), ("gate", 24), ("branch", 12), ("out", 8), ("ffn", 3 * FC2)]
SLOT = {}
NSLOT = 0
for _name, _n in STREAM:
    SLOT[_name] = NSLOT
    NSLOT += _n

PARAMS = [("g_q", 3), ("g_kv", 2), ("ln_mix_g", 16), ("ln_mix_b", 16), ("ln_mlp_g", 16), ("ln_mlp_b", 16),
          ("norm1", 8), ("mu", 14), ("w0", 4), ("a0", 4), ("k_k", 4), ("k_a", 4), ("r_k", 4), ("lnx_g", 4),
          ("lnx_b", 4), ("sbq_g", 1), ("sbk_g", 1), ("mem_g", 8), ("memq_g", 1), ("memk_g", 1), ("norm2", 8),
          ("conv0", 44), ("conv1", 44), ("conv2", 44), ("conv_b", 44), ("sinks", 16)]
PCOL = {}
NPAR = 0
for _name, _n in PARAMS:
    PCOL[_name] = NPAR
    NPAR += _n

CONSTS = [("ident", 128), ("ones", 1), ("causal", 384), ("cos", 256), ("sin", 256), ("blockones", 128), ("later", 128),
          ("before", 128), ("upto", 128), ("level", 7 * 128), ("level0t", 128)]
CCOL = {}
NCON = 0
for _name, _n in CONSTS:
    CCOL[_name] = NCON
    NCON += _n


def constants():
    i = np.arange(P)
    row, col = i[:, None], i[None, :]
    c = {"ident": np.eye(P), "ones": np.ones((P, 1)), "blockones": (row // 64 == col // 64)}
    c["later"] = row > col
    future = np.where(col > row, NEG, 0.0)
    c["causal"] = np.concatenate([future, np.zeros((P, P)), future], 1)
    half = ROPE // 2
    inv = np.float32(10000.0) ** (-np.arange(half, dtype=np.float32) / np.float32(half))
    ang = (np.arange(T, dtype=np.float32)[None, :] * inv[:, None]).astype(np.float32)
    c["cos"] = np.tile(np.cos(ang), (4, 1))
    c["sin"] = np.tile(np.concatenate([-np.sin(ang), np.sin(ang)], 0), (2, 1))
    c["before"] = row < col
    c["upto"] = row <= col
    levels = []
    for l in range(7):
        b = 1 << l
        levels.append((row // (2 * b) == col // (2 * b)) & (row // b % 2 == 0) & (col // b % 2 == 1))
    c["level"] = np.concatenate(levels, 1)
    c["level0t"] = levels[0].T
    dist = np.arange(384) - 127
    ok = (dist >= 0) & (dist < 128)
    n = np.maximum(dist, 0)
    nf = np.maximum(n, 1).astype(np.float32)
    large = 16 + (np.log(nf / np.float32(16)) / np.float32(math.log(8)) * np.float32(16)).astype(np.int32)
    bucket = np.where(n < 16, n, np.minimum(large, 31))
    onehot = np.zeros((P, 384))
    onehot[:32] = (bucket[None, :] == np.arange(32)[:, None]) & ok[None, :]
    out = np.zeros((P, NCON), np.float32)
    for name, n_ in CONSTS:
        out[:, CCOL[name]:CCOL[name] + n_] = c[name]
    band = np.zeros((32, 2, 384), np.float32)
    band[:, 0] = onehot[:32]
    band[:, 1] = np.where(ok, 0.0, NEG)[None, :]
    return out, band


class Tally:

    def __init__(self, engine, sem):
        self.engine, self.sem, self.n, self.i, self.per = engine, sem, 0, None, 0

    def value(self, n):
        return n if self.i is None else self.i * self.per + n

    def link(self, ins):
        ins.then_inc(self.sem, 1)
        self.n += 1
        self.engine.wait_ge(self.sem, self.value(self.n))

    def enter(self, i, per):
        self.i, self.per, self.at = i, per, self.n

    def leave(self, times):
        assert self.n - self.at == self.per, (self.n - self.at, self.per)
        self.n = self.at + self.per * times
        self.i = None



def pipeline(steps):
    kinds, heads = steps
    return [(kind, t - lag) for t in range(heads + kinds[-1][1] + 1) for kind, lag in kinds
            if 0 <= t - lag < heads]


MLA_STEPS = ([("s", 0), ("t", 2), ("o", 3), ("u", 4)], MLA_H)
SWA_STEPS = ([("s", 0), ("t", 3), ("o", 4)], SWA_H)
MEM_STEPS = ([("s", 0), ("t", 2), ("o", 3)], 4)

MATS = [(m, g) for g in range(2) for m in ("at", "a0")] + [(m, g) for m in ("kk", "rb", "rk") for g in range(2)]

RESULTS = []
KAPPA = math.exp(-0.5)
SWA_ORDER = [h for a in (0, 8) for c in range(4) for h in (a + c, a + 4 + c)]


def _results(stage, names):
    RESULTS.extend((stage, n) for n in names)


_results("brow", [0])
_results("in", range(4))
_results("memstat", [0])
_results("in", range(4, 7))
_results("mlastat", [0])
_results("memk", range(4))
_results("ckvt", [0])
_results("q", range(16))
_results("qlat", range(8))
_results("mla", pipeline(MLA_STEPS))
_results("wo", range(8))
_results("ln0", [0])
_results("memva", range(2))
_results("ln0", [1, 2])
_results("mlp0", range(FC))
_results("memvb", range(2))
_results("ln1", range(3))
_results("swaq", range(8))
_results("swak", range(2))
_results("swav", range(2))
_results("swa", [k for k in pipeline(SWA_STEPS) if k[0] != "o"])
_results("swao", range(8))
_results("ln2", range(3))
_results("mlp1", range(FC))
_results("ln3", range(3))
_results("rms1", range(2))
_results("rwkv", range(14))
_results("loraw", range(2))
_results("loraa", range(2))
_results("vtok", range(2))
_results("kkstat", [0])
_results("bonus", range(2))
_results("kkspread", range(2))
_results("btok", range(2))
_results("sbqstat", [0])
for _tc in range(2):
    _results(f"mat{_tc}", MATS)
    for _l in range(1, 7):
        _results(f"inv{_tc}", [(_l, "h", g) for g in range(2)])
        if (_tc, _l) == (1, 1):
            _results("sbstat", [0])
        _results(f"inv{_tc}", [(_l, m, g) for g in range(2) for m in (("d", "dt") if _l < 6 else ("dt",))])
        if (_tc, _l) == (1, 3):
            _results("sbspread", range(2))
    if _tc == 0:
        _results("end0", ["rhs0", "rhs1", "sa", "y", "state"])
    else:
        _results("end1", ["rhs0", "rhs1"])
        _results("memstat2", [0])
        _results("end1", ["sa"])
        _results("lorag", range(2))
        _results("end1", ["y"])
_results("sbz", range(4))
_results("ystat", [0])
_results("sbz", range(4, 8))
_results("memspread", range(2))
_results("yspread", range(4))
_results("sbo", [("b", 0), ("b", 1)] + [(k, h) for h in range(2, 10) for k in ("b", "o")
                                        if (k == "b" and h < 8) or (k == "o" and h % 2)])
_results("mem", pipeline(MEM_STEPS))
_results("branch", range(24))
_results("out", range(8))
_results("rms2", range(2))
_results("ffn", range(2 * FC2))
RESULT = {key: n for n, key in enumerate(RESULTS)}
assert len(RESULT) == len(RESULTS)

SIDE = {key: n for n, key in enumerate([("sbqk", j) for j in range(8)] + [("sbv", t) for t in range(2)] +
                                       [("memq", j) for j in range(4)] + [("gate", j) for j in range(24)])}
FILLED_GATES = 16
SIDE_SLOTS = [(stage, j) for stage, n in (("sbqk", 8), ("sbv", 4), ("memq", 4), ("gate", FILLED_GATES)) for j in range(n)]
GATE_ORDER = list(range(4, 24)) + list(range(4))
SB_FILLS = {("b", 1): 19, ("o", 3): 20, ("o", 5): 21, ("o", 7): 22}
MEM_FILLS = {("s", 1): [23, 24], ("t", 0): [25], ("o", 0): [26], ("o", 1): [27, 28], ("o", 2): [29, 30], ("o", 3): [31]}
MEM_TURNS = {1: [23, 24], 2: [25], 3: [26], 4: [27, 28], 5: [29, 30], 6: [31]}


def build(nc, w, xt, memt, consts_in, band_in, params_in, lora_in, gate2_in, relb_in, out):
    ctx = ExitStack()
    with ctx:
        def tensor(stack, name, shape, dt=F32):
            return stack.enter_context(nc.sbuf_tensor(name, shape, dt))

        def flat(ap):
            return ap[:, :, :].rearrange("p a t -> p (a t)")

        raw = tensor(ctx, "raw", [P, RING, 1024])
        whi = tensor(ctx, "whi", [P, RING, 1024], F32R)
        wlo = tensor(ctx, "wlo", [P, RING, 1024], F32R)
        con = tensor(ctx, "con", [P, NCON])
        par = tensor(ctx, "par", [P, NPAR])
        lora = tensor(ctx, "lora", [P, 512])
        gate2 = tensor(ctx, "gate2", [P, 512])
        relb = tensor(ctx, "relb", [32, 16])
        zeros = tensor(ctx, "zeros", [P, P], BF16)
        x = tensor(ctx, "x", [P, DC, T])
        xh = tensor(ctx, "xh", [P, DC, T], F32R)
        xl = tensor(ctx, "xl", [P, DC, T], F32R)
        res = tensor(ctx, "res", [P, DC, T])
        sqr = tensor(ctx, "sqr", [P, DC, T])
        stat = tensor(ctx, "stat", [P, 4, T])
        km = tensor(ctx, "km", [P, 4, T])
        vm = tensor(ctx, "vm", [P, 2, 512])
        sc = tensor(ctx, "sc", [P, 2, 512])
        pr = tensor(ctx, "pr", [P, 2, 512])
        pT = tensor(ctx, "pT", [P, 4, 512])
        sm = tensor(ctx, "sm", [P, 4, 8])
        hh = tensor(ctx, "hh", [P, 2, T], F32R)
        hl = tensor(ctx, "hl", [P, 2, T], F32R)
        ha = tensor(ctx, "ha", [P, 2, T])
        hb = tensor(ctx, "hb", [P, 2, T])
        hst = stat[:, 3, 0:P].rearrange("p (a b) -> p a b", b=32)
        with ExitStack() as first:
            oh = tensor(first, "oh", [P, 8, T], F32R)
            ol = tensor(first, "ol", [P, 8, T], F32R)
            with ExitStack() as inner:
                memh = tensor(inner, "memh", [P, DC, T], F32R)
                meml = tensor(inner, "meml", [P, DC, T], F32R)
            bias = tensor(first, "bias", [P, 16, T])
            cqh = tensor(first, "cqh", [P, 3, T], F32R)
            cql = tensor(first, "cql", [P, 3, T], F32R)
            ckv = tensor(first, "ckv", [P, 2, T])
            ckvt = tensor(first, "ckvt", [P, 2, T])
            kr = tensor(first, "kr", [P, T])
            qr = tensor(first, "qr", [P, 4, T])
            nsink = tensor(first, "nsink", [P, 16])
            qlat = tensor(first, "qlat", [P, 8, 2 * T])
            qnh, qnl = oh, ol
            olh, oll = flat(hh), flat(hl)
            qs = qlat[:, 0:4, :].rearrange("p a (b t) -> p (a b) t", t=T)
            ks = qlat[:, 4, :].rearrange("p (b t) -> p b t", t=T)
            vs = qlat[:, 5, :].rearrange("p (b t) -> p b t", t=T)
            bandt = qlat[0:32, 6:8, 0:384]
            brow = qlat[0:16, 5, 0:384]
            hraw = sqr[:, 0:5, :]
        with ExitStack() as second:
            with ExitStack() as inner:
                tensor(inner, "free_yh", [P, 4, T])
                sbk = tensor(inner, "sbk", [P, 4, T])
                memq = tensor(inner, "memq", [P, 4, T])
                tensor(inner, "free_yl", [P, 4, T])
                sbq = tensor(inner, "sbq", [P, 4, T])
                vsb = tensor(inner, "vsb", [P, 2, 512])
            yh = tensor(second, "yh", [P, 12, T], F32R)
            yl = tensor(second, "yl", [P, 12, T], F32R)
            with ExitStack() as inner:
                with ExitStack() as innermost:
                    cum = tensor(innermost, "cum", [P, 8, 129])
                rb = tensor(inner, "rb", [P, 2, 512])
                rk = tensor(inner, "rk", [P, 2, 512])
                vtok = tensor(inner, "vtok", [P, 2, 512])
                btok = tensor(inner, "btok", [P, 2, 512])
                aa = tensor(inner, "aa", [P, 4, T])
                k_ = tensor(inner, "k_", [P, 4, T])
                r_ = tensor(inner, "r_", [P, 4, T])
                dlora = tensor(inner, "dlora", [P, T])
                tensor(inner, "free_gates", [P, 2, T])
                glora = tensor(inner, "glora", [P, T])
                v_ = tensor(inner, "v_", [P, 4, T])
                kk = tensor(inner, "kk", [P, 4, T])
                bon = tensor(inner, "bon", [P, 4, T])
                gg = kk
                yy = v_
                rhs, sa = flat(ha), flat(hb)
                st = stat[:, 0, :].rearrange("p (c i) -> p c i", c=4)
                mid = stat[:, 1, 0:24].rearrange("p (a c) -> p a c", a=3)
                fac = stat[:, 2, 0:4]
                pb = sc[:, :, 0:T + 1]
                em = pr[:, :, :].rearrange("p a (b t) -> p (a b) t", t=128)
                ep = pT[:, :, :].rearrange("p a b -> p (a b)")[:, 0:8 * 129].rearrange("p (a b) -> p a b", b=129)
            with ExitStack() as inner:
                z8 = tensor(inner, "z8", [P, 8, 384])
                with ExitStack() as innermost:
                    e8 = tensor(innermost, "e8", [P, 8, 384])
                tensor(inner, "before_gates", [P, 8, T])
                gates = tensor(inner, "gates", [P, 24, T])
            with ExitStack() as inner:
                cg = tensor(inner, "cg", [P, 2, T + 2])
                cv = tensor(inner, "cv", [P, 2, T + 2])
                fa = tensor(inner, "fa", [P, 2, T])
                fb = tensor(inner, "fb", [P, 2, T])
                fs = tensor(inner, "fs", [P, 2, T])
        acc = [ctx.enter_context(nc.psum_tensor(f"acc{b}", [P, 512], F32)) for b in range(4)]
        work = [ctx.enter_context(nc.psum_tensor(f"work{b}", [P, 512], F32)) for b in range(4)]
        scratch = nc.dram_tensor("bias_scratch", [16, 384], F32, kind="Internal").ap()

        def spc(h):
            at_, h_ = (sqr, h) if h < 5 else (res, h - 5)
            return flat(at_)[:, h_ * 384:(h_ + 1) * 384]

        mst = hb[:, 0, :]
        at = res[:, 0:4, :].rearrange("p (g a) t -> p g (a t)", g=2)
        kkm = res[:, 4:8, :].rearrange("p (g a) t -> p g (a t)", g=2)
        tinv = sqr[:, 0:4, :].rearrange("p (g a) t -> p g (a t)", g=2)
        uinv = sqr[:, 4:8, :].rearrange("p (g a) t -> p g (a t)", g=2)

        def memc(c):
            return qlat[:, c // 2, c % 2 * T:c % 2 * T + T]

        def mem2(c):
            return qlat[:, c, :].rearrange("p (a t) -> p a t", a=2)

        def hsq(j):
            return pT[:, j // 2, j % 2 * T:j % 2 * T + T]

        memraw = qlat[:, 0:4, :]

        def score_buffer(stage, h):
            return (sc, pr)[h % 2][:, h // 2 % 2] if stage == "swa" else sc[:, h % 2]

        def probability_buffer(stage, h):
            return score_buffer(stage, h) if stage == "swa" else pr[:, h % 2]

        def softmax_set(stage, h):
            return h % 4 if stage == "swa" else h % 2

        def projected(j):
            return (k_, r_, v_)[j // 4][:, j % 4, :] if j < 12 else (dlora, glora)[j - 12][:, :]

        def side_sq(j):
            if j < 4:
                return res[:, j, :]
            return pT[:, (j - 4) // 2, (j - 4) % 2 * T:(j - 4) % 2 * T + T]

        def C(name, width=P, col=0):
            return con[:, CCOL[name] + col:CCOL[name] + col + width]

        ones = C("ones", 1).broadcast_to([P, P])

        def G(name, col=0):
            return par[:, PCOL[name] + col:PCOL[name] + col + 1]

        def half(t):
            return slice(t * P, (t + 1) * P)

        def four(ap):
            return ap.rearrange("p (a b) -> p a b", b=P)

        def half_columns(ap, level, second):
            b = 1 << level
            return ap.rearrange("p (n a b) -> p n a b", a=2, b=b)[:, :, int(second), :]

        def mask4(ap):
            return ap.rearrange("p (a b) -> p a b", a=1).broadcast_to([P, 4, P])

        def odd_on_dve(c):
            return c in (0, 3)

        def sem(name):
            return ctx.enter_context(nc.semaphore(name))

        filled = [sem(f"filled{b}") for b in range(4)]
        drained = [sem(f"drained{b}") for b in range(4)]
        raw_loaded = [sem(f"raw_loaded{r}") for r in range(RING)]
        side_filled = [sem(f"side_filled{b}") for b in range(4)]
        side_drained = [sem(f"side_drained{b}") for b in range(4)]
        cut_hi = sem("cut_hi")
        cut_lo = sem("cut_lo")
        slots_used = sem("slots_used")
        named = {}

        def sig(name):
            if name not in named:
                named[name] = sem(name)
            return named[name]

        def wait_filled(eng, key, it=None, per=0):
            n = RESULT[key]
            eng.wait_ge(filled[n % 4], n // 4 + 1 if it is None else it * (per // 4) + (n // 4 + 1))
            return work[n % 4]

        def wait_drained(eng, key, it=None, per=0):
            n = RESULT[key]
            eng.wait_ge(drained[n % 4], n // 4 + 1 if it is None else it * (per // 4) + (n // 4 + 1))

        def drain(ins, key):
            ins.then_inc(drained[RESULT[key] % 4], 1)

        def wait_side_filled(eng, key, it=None):
            n = SIDE[key]
            eng.wait_ge(side_filled[n % 4], n // 4 + 1 if it is None else it + (n // 4 + 1))
            return acc[n % 4]

        def wait_side_drained(eng, key):
            n = SIDE[key]
            eng.wait_ge(side_drained[n % 4], n // 4 + 1)

        def side_drain(ins, key):
            ins.then_inc(side_drained[SIDE[key] % 4], 1)

        block = ctx.enter_context(nc.Block())

        @block.sync
        def _(sp):
            for n in range(RING):
                sp.dma_start(raw[:, n, :], w[n]).then_inc(raw_loaded[n], 16)
            rounds = NSLOT // RING
            with sp.Fori(1, rounds) as i:
                for r in range(RING):
                    sp.wait_ge(cut_lo, i * RING + (r + 1 - RING))
                    sp.dma_start(raw[:, r, :], w[bass.ds(i * RING + r, 1), :, :].rearrange("a p n -> p (a n)"))\
                        .then_inc(raw_loaded[r], 16)
            for n in range(rounds * RING, NSLOT):
                sp.wait_ge(cut_lo, n + 1 - RING)
                sp.dma_start(raw[:, n % RING, :], w[n]).then_inc(raw_loaded[n % RING], 16)
            for b in range(4):
                sp.wait_ge(sig("final"), b + 1)
                sp.dma_start(out[:, 2 * b:2 * b + 2, :], res[:, 2 * b:2 * b + 2, :]).then_inc(sig("stored"), 16)
            sp.wait_ge(sig("stored"), 64)

        @block.gpsimd
        def _(pool):
            nc.gpsimd.memset(zeros[:, :], 0.0).then_inc(sig("zeros_set"), 1)
            pool.dma_start(relb[:, :], relb_in).then_inc(sig("band_loaded"), 16)
            pool.dma_start(bandt, band_in).then_inc(sig("band_loaded"), 16)
            wait_drained(pool, ("brow", 0))
            pool.dma_start(scratch, brow).then_inc(sig("brow_stored"), 16)
            pool.wait_ge(sig("brow_stored"), 16)
            pool.dma_start(lora[:, :], lora_in).then_inc(sig("lora_loaded"), 16)
            pool.dma_start(gate2[:, :], gate2_in).then_inc(sig("lora_loaded"), 16)
            pool.wait_ge(sig("qr_ready"), 4)
            pool.dma_start(con[:, CCOL["blockones"]:], consts_in[:, CCOL["blockones"]:]).then_inc(sig("con2_loaded"), 16)
            wait_drained(pool, ("memvb", 0))
            wait_drained(pool, ("memvb", 1))
            pool.dma_start(bias[:, :, :], bass.AP(scratch.tensor, 0, [[1, P], [384, 16], [1, T]]))\
                .then_inc(sig("bias_loaded"), 16)
            pool.wait_ge(sig("rinv"), 5)
            nc.gpsimd.memset(pb[:, :, 0:1], 0.0).then_inc(sig("pb_zero"), 1)
            nc.gpsimd.memset(cum[:, :, 0:1], 0.0).then_inc(sig("pb_zero"), 1)
            wait_drained(pool, ("mem", ("o", 3)))
            nc.gpsimd.memset(cg[:, :, 0:2], 0.0).then_inc(sig("cg_zero"), 1)
            nc.gpsimd.memset(cv[:, :, 0:2], 0.0).then_inc(sig("cg_zero"), 1)

        @block.tensor
        def _(pe):
            mm = nc.tensor.matmul

            def slot_start(n, it=None, per=0):
                pe.wait_ge(cut_lo, n + 1 if it is None else it * per + (n + 1))

            def open_result(key, it=None, per=0):
                n = RESULT[key]
                if n >= 4:
                    pe.wait_ge(drained[n % 4], n // 4 if it is None else it * (per // 4) + (n // 4))
                return work[n % 4]

            def close_result(ins, key):
                ins.then_inc(filled[RESULT[key] % 4], 1)

            def cut_product(dst, n, tile, hi, lo, start, stop, first=False, shared=False):
                col = slice(tile * P, tile * P + P)
                a = mm(dst, whi[:, n % RING, col], hi, start=start, stop=False, skip_group_check=shared)
                if first and n > 0:
                    a.then_inc(slots_used, 1)
                mm(dst, whi[:, n % RING, col], lo, start=False, stop=False, skip_group_check=shared)
                return mm(dst, wlo[:, n % RING, col], hi, start=False, stop=stop, skip_group_check=shared)

            def chunk(stage, j, key, hi, lo, waits=None):
                n = SLOT[stage] + j
                bank = open_result(key)
                slot_start(n)
                for k in range(DC):
                    if waits is not None:
                        waits(k)
                    last = cut_product(bank[:, 0:T], n, k, hi[:, k, :], lo[:, k, :], k == 0, k == DC - 1, k == 0)
                close_result(last, key)

            def chunk_pair(stage, keys, hi, lo, waits):
                n = SLOT[stage]
                banks = [open_result(key) for key in keys]
                slot_start(n + 1)
                for k in range(DC):
                    waits(k)
                    for j in range(2):
                        last = cut_product(banks[j][:, 0:T], n + j, k, hi[:, k, :], lo[:, k, :], k == 0, k == DC - 1, k == j * (DC - 1))
                        if k == DC - 1:
                            close_result(last, keys[j])

            def token_major(stage, slots, width, hi, lo, between=None):
                rows = 1024 // width
                banks = [open_result((stage, t)) for t in range(2)]
                for j in range(slots):
                    n = SLOT[stage] + j
                    slot_start(n)
                    for r in range(rows):
                        k = j * rows + r
                        col = slice(r * width, (r + 1) * width)
                        for t in range(2):
                            dst = banks[t][:, 0:width]
                            a = mm(dst, hi[:, k, half(t)], whi[:, n % RING, col], start=k == 0, stop=False)
                            if r == 0 and t == 0:
                                a.then_inc(slots_used, 1)
                            mm(dst, hi[:, k, half(t)], wlo[:, n % RING, col], start=False, stop=False)
                            last = mm(dst, lo[:, k, half(t)], whi[:, n % RING, col], start=False, stop=k == DC - 1)
                            if k == DC - 1:
                                close_result(last, (stage, t))
                    if between is not None:
                        between(j)

            def sums(keys, srcs, weights, chunks, waits):
                banks = [open_result(k) for k in keys]
                for c in range(chunks):
                    for a, (bank, src) in enumerate(zip(banks, srcs)):
                        waits(c, a)
                        last = mm(bank[:, 0:T], weights, src[:, c, :], start=c == 0, stop=c == chunks - 1)
                        if c == chunks - 1:
                            close_result(last, keys[a])

            def token_sums(bank, n, products, src, heads):
                width = 512 // products
                one = (C("blockones")[:, 0:P:64] if heads == 2 else C("ones", 1)).rearrange("p (h o) -> p h o", o=1)
                for t in range(2):
                    dst = bank[:, (n + 4 * t) * width:(n + 4 * t + 1) * width].rearrange("p (h o) -> p h o", h=heads)
                    last = mm(dst, src[:, half(t)], one.broadcast_to([P, heads, width // heads]), start=True, stop=True)
                return last

            def spread(bank, src, heads):
                width = P // heads
                for c in range(2):
                    for t in range(2):
                        for h in range(heads):
                            values = src(c, t)[:, h:h + 1].broadcast_to([P, width])
                            dst = bank[h * width:(h + 1) * width, c * T + t * P:c * T + (t + 1) * P]
                            last = mm(dst, values, C("ident"), start=True, stop=True)
                return last

            def side_open(key, it=None):
                n = SIDE[key]
                if n >= 4:
                    pe.wait_ge(side_drained[n % 4], n // 4 if it is None else it + n // 4)
                return acc[n % 4]

            def fill(i):
                stage, j = SIDE_SLOTS[i]
                n = SLOT[stage] + j
                if stage != "sbv":
                    bank = side_open((stage, j))
                    slot_start(n)
                    for k in range(DC):
                        last = cut_product(bank[:, 0:T], n, k, xh[:, k, :], xl[:, k, :], k == 0, k == DC - 1, k == 0)
                    last.then_inc(side_filled[SIDE[(stage, j)] % 4], 1)
                    return
                banks = [side_open((stage, t)) if j == 0 else acc[SIDE[(stage, t)] % 4] for t in range(2)]
                slot_start(n)
                for r in range(2):
                    k, col = 2 * j + r, slice(r * 512, r * 512 + 512)
                    for t in range(2):
                        a = mm(banks[t][:, :], xh[:, k, half(t)], whi[:, n % RING, col], start=k == 0, stop=False)
                        if r == 0 and t == 0:
                            a.then_inc(slots_used, 1)
                        mm(banks[t][:, :], xh[:, k, half(t)], wlo[:, n % RING, col], start=False, stop=False)
                        last = mm(banks[t][:, :], xl[:, k, half(t)], whi[:, n % RING, col], start=False, stop=k == DC - 1)
                        if k == DC - 1:
                            last.then_inc(side_filled[SIDE[(stage, t)] % 4], 1)

            pe.wait_ge(sig("band_loaded"), 32)
            close_result(mm(open_result(("brow", 0))[0:16, 0:384], relb[:, :], bandt[:, 0, :], start=True, stop=True), ("brow", 0))
            for j in range(4):
                chunk("in", j, ("in", j), xh, xl, (lambda k: pe.wait_ge(sig("x_cut"), k // 2 + 1)) if j == 0 else None)
            pe.wait_ge(sig("con_loaded"), 16)
            sums([("memstat", 0)], [res], ones, DC, lambda c, a: pe.wait_ge(sig("mem_sq"), 1))
            for j in range(4, 7):
                chunk("in", j, ("in", j), xh, xl)
            bank = open_result(("mlastat", 0))
            pe.wait_ge(sig("in_sq"), 5)
            for j in range(5):
                dst = bank[:, 0:T] if j < 3 else bank[:, T:2 * T]
                last = mm(dst, ones, hsq(j), start=j in (0, 3), stop=j in (2, 4))
            close_result(last, ("mlastat", 0))
            for j in range(4):
                chunk("memk", j, ("memk", j), memh, meml, (lambda k: pe.wait_ge(sig("mem_cut"), k // 2 + 1)) if j == 0 else None)
            bank = open_result(("ckvt", 0))
            pe.wait_ge(sig("ckv_ready"), 2)
            for t in range(2):
                for c in range(2):
                    last = nc.tensor.transpose(bank[:, t * T + c * P:t * T + c * P + P], ckv[:, c, half(t)], C("ident"))
            close_result(last, ("ckvt", 0))
            pe.wait_ge(sig("cq_cut"), 1)
            for j in range(16):
                bank = open_result(("q", j))
                for k in range(3):
                    s, tile = divmod(3 * j + k, 8)
                    if tile == 0:
                        slot_start(SLOT["q"] + s)
                    last = cut_product(bank[:, 0:T], SLOT["q"] + s, tile, cqh[:, k, :], cql[:, k, :], k == 0, k == 2, tile == 0)
                close_result(last, ("q", j))
            for h in range(MLA_H):
                bank = open_result(("qlat", h))
                wait_drained(pe, ("q", h))
                for c in range(2):
                    s, tile = divmod(2 * h + c, 8)
                    if tile == 0:
                        slot_start(SLOT["uk"] + s)
                    last = cut_product(bank[:, c * T:(c + 1) * T], SLOT["uk"] + s, tile, qnh[:, h, :], qnl[:, h, :], True, True, tile == 0)
                close_result(last, ("qlat", h))

            def transposes(stage, h, blocks):
                bank = open_result((stage, ("t", h)))
                pe.wait_ge(sig(f"{stage}_norm"), h + 1)
                for a, b in blocks:
                    last = nc.tensor.transpose(bank[:, b * P:b * P + P], probability_buffer(stage, h)[:, a * P:a * P + P], C("ident"))
                close_result(last, (stage, ("t", h)))

            pe.wait_ge(sig("kr_ready"), 1)
            pe.wait_ge(sig("qr_ready"), 4)
            wait_drained(pe, ("ckvt", 0))
            for kind, h in pipeline(MLA_STEPS):
                key = ("mla", (kind, h))
                if kind == "s":
                    bank = open_result(key)
                    wait_drained(pe, ("qlat", h))
                    off = slice(64 * (h % 2), 64 * (h % 2) + 64)
                    for dst, q, keys in ((bank[:, 0:P], 0, P), (bank[:, P:3 * P], P, T)):
                        for c in range(2):
                            mm(dst, qlat[:, h, c * T + q:c * T + q + P], ckv[:, c, 0:keys], start=c == 0, stop=False)
                        last = mm(dst, qr[off, h // 2, q:q + P], kr[off, 0:keys], start=False, stop=True)
                    close_result(last, key)
                elif kind == "t":
                    transposes("mla", h, [(0, 0), (1, 1), (2, 2)])
                elif kind == "o":
                    bank = open_result(key)
                    wait_drained(pe, ("mla", ("t", h)))
                    for c in range(2):
                        mm(bank[:, c * T:(c + 1) * T], ckvt[:, 0, half(c)], pT[:, h % 4, 0:T], start=True, stop=False)
                        last = mm(bank[:, c * T + P:(c + 1) * T], ckvt[:, 1, half(c)], pT[:, h % 4, T:3 * P], start=False, stop=True)
                    close_result(last, key)
                else:
                    bank = open_result(key)
                    wait_drained(pe, ("mla", ("o", h)))
                    for c in range(2):
                        s, tile = divmod(2 * h + c, 8)
                        if tile == 0:
                            slot_start(SLOT["uv"] + s)
                        last = cut_product(bank[:, 0:T], SLOT["uv"] + s, tile, olh[:, c * T:(c + 1) * T],
                                           oll[:, c * T:(c + 1) * T], c == 0, c == 1, tile == 0)
                    close_result(last, key)
            for j in range(DC):
                chunk("wo", j, ("wo", j), oh, ol, (lambda k: wait_drained(pe, ("mla", ("u", k)))) if j == 0 else None)

            norms = [0, 0]

            def norm_sums(name, pieces):
                bank = open_result((name, 0))
                mm(bank[:, :], zeros[:, :], mask4(zeros[:, :]), start=True, stop=False, skip_group_check=True)
                for n, (src, squares, wait) in enumerate(pieces):
                    wait()
                    for t in range(2):
                        col = (2 * squares + t) * P
                        last = mm(bank[:, col:col + P], src[:, half(t)], ones, start=False,
                                  stop=n == len(pieces) - 1, skip_group_check=True)
                close_result(last, (name, 0))

            def added_sums(name, which):
                norms[1] += 1
                norm_sums(name, [(ha[:, a, :], a if len(which) == 2 else 0, lambda: pe.wait_ge(sig("added"), norms[1])) for a in which])

            def column_spread(key, col):
                bank = open_result(key)
                for t in range(2):
                    last = mm(bank[:, half(t)], stat[:, 0, col + t:col + t + 1].broadcast_to([P, P]), C("ident"), start=True, stop=True)
                close_result(last, key)

            def mean_spread(name):
                wait_drained(pe, (name, 0))
                column_spread((name, 1), 0)

            def rstd_spread(name, centred=True):
                norms[0] += 1
                pe.wait_ge(sig("rstd"), norms[0])
                column_spread((name, 2 if centred else 1), 8)

            def sums_after_mlp(name):
                norms[1] += 1
                norm_sums(name, [(res[:, c, :], 0, lambda c=c: pe.wait_ge(sig(f"{name}_sum"), c // 2 + 1)) for c in range(DC)] +
                          [(ha[:, a, :], 1, lambda: pe.wait_ge(sig("added"), norms[1])) for a in range(2)])

            def mlp(stage, normed):
                base = SLOT[stage]
                for b in range(4):
                    mm(acc[b][:, :], zeros[:, :], mask4(zeros[:, :]), start=True, stop=False, skip_group_check=True)
                chunk_pair(stage, [(stage, 0), (stage, 1)], xh, xl, lambda k: pe.wait_ge(sig("x_normed"), normed + k // 2 + 1))

                def step(f, it=None):
                    key = (stage, f + 1)
                    bank = open_result(key, it, 4)
                    n = base + 2 * f + 1
                    slot_start(n, it, 8)
                    for k in range(DC):
                        last = cut_product(bank[:, 0:T], n, k, xh[:, k, :], xl[:, k, :], k == 0, k == DC - 1, k == 0)
                    close_result(last, key)
                    down(f, n + 1, it)

                def down(f, n, it=None):
                    slot_start(n, it, 8)
                    wait_drained(pe, (stage, f), it, 4)
                    for c in range(DC):
                        last = cut_product(acc[c // 2][:, (c % 2) * T:(c % 2 + 1) * T], n, c, hh[:, f % 2, :], hl[:, f % 2, :],
                                           False, c == DC - 1, c == 0, True)
                        if f == FC - 1 and c % 2:
                            last.then_inc(sig("acc_full"), 1)

                down(0, base + 2)
                rounds = (FC - 2) // 4
                with pe.Fori(0, rounds) as it:
                    for f in range(1, 5):
                        step(f, it)
                for f in range(4 * rounds + 1, FC - 1):
                    step(f)
                down(FC - 1, base + 2 * FC - 1)

            pe.wait_ge(sig("zeros_set"), 1)
            added_sums("ln0", (0, 1))
            def spread_between(j):
                if j == 0:
                    mean_spread("ln0")
                    rstd_spread("ln0")
            token_major("memva", 2, T, memh, meml, spread_between)
            mlp("mlp0", 0)
            token_major("memvb", 2, T, memh, meml, lambda j: sums_after_mlp("ln1") if j == 0 else None)
            mean_spread("ln1")
            rstd_spread("ln1")

            chunk_pair("swaq", [("swaq", 0), ("swaq", 1)], xh, xl, lambda k: pe.wait_ge(sig("x_normed"), 4 + k // 2 + 1))
            for j in range(2, 8):
                chunk("swaq", j, ("swaq", j), xh, xl)
            for j in range(2):
                chunk("swak", j, ("swak", j), xh, xl)
            token_major("swav", 2, T, xh, xl)
            for kind, h in pipeline(SWA_STEPS):
                key = ("swa", (kind, h))
                chunk_, off = h // 2, slice(64 * (h % 2), 64 * (h % 2) + 64)
                if kind == "s":
                    bank = open_result(key)
                    wait_drained(pe, ("swaq", chunk_))
                    wait_drained(pe, ("swak", chunk_ // 4))
                    for dst, q, keys in ((bank[:, 0:P], 0, P), (bank[:, P:3 * P], P, T)):
                        last = mm(dst, qs[off, chunk_, q:q + P], ks[off, chunk_ // 4, 0:keys], start=True, stop=True)
                    close_result(last, key)
                elif kind == "t":
                    transposes("swa", h, [(0, 0), (1, 1), (2, 2)])
                else:
                    bank = acc[h // 2 % 4]
                    if h >= 8 and h % 2 == 0:
                        pe.wait_ge(sig("swa_cut"), h // 2 - 3)
                    for t in range(2):
                        wait_drained(pe, ("swav", t))
                    wait_drained(pe, ("swa", ("t", h)))
                    o = slice(64 * (h % 2), 64 * (h % 2) + 64)
                    kv = 2 * (h // 8) + h % 2
                    mm(bank[o, 0:T], vs[:, 0, kv * 64:kv * 64 + 64], pT[:, h % 4, 0:T], start=True, stop=False)
                    last = mm(bank[o, P:T], vs[:, 1, kv * 64:kv * 64 + 64], pT[:, h % 4, T:3 * P], start=False, stop=True)
                    if h % 2:
                        last.then_inc(sig("swa_out"), 1)
            for j in range(DC):
                chunk("swao", j, ("swao", j), oh, ol, (lambda k: pe.wait_ge(sig("swa_cut"), k + 1)) if j == 0 else None)
            added_sums("ln2", (0, 1))
            mean_spread("ln2")
            rstd_spread("ln2")
            mlp("mlp1", 8)
            sums_after_mlp("ln3")
            mean_spread("ln3")
            rstd_spread("ln3")

            norm_sums("rms1", [(sqr[:, c, :], 0, lambda c=c: pe.wait_ge(sig("squared"), 32 + c + 1)) for c in range(DC)])
            rstd_spread("rms1", False)
            chunk_pair("rwkv", [("rwkv", 0), ("rwkv", 1)], xh, xl, lambda k: pe.wait_ge(sig("x_normed"), 12 + k // 2 + 1))
            for j in range(2, 14):
                chunk("rwkv", j, ("rwkv", j), xh, xl)
            fill(0)
            pe.wait_ge(sig("lora_loaded"), 32)
            pe.wait_ge(sig("lora_act"), 2)
            wait_drained(pe, ("rwkv", 12))

            def lora_out(name, weights, src):
                for j in range(2):
                    bank = open_result((name, j))
                    for c in range(2):
                        last = mm(bank[:, c * T:(c + 1) * T], weights[:, (2 * j + c) * P:(2 * j + c + 1) * P], src, start=True, stop=True)
                    close_result(last, (name, j))

            lora_out("loraw", lora[0:64, :], dlora[0:64, :])
            lora_out("loraa", lora[64:P, :], dlora[64:P, :])
            for t in range(2):
                bank = open_result(("vtok", t))
                for c in range(4):
                    last = nc.tensor.transpose(bank[:, c * P:c * P + P], v_[:, c, half(t)], C("ident"))
                close_result(last, ("vtok", t))
            pe.wait_ge(sig("con2_loaded"), 16)
            bank = open_result(("kkstat", 0))
            pe.wait_ge(sig("kk_sq"), 1)
            for c in range(4):
                last = token_sums(bank, c, 8, sqr[:, c, :], 2)
            close_result(last, ("kkstat", 0))
            fill(1)
            pe.wait_ge(sig("rk_prod"), 1)
            for j in range(2):
                key = ("bonus", j)
                close_result(mm(open_result(key)[:, :], C("blockones"), flat(sqr[:, 4 + 2 * j:6 + 2 * j, :]), start=True, stop=True), key)
            pe.wait_ge(sig("kk_rstd"), 1)
            for j in range(2):
                close_result(spread(open_result(("kkspread", j)), lambda c, t: hst[:, 2, t * 8 + 4 * j + 2 * c:t * 8 + 4 * j + 2 * c + 2], 2), ("kkspread", j))
            fill(2)
            fill(3)
            pe.wait_ge(sig("factors"), 1)
            for j, src in enumerate((aa, k_)):
                bank = open_result(("btok", j))
                for c in range(4):
                    last = nc.tensor.transpose(bank[:, c * P:c * P + P], src[:, c, 0:P], C("ident"))
                close_result(last, ("btok", j))
            bank = open_result(("sbqstat", 0))
            pe.wait_ge(sig("side_squares"), 4)
            for c in range(4):
                last = token_sums(bank, c, 8, side_sq(c), 2)
            close_result(last, ("sbqstat", 0))

            def blk(j):
                return slice(j * P, j * P + P)

            levels = 0
            for tc in range(2):
                pe.wait_ge(sig("factors"), tc + 1)
                mats = {"at": (aa, kk), "a0": (kk, aa), "kk": (k_, kk), "rb": (aa, r_), "rk": (k_, r_)}
                for m, g in MATS:
                    left, right = mats[m]
                    key = (f"mat{tc}", (m, g))
                    bank = open_result(key)
                    for j in range(4):
                        off = slice(64 * g, 64 * g + 64)
                        last = mm(bank[:, blk(j)], left[off, j, half(tc)], right[off, j, half(tc)], start=True, stop=True)
                    close_result(last, key)
                for l in range(1, 7):
                    for g in range(2):
                        key = (f"inv{tc}", (l, "h", g))
                        bank = open_result(key)
                        pe.wait_ge(sig("inv_mask"), levels + g + 1)
                        if l > 1:
                            wait_drained(pe, (f"inv{tc}", (l - 1, "dt", g)))
                        for j in range(4):
                            last = mm(bank[:, blk(j)], sc[:, g, blk(j)], tinv[:, g, blk(j)], start=True, stop=True)
                        close_result(last, key)
                    levels += 2
                    if tc == 0:
                        fill(3 + l)
                    elif l < 6:
                        fill(10 + l)
                    if (tc, l) == (1, 1):
                        bank = open_result(("sbstat", 0))
                        pe.wait_ge(sig("side_squares"), 8)
                        for c in range(4):
                            last = token_sums(bank, c, 8, side_sq(4 + c), 2)
                        close_result(last, ("sbstat", 0))
                    for g in range(2):
                        wait_drained(pe, (f"inv{tc}", (l, "h", g)))
                        for m in ("d", "dt")[l == 6:]:
                            key = (f"inv{tc}", (l, m, g))
                            bank = open_result(key)
                            for j in range(4):
                                left, right = (uinv, pr) if m == "d" else (pr, uinv)
                                last = mm(bank[:, blk(j)], left[:, g, blk(j)], right[:, g, blk(j)], start=True, stop=True)
                            close_result(last, key)
                    if (tc, l) == (1, 3):
                        pe.wait_ge(sig("sb_rstd"), 1)
                        for j in range(2):
                            key = ("sbspread", j)
                            close_result(spread(open_result(key), lambda c, t: hst[:, 0, t * 8 + 4 * j + 2 * c:t * 8 + 4 * j + 2 * c + 2], 2), key)
                banks = [open_result((f"end{tc}", f"rhs{g}")) for g in range(2)]
                pe.wait_ge(sig("mats_masked"), 3 * (tc + 1))
                if tc == 0:
                    wait_drained(pe, ("vtok", 1))
                else:
                    wait_drained(pe, ("end0", "state"))
                for h in range(8):
                    c, off, col = h // 2, slice(64 * (h % 2), 64 * (h % 2) + 64), slice(h * 64, h * 64 + 64)
                    dst = banks[h % 2][:, c * 64:c * 64 + 64]
                    last = mm(dst, kkm[:, h % 2, blk(c)], vtok[:, tc, col], start=True, stop=tc == 0)
                    if tc:
                        last = mm(dst, kk[off, c, half(1)], st[off, c, :], start=False, stop=True)
                    if h >= 6:
                        close_result(last, (f"end{tc}", f"rhs{h % 2}"))
                if tc == 0:
                    fill(10)
                else:
                    bank = open_result(("memstat2", 0))
                    pe.wait_ge(sig("side_squares"), 16)
                    for c in range(8):
                        last = token_sums(bank, c // 4 * 8 + c % 4, 16, side_sq(8 + c if c < 4 else c), 1)
                    close_result(last, ("memstat2", 0))
                key = (f"end{tc}", "sa")
                bank = open_result(key)
                for g in range(2):
                    wait_drained(pe, (f"end{tc}", f"rhs{g}"))
                for g in range(2):
                    wait_drained(pe, (f"inv{tc}", (6, "dt", g)))
                for h in range(8):
                    src = rhs[:, h % 2 * T + h // 2 * 64:h % 2 * T + h // 2 * 64 + 64]
                    last = mm(bank[:, h * 64:h * 64 + 64], uinv[:, h % 2, blk(h // 2)], src, start=True, stop=True)
                close_result(last, key)
                if tc:
                    lora_out("lorag", gate2[:, :], glora[:, :])
                key = (f"end{tc}", "y")
                bank = open_result(key)
                wait_drained(pe, (f"end{tc}", "sa"))
                for h in range(8):
                    c, off, col = h // 2, slice(64 * (h % 2), 64 * (h % 2) + 64), slice(h * 64, h * 64 + 64)
                    dst = bank[off, blk(c)]
                    mm(dst, vtok[:, tc, col], rk[:, h % 2, blk(c)], start=True, stop=False)
                    last = mm(dst, sa[:, col], rb[:, h % 2, blk(c)], start=False, stop=tc == 0)
                    if tc:
                        last = mm(dst, st[off, c, :], r_[off, c, half(1)], start=False, stop=True)
                close_result(last, key)
                if tc == 0:
                    key = ("end0", "state")
                    bank = open_result(key)
                    for j in range(2):
                        wait_drained(pe, ("btok", j))
                    for h in range(8):
                        c, off, col = h // 2, slice(64 * (h % 2), 64 * (h % 2) + 64), slice(h * 64, h * 64 + 64)
                        dst = bank[off, c * 64:c * 64 + 64]
                        mm(dst, btok[:, 0, col], sa[:, col], start=True, stop=False)
                        last = mm(dst, btok[:, 1, col], vtok[:, 0, col], start=False, stop=True)
                    close_result(last, key)

            def sbz(h):
                key = ("sbz", h)
                bank = open_result(key)
                c, off = h // 2, slice(64 * (h % 2), 64 * (h % 2) + 64)
                mm(bank[:, 0:T], sbk[off, c, 0:P], sbq[off, c, :], start=True, stop=True)
                last = mm(bank[:, T:3 * P], sbk[off, c, P:T], sbq[off, c, P:T], start=True, stop=True)
                close_result(last, key)

            for j in range(2):
                wait_drained(pe, ("sbspread", j))
            for h in range(4):
                sbz(h)
            bank = open_result(("ystat", 0))
            pe.wait_ge(sig("y_sq"), 1)
            for a, src in enumerate((yy, sqr)):
                for c in range(4):
                    last = token_sums(bank, 8 * a + c, 16, src[:, c, :], 2)
            close_result(last, ("ystat", 0))
            fill(16)
            for h in range(4, 8):
                sbz(h)
            fill(17)
            pe.wait_ge(sig("mem_norm_rstd"), 1)
            for j in range(2):
                key = ("memspread", j)
                close_result(spread(open_result(key), lambda c, t: hst[:, 1, 8 + 4 * t + 2 * j + c:8 + 4 * t + 2 * j + c + 1], 1), key)
            for j in range(2):
                key = ("yspread", j)
                close_result(mm(open_result(key)[:, :], C("blockones"), flat(yy[:, 2 * j:2 * j + 2, :]), start=True, stop=True), key)
            pe.wait_ge(sig("y_rstd"), 1)
            for j in range(2):
                key, first = ("yspread", 2 + j), 16 + 4 * j
                close_result(spread(open_result(key), lambda c, t: hst[:, 3, first + 8 * t + 2 * c:first + 8 * t + 2 * c + 2], 2), key)
            fill(18)
            for kind, h in [k[1] for k in RESULTS if k[0] == "sbo"]:
                key = ("sbo", (kind, h))
                bank = open_result(key)
                if kind == "b":
                    pe.wait_ge(sig("softplus"), h + 1)
                    mm(bank[:, 0:T], C("later"), spc(h)[:, 0:T], start=True, stop=False)
                    mm(bank[:, P:T], ones, spc(h)[:, T:3 * P], start=False, stop=True)
                    last = mm(bank[:, T:3 * P], C("later"), spc(h)[:, T:3 * P], start=True, stop=True)
                else:
                    for t in range(2):
                        wait_side_drained(pe, ("sbv", t))
                    pe.wait_ge(sig("sb_attn"), h - 1)
                    for g in (h - 3, h - 2):
                        o = slice(64 * (g % 2), 64 * (g % 2) + 64)
                        mm(bank[o, 0:T], vsb[:, 0, g * 64:g * 64 + 64], z8[:, g, 0:T], start=True, stop=False)
                        last = mm(bank[o, P:T], vsb[:, 1, g * 64:g * 64 + 64], z8[:, g, T:3 * P], start=False, stop=True)
                close_result(last, key)
                if (kind, h) in SB_FILLS:
                    fill(SB_FILLS[(kind, h)])

            for j in range(2):
                wait_drained(pe, ("memspread", j))
            for kind, h in pipeline(MEM_STEPS):
                key = ("mem", (kind, h))
                if kind == "s":
                    bank = open_result(key)
                    for t in range(2):
                        last = mm(bank[:, t * T:(t + 1) * T], memq[:, h, half(t)], km[:, h, :], start=True, stop=True)
                    close_result(last, key)
                elif kind == "t":
                    transposes("mem", h, [(0, 0), (1, 2), (2, 1), (3, 3)])
                else:
                    bank = open_result(key)
                    wait_drained(pe, ("mem", ("t", h)))
                    for t in range(2):
                        wait_drained(pe, ("memva", t))
                        wait_drained(pe, ("memvb", t))
                    for t in range(2):
                        last = mm(bank[:, 0:T], vm[:, t, h * P:h * P + P], pT[:, h % 4, t * T:(t + 1) * T], start=t == 0, stop=t == 1)
                    close_result(last, key)
                for i in MEM_FILLS.get((kind, h), []):
                    fill(i)

            def gate(j):
                bank = side_open(("gate", j))
                n = SLOT["gate"] + j
                slot_start(n)
                for k in range(DC):
                    last = cut_product(bank[:, 0:T], n, k, xh[:, k, :], xl[:, k, :], k == 0, k == DC - 1, k == 0)
                last.then_inc(side_filled[SIDE[("gate", j)] % 4], 1)

            for j in range(FILLED_GATES, 24):
                gate(j)
            for c in range(4):
                wait_drained(pe, ("mem", ("o", c)))
            pe.wait_ge(sig("y_cut"), 1)
            for r in range(24):
                bank = open_result(("branch", r))
                n = SLOT["branch"] + r // 2
                if r % 2 == 0:
                    slot_start(n)
                for k in range(4):
                    tile, part = 4 * (r % 2) + k, r // 8 * 4 + k
                    last = cut_product(bank[:, 0:T], n, tile, yh[:, part, :], yl[:, part, :], k == 0, k == 3, tile == 0)
                close_result(last, ("branch", r))
            chunk_pair("out", [("out", 0), ("out", 1)], xh, xl, lambda k: pe.wait_ge(sig("x_normed"), 16 + k // 2 + 1))
            for j in range(2, DC):
                chunk("out", j, ("out", j), xh, xl)
            added_sums("rms2", (1,))
            rstd_spread("rms2", False)

            base = SLOT["ffn"]
            for b in range(4):
                mm(acc[b][:, :], zeros[:, :], mask4(zeros[:, :]), start=True, stop=False, skip_group_check=True)
            chunk_pair("ffn", [("ffn", 0), ("ffn", 1)], xh, xl, lambda k: pe.wait_ge(sig("x_normed"), 20 + k // 2 + 1))

            def ffn_down(f, n, it=None):
                slot_start(n, it, 12)
                wait_drained(pe, ("ffn", 2 * f + 1), it, 8)
                for c in range(DC):
                    last = cut_product(acc[c // 2][:, (c % 2) * T:(c % 2 + 1) * T], n, c, hh[:, f % 2, :], hl[:, f % 2, :],
                                       False, c == DC - 1, c == 0, True)
                    if f == FC2 - 1 and c % 2:
                        last.then_inc(sig("acc_full"), 1)

            def ffn_step(f, it=None):
                for j in range(2):
                    key = ("ffn", 2 * f + 2 + j)
                    bank = open_result(key, it, 8)
                    n = base + 3 * f + 2 + j
                    slot_start(n, it, 12)
                    for k in range(DC):
                        last = cut_product(bank[:, 0:T], n, k, xh[:, k, :], xl[:, k, :], k == 0, k == DC - 1, k == 0)
                    close_result(last, key)
                ffn_down(f, base + 3 * f + 4, it)

            rounds = (FC2 - 1) // 4
            with pe.Fori(0, rounds) as it:
                for f in range(4):
                    ffn_step(f, it)
            for f in range(4 * rounds, FC2 - 1):
                ffn_step(f)
            ffn_down(FC2 - 1, base + 3 * FC2 - 1)
        @block.scalar
        def _(act):
            own = Tally(act, sig("act_step"))
            act_fn = nc.scalar.activation
            count = {"norm": 0, "x_ready": 0, "scaled": 0, "made": 0, "odd": 0}

            def cut(n, it=None, per=0):
                if n >= NSLOT:
                    return
                loaded, used = 16 * (n // RING + 1), n - RING + 1
                act.wait_ge(raw_loaded[n % RING], loaded if it is None else it * (16 * per // RING) + loaded)
                if n >= RING:
                    act.wait_ge(slots_used, used if it is None else it * per + used)
                act_fn(whi[:, n % RING, :], raw[:, n % RING, :], ACT.Copy).then_inc(cut_hi, 1)

            def cuts(stage, s, it=None, per=0):
                cut(SLOT[stage] + s + AHEAD, it, per)

            def fill_cut(i):
                cuts("sbqk", i)

            def fill_evac(i):
                stage, j = SIDE_SLOTS[i]
                if stage == "sbv":
                    if j == 3:
                        for t in range(2):
                            bank = wait_side_filled(act, ("sbv", t))
                            side_drain(act_fn(vsb[:, t, :], bank[:, :], ACT.Copy), ("sbv", t))
                    return
                key = (stage, j)
                bank = wait_side_filled(act, key)[:, 0:T]
                if stage == "sbqk":
                    act_fn(side_sq(j), bank, ACT.Square).then_inc(sig("side_squares"), 1)
                    if j < 4:
                        side_drain(act_fn(sbq[:, j, :], bank, ACT.Copy), key)
                    else:
                        side_drain(act_fn(sbk[:, j - 4, :], bank, ACT.Identity, scale=G("sbk_g")), key)
                elif stage == "memq":
                    act_fn(side_sq(8 + j), bank, ACT.Square).then_inc(sig("side_squares"), 1)
                    side_drain(act_fn(memq[:, j, :], bank, ACT.Identity, scale=G("memq_g")), key)
                else:
                    if j >= 8:
                        act.wait_ge(sig("y_cut"), 1)
                    side_drain(act_fn(gates[:, GATE_ORDER[j], :], bank, ACT.Copy), key)

            act.dma_start(x[:, 0:2, :], xt[:, 0:2, :]).then_inc(sig("x_loaded"), 16)
            act.dma_start(x[:, 2:DC, :], xt[:, 2:DC, :]).then_inc(sig("x_rest_loaded"), 16)
            first_con = CCOL["blockones"]
            act.dma_start(con[:, 0:first_con], consts_in[:, 0:first_con]).then_inc(sig("con_loaded"), 16)
            act.dma_start(par[:, :], params_in).then_inc(sig("par_loaded"), 16)
            act.dma_start(flat(memraw), memt).then_inc(sig("mem_loaded"), 16)

            def root():
                count["norm"] += 1
                own.link(act_fn(stat[:, 0, 12:13], par[:, 0:1], ACT.Sqrt, scale=0.0))
                act.wait_ge(sig("rinv"), count["norm"])
                act_fn(stat[:, 0, 8:10], stat[:, 0, 6:8], ACT.Sqrt).then_inc(sig("rstd"), 1)

            def square_chunk(stage, src, j):
                wait_drained(act, (stage, j))
                act_fn(sqr[:, j, :], src[:, j, :], ACT.Square).then_inc(sig("squared"), 1)

            def square_pair(src, c):
                pair = slice(2 * c, 2 * c + 2)
                act_fn(sqr[:, pair, :], src[:, pair, :], ACT.Square).then_inc(sig("squared"), 2)

            def scale_shift(name, g, b, col, cut_after=True, halfway=None):
                for c in range(4):
                    if c < 3:
                        count["scaled"] += 1
                        act.wait_ge(sig("scaled"), count["scaled"])
                    else:
                        wait_drained(act, (name, 2))
                    for d in (2 * c,) if odd_on_dve(c) else (2 * c, 2 * c + 1):
                        last = act_fn(x[:, d, :], res[:, d, :], ACT.Identity, scale=G(g, col + d), bias=G(b, col + d))
                    last.then_inc(sig("x_made"), 1)
                    count["made"] += 1
                    act.wait_ge(sig("x_made"), count["made"])
                    if odd_on_dve(c):
                        count["odd"] += 1
                        act.wait_ge(sig("x_odd"), count["odd"])
                    if cut_after:
                        act_fn(xh[:, 2 * c:2 * c + 2, :], x[:, 2 * c:2 * c + 2, :], ACT.Copy).then_inc(sig("x_hi"), 1)
                        if c == 2 and halfway:
                            halfway()
                    else:
                        square_pair(x, c)

            def square_sums(name):
                for c in range(4):
                    act.wait_ge(sig(f"{name}_sum"), c + 1)
                    square_pair(res, c)

            def cut_x(src, hooks=None, merged=False):
                for c in range(4):
                    if merged:
                        act.wait_ge(sig("merged"), 8 + 2 * c + 2)
                    else:
                        count["x_ready"] += 1
                        act.wait_ge(sig("x_ready"), count["x_ready"])
                    act_fn(xh[:, 2 * c:2 * c + 2, :], src[:, 2 * c:2 * c + 2, :], ACT.Copy).then_inc(sig("x_hi"), 1)
                    if hooks:
                        hooks(c)

            for c in range(4):
                act.wait_ge(sig("x_rest_loaded" if c else "x_loaded"), 16)
                pair = slice(2 * c, 2 * c + 2)
                act_fn(xh[:, pair, :], x[:, pair, :], ACT.Copy).then_inc(sig("x0_hi"), 1)
                if c == 0:
                    cut(0)
            for n in range(1, AHEAD):
                cut(n)
            for j in range(7):
                cuts("in", j)
                if j < 5:
                    bank = wait_filled(act, ("in", j))
                    act_fn(hsq(j), bank[:, 0:T], ACT.Square).then_inc(sig("in_sq"), 1)
                if j == 1:
                    act.wait_ge(sig("mem_loaded"), 16)
                    act_fn(flat(res), flat(memraw), ACT.Square).then_inc(sig("mem_sq"), 1)
                if j == 4:
                    act.wait_ge(sig("mem_inv"), 1)
                    act_fn(mst[:, :], mst[:, :], ACT.Sqrt).then_inc(sig("mem_rstd"), 1)
                for c in {5: (0, 1), 6: (2, 3)}.get(j, ()):
                    act.wait_ge(sig("mem_ready"), c + 1)
                    act_fn(memh[:, 2 * c:2 * c + 2, :], mem2(c), ACT.Copy).then_inc(sig("mem_hi"), 1)
            cuts("memk", 0)
            act.wait_ge(sig("mla_inv"), 1)
            act_fn(stat[:, 2:4, :], stat[:, 0:2, :], ACT.Sqrt).then_inc(sig("mla_rstd"), 1)
            act.wait_ge(sig("cq_ready"), 1)
            act_fn(flat(cqh), flat(hraw[:, 0:3, :]), ACT.Copy).then_inc(sig("cq_hi"), 1)
            for j in range(4):
                if j:
                    cuts("memk", j)
                bank = wait_filled(act, ("memk", j))
                drain(act_fn(km[:, j, :], bank[:, 0:T], ACT.Copy), ("memk", j))
            bank = wait_filled(act, ("ckvt", 0))
            drain(act_fn(flat(ckvt), bank[:, :], ACT.Copy), ("ckvt", 0))
            for j in range(16):
                for s in range(6):
                    if 3 * j <= 8 * s < 3 * j + 3:
                        cuts("q", s)
                if j < 8:
                    bank = wait_filled(act, ("q", j))
                    act_fn(qnh[:, j, :], bank[:, 0:T], ACT.Copy).then_inc(sig("qn_hi"), 1)
            act.wait_ge(sig("brow_stored"), 16)
            for h in range(8):
                if h % 4 == 0:
                    cuts("uk", h // 4)
                if h % 2 == 0:
                    bank = wait_filled(act, ("qlat", h))
                    drain(act_fn(qlat[:, h, :], bank[:, :], ACT.Copy), ("qlat", h))

            def probabilities(stage, h, parts, sink=None):
                p = softmax_set(stage, h)
                src, dst = score_buffer(stage, h), probability_buffer(stage, h)
                act.wait_ge(sig(f"{stage}_max"), h + 1)
                for b, cols in enumerate(parts):
                    last = act_fn(dst[:, cols], src[:, cols], ACT.Exp, bias=sm[:, p, b:b + 1], accum_out=sm[:, p, 2 + b:3 + b])
                    if sink is not None:
                        own.link(last)
                if sink is not None:
                    last = act_fn(sm[:, p, 4:6], sm[:, p, 0:2], ACT.Exp, bias=sink)
                last.then_inc(sig(f"{stage}_exp"), 1)

            def key_major(stage, h, width):
                bank = wait_filled(act, (stage, ("t", h)))
                drain(act_fn(pT[:, h % 4, 0:width], bank[:, 0:width], ACT.Copy), (stage, ("t", h)))

            three = (slice(0, P), slice(P, 3 * P))
            for t in range(MLA_H + 4):
                if 0 <= t - 2 < MLA_H:
                    key_major("mla", t - 2, 384)
                if 0 <= t - 4:
                    bank = wait_filled(act, ("mla", ("u", t - 4)))
                    act_fn(oh[:, t - 4, :], bank[:, 0:T], ACT.Copy).then_inc(sig("oh_hi"), 1)
                if 0 <= t - 3 < MLA_H:
                    bank = wait_filled(act, ("mla", ("o", t - 3)))
                    act_fn(olh[:, :], bank[:, :], ACT.Copy).then_inc(sig("ol_hi"), 1)
                if t < MLA_H:
                    probabilities("mla", t, three)
                if t >= 4 and t % 4 == 0:
                    cuts("uv", (t - 4) // 4)
            for j in range(DC):
                if j < DC - 1:
                    cuts("wo", j)
                if j:
                    square_chunk("wo", res, j - 1)
            square_chunk("wo", res, DC - 1)
            cuts("wo", DC - 1)
            def memory_values(stage, first):
                for t in range(2):
                    bank = wait_filled(act, (stage, t))
                    drain(act_fn(vm[:, t, first:first + T], bank[:, 0:T], ACT.Copy), (stage, t))

            root()
            cuts("memva", 0)
            scale_shift("ln0", "ln_mix_g", "ln_mix_b", 0, halfway=lambda: memory_values("memva", 0))
            cuts("memva", 1)

            def mlp(stage, units_before):
                def hidden(f, it=None):
                    bank = wait_filled(act, (stage, f), it, 4)
                    act_fn(ha[:, f % 2, :], bank[:, 0:T], ACT.Relu).then_inc(sig("relu"), 1)
                    done = units_before + f + 1
                    act.wait_ge(sig("relu"), done if it is None else it * 4 + done)
                    act_fn(hh[:, f % 2, :], ha[:, f % 2, :], ACT.Square).then_inc(sig("h_hi"), 1)

                cuts(stage, 0)
                hidden(0)

                def step(f, it=None):
                    cuts(stage, 2 * f + 1, it, 8)
                    hidden(f + 1, it)
                    cuts(stage, 2 * f + 2, it, 8)

                rounds = (FC - 1) // 4
                with act.Fori(0, rounds) as it:
                    for f in range(4):
                        step(f, it)
                for f in range(4 * rounds, FC - 1):
                    step(f)
                cuts(stage, 2 * FC - 1)

            mlp("mlp0", 0)
            square_sums("ln1")
            root()
            cuts("memvb", 0)
            memory_values("memvb", T)
            scale_shift("ln1", "ln_mlp_g", "ln_mlp_b", 0)
            cuts("memvb", 1)
            for j in range(8):
                cuts("swaq", j)
                bank = wait_filled(act, ("swaq", j))
                drain(act_fn(qs[:, j, :], bank[:, 0:T], ACT.Copy), ("swaq", j))
            for j in range(2):
                cuts("swak", j)
                bank = wait_filled(act, ("swak", j))
                drain(act_fn(ks[:, j, :], bank[:, 0:T], ACT.Copy), ("swak", j))
            for j in range(2):
                cuts("swav", j)
            for t in range(2):
                bank = wait_filled(act, ("swav", t))
                drain(act_fn(vs[:, t, :], bank[:, 0:T], ACT.Copy), ("swav", t))
            for t in range(SWA_H + 5):
                if 0 <= t - 5 and (t - 5) % 2:
                    pair = (t - 5) // 2
                    act.wait_ge(sig("swa_out"), pair + 1)
                    act_fn(oh[:, pair, :], acc[pair % 4][:, 0:T], ACT.Copy).then_inc(sig("oh_hi"), 1)
                if 0 <= t - 3 < SWA_H:
                    key_major("swa", t - 3, 384)
                if t < SWA_H:
                    probabilities("swa", t, three, par[:, PCOL["sinks"] + SWA_ORDER[t]:PCOL["sinks"] + SWA_ORDER[t] + 1])
                if 0 <= t - 1 < SWA_H:
                    p, ap = softmax_set("swa", t - 1), probability_buffer("swa", t - 1)
                    act.wait_ge(sig("swa_inverse"), t)
                    for b, cols in enumerate(three):
                        last = act_fn(ap[:, cols], ap[:, cols], ACT.Copy, scale=sm[:, p, 6 + b:7 + b])
                    last.then_inc(sig("swa_norm"), 1)
            for j in range(DC):
                if j < DC - 1:
                    cuts("swao", j)
                if j:
                    square_chunk("swao", res, j - 1)
            square_chunk("swao", res, DC - 1)
            cuts("swao", DC - 1)
            root()
            scale_shift("ln2", "ln_mix_g", "ln_mix_b", 8)
            mlp("mlp1", FC)
            square_sums("ln3")
            root()
            scale_shift("ln3", "ln_mlp_g", "ln_mlp_b", 8, False)

            root()
            cut_x(res)
            for j in range(14):
                cuts("rwkv", j)
                bank = wait_filled(act, ("rwkv", j))
                if j == 0:
                    act.wait_ge(sig("pb_zero"), 2)
                if j >= 2:
                    wait_drained(act, ("rwkv", j - 2))
                act_fn(pb[:, j % 2, 1:T + 1], bank[:, 0:T], ACT.Copy).then_inc(sig("pb_full"), 1)
            wait_drained(act, ("rwkv", 12))
            act_fn(dlora[0:64, :], dlora[0:64, :], ACT.Tanh).then_inc(sig("lora_act"), 1)
            wait_drained(act, ("rwkv", 13))
            act_fn(glora[:, :], glora[:, :], ACT.Sigmoid).then_inc(sig("lora_act"), 1)
            fill_cut(0)
            fill_evac(0)
            for name, col in (("loraw", "w0"), ("loraa", "a0")):
                for j in range(2):
                    bank = wait_filled(act, (name, j))
                    for c in range(2):
                        src, chunk_ = bank[:, c * T:(c + 1) * T], 2 * j + c
                        if name == "loraw":
                            last = act_fn(em[:, 2 * chunk_:2 * chunk_ + 2, :], src.rearrange("p (a t) -> p a t", a=2), ACT.Sigmoid, bias=G(col, chunk_))
                        else:
                            last = act_fn(aa[:, chunk_, :], src, ACT.Sigmoid, bias=G(col, chunk_))
                    drain(last, (name, j))
            act.wait_ge(sig("kk_raw"), 1)
            act_fn(sqr[:, 0:4, :], kk[:, :, :], ACT.Square).then_inc(sig("kk_sq"), 1)
            act.wait_ge(sig("cum_ready"), 1)
            for c in range(8):
                last = act_fn(ep[:, c, :], cum[:, c, :], ACT.Exp, scale=-KAPPA, bias=mid[:, 0, c:c + 1])
            for c in range(8):
                last = act_fn(em[:, c, :], cum[:, c, 1:129], ACT.Exp, scale=KAPPA, bias=mid[:, 1, c:c + 1])
            last.then_inc(sig("exps"), 1)
            act.wait_ge(sig("fac_ready"), 1)
            act_fn(fac[:, :], fac[:, :], ACT.Exp, scale=-KAPPA).then_inc(sig("fac_exp"), 1)
            act.wait_ge(sig("kk_inv"), 1)
            act_fn(hst[:, 2, 0:16], hst[:, 2, 0:16], ACT.Sqrt).then_inc(sig("kk_rstd"), 1)
            for t in range(2):
                bank = wait_filled(act, ("vtok", t))
                drain(act_fn(vtok[:, t, :], bank[:, :], ACT.Copy), ("vtok", t))
            fill_cut(1)
            fill_evac(1)
            for i in (2, 3):
                fill_cut(i)
                fill_evac(i)
            for t in range(2):
                bank = wait_filled(act, ("btok", t))
                drain(act_fn(btok[:, t, :], bank[:, :], ACT.Copy), ("btok", t))
            for tc in range(2):
                for m, g in MATS[4:]:
                    key = (f"mat{tc}", (m, g))
                    bank = wait_filled(act, key)
                    drain(act_fn({"kk": kkm, "rb": rb, "rk": rk}[m][:, g, :], bank[:, :], ACT.Copy), key)
                for l in range(1, 7):
                    for g in range(2):
                        key = (f"inv{tc}", (l, "h", g))
                        bank = wait_filled(act, key)
                        drain(act_fn(pr[:, g, :], bank[:, :], ACT.Copy), key)
                    if (tc, l) == (1, 2):
                        act.wait_ge(sig("sb_inv"), 1)
                        act_fn(hst[:, 0, :], hst[:, 0, :], ACT.Sqrt).then_inc(sig("sb_rstd"), 1)
                    if tc == 0 or l < 6:
                        i = 3 + l if tc == 0 else 10 + l
                        fill_cut(i)
                        fill_evac(i)
                    if (tc, l) == (1, 3):
                        wait_filled(act, ("sbstat", 0))
                        act_fn(pT[:, 0:2, :].rearrange("p a (b t) -> p (a b) t", b=2), km[:, :, :], ACT.Square).then_inc(sig("side_squares"), 4)
                if tc == 0:
                    fill_cut(10)
                bank = wait_filled(act, (f"end{tc}", "sa"))
                drain(act_fn(sa[:, :], bank[:, :], ACT.Copy), (f"end{tc}", "sa"))
                if tc == 0:
                    fill_evac(10)
            for j in range(2):
                bank = wait_filled(act, ("lorag", j))
                drain(act_fn(flat(gg[:, 2 * j:2 * j + 2, :]), bank[:, :], ACT.Copy), ("lorag", j))
            act.wait_ge(sig("mem_inv2"), 1)
            act_fn(hst[:, 1, 0:16], hst[:, 1, 0:16], ACT.Sqrt).then_inc(sig("mem_norm_rstd"), 1)
            wait_drained(act, ("end1", "y"))
            act_fn(sqr[:, 0:4, :], yy[:, :, :], ACT.Square).then_inc(sig("y_sq"), 1)

            def sbz(h):
                bank = wait_filled(act, ("sbz", h))
                act_fn(z8[:, h, 0:T], bank[:, 0:T], ACT.Copy, scale=hst[:, 0, 16 + h:17 + h])
                drain(act_fn(z8[:, h, T:3 * P], bank[:, T:3 * P], ACT.Copy, scale=hst[:, 0, 24 + h:25 + h]), ("sbz", h))

            for h in range(4):
                sbz(h)
            act.wait_ge(sig("y_inv"), 1)
            act_fn(hst[:, 3, 16:32], hst[:, 3, 16:32], ACT.Sqrt).then_inc(sig("y_rstd"), 1)
            fill_cut(16)
            for h in range(8):
                if h < 4:
                    sbz(4 + h)
                act.wait_ge(sig("sb_abs"), h + 1)
                own.link(act_fn(e8[:, h, :], e8[:, h, :], ACT.Exp, scale=-1.0))
            for h in range(8):
                act_fn(e8[:, h, :], e8[:, h, :], ACT.Ln, bias=1.0).then_inc(sig("sb_ln"), 1)
            fill_cut(17)
            fill_evac(16)
            fill_evac(17)
            fill_cut(18)
            fill_evac(18)
            for t in range(10):
                if t < 8:
                    wait_drained(act, ("sbo", ("b", t)))
                    act_fn(z8[:, t, :], z8[:, t, :], ACT.Exp).then_inc(sig("sb_exp"), 1)
                if t >= 2 and (t + 1) % 2 == 0:
                    key = ("sbo", ("o", t))
                    bank = wait_filled(act, key)
                    act_fn(yh[:, 4 + (t - 3) // 2, :], bank[:, 0:T], ACT.Copy).then_inc(sig("sbo_hi"), 1)
                for key, i in SB_FILLS.items():
                    if key[1] == t:
                        fill_cut(i)
                        fill_evac(i)

            for t in range(4 + 3):
                if 0 <= t - 2 < 4:
                    key_major("mem", t - 2, 512)
                if 0 <= t - 3:
                    bank = wait_filled(act, ("mem", ("o", t - 3)))
                    act_fn(yh[:, 8 + t - 3, :], bank[:, 0:T], ACT.Copy).then_inc(sig("memo_hi"), 1)
                if t < 4:
                    probabilities("mem", t, (slice(0, T), slice(T, 2 * T)))
                if t == 1:
                    act.wait_ge(sig("y_done"), 1)
                    act_fn(yh[:, 0:4, :], yy[:, :, :], ACT.Copy).then_inc(sig("y_hi"), 1)
                for i in MEM_TURNS.get(t, []):
                    fill_cut(i)
                    fill_evac(i)

            for b in range(4):
                wait_side_drained(act, ("gate", FILLED_GATES - 4 + b))
            filled_gates = flat(gates[:, GATE_ORDER[0]:GATE_ORDER[0] + FILLED_GATES, :])
            act_fn(filled_gates, filled_gates, ACT.Sigmoid).then_inc(sig("gates_sigm"), 1)
            for j in range(FILLED_GATES, 24):
                cuts("gate", j)
                bank = wait_side_filled(act, ("gate", j))
                side_drain(act_fn(gates[:, GATE_ORDER[j], :], bank[:, 0:T], ACT.Sigmoid), ("gate", j))
            for r in range(10):
                cuts("branch", r)
            cut_x(res, lambda c: cuts("branch", 10 + c) if c < 2 else None, merged=True)
            for j in range(DC):
                if j < DC - 1:
                    cuts("out", j)
                if j:
                    square_chunk("out", x, j - 1)
            square_chunk("out", x, DC - 1)
            cuts("out", DC - 1)
            root()
            cut_x(res)

            act.wait_ge(sig("cg_zero"), 2)

            def first_tap(dst, bank, f, it, is_value):
                col = f + (FC2 if is_value else 0)
                scale, shift = [par[:, PCOL[name] + col:PCOL[name] + col + 1] if it is None else
                                par[:, bass.ds(it * 4 + (PCOL[name] + col), 1)] for name in ("conv2", "conv_b")]
                return act_fn(dst, bank[:, 0:T], ACT.Identity, scale=scale, bias=shift)

            def ffn_gate(f, it=None):
                bank = wait_filled(act, ("ffn", 2 * f), it, 8)
                act_fn(cg[:, f % 2, 2:T + 2], bank[:, 0:T], ACT.Copy).then_inc(sig("gate_in"), 1)
                first_tap(fa[:, f % 2, :], bank, f, it, False).then_inc(sig("gate_in"), 1)

            def ffn_value(f, it=None):
                bank = wait_filled(act, ("ffn", 2 * f + 1), it, 8)
                act_fn(cv[:, f % 2, 2:T + 2], bank[:, 0:T], ACT.Copy).then_inc(sig("value_in"), 1)
                first_tap(fb[:, f % 2, :], bank, f, it, True).then_inc(sig("value_in"), 1)
                wait_drained(act, ("ffn", 2 * f), it, 8)
                act_fn(fs[:, f % 2, :], fa[:, f % 2, :], ACT.Sigmoid).then_inc(sig("sigm"), 1)
                cuts("ffn", 3 * f + 1, it, 12)
                act.wait_ge(sig("ffn_prod"), f + 1 if it is None else it * 4 + (f + 1))
                act_fn(hh[:, f % 2, :], hb[:, f % 2, :], ACT.Copy).then_inc(sig("ffn_hi"), 1)

            cuts("ffn", 0)
            ffn_gate(0)
            ffn_value(0)

            def ffn_step(f, it=None):
                cuts("ffn", 3 * f + 2, it, 12)
                ffn_gate(f + 1, it)
                cuts("ffn", 3 * f + 3, it, 12)
                ffn_value(f + 1, it)

            rounds = (FC2 - 1) // 4
            with act.Fori(0, rounds) as it:
                for f in range(4):
                    ffn_step(f, it)
            for f in range(4 * rounds, FC2 - 1):
                ffn_step(f)
        @block.vector
        def _(dve):
            own = Tally(dve, sig("dve_step"))
            tt, ts, stt = nc.vector.tensor_tensor, nc.vector.tensor_scalar, nc.vector.scalar_tensor_tensor
            count = {"x_hi": 0, "scaled": 0, "squared": 0, "odd": 0, "ready": {"rms1": 4, "rms2": 8}}

            def cut(n, it=None, per=0):
                if n >= NSLOT:
                    return
                dve.wait_ge(cut_hi, n + 1 if it is None else it * per + (n + 1))
                tt(wlo[:, n % RING, :], raw[:, n % RING, :], whi[:, n % RING, :].bitcast(F32), ALU.subtract).then_inc(cut_lo, 1)

            def cuts(stage, s, it=None, per=0):
                cut(SLOT[stage] + s + AHEAD, it, per)

            def fill_cut(i):
                cuts("sbqk", i)

            def minus(dst, src, hi):
                return tt(dst, src, hi.bitcast(F32), ALU.subtract)

            def finish(ins, key):
                drain(ins, key)
                wait_drained(dve, key)

            def norm_stats(name, centred=True):
                s = stat[:, 0, :]
                bank = wait_filled(dve, (name, 0))
                if centred:
                    finish(ts(s[:, 0:4], bank[:, 0:512:P], 1.0 / D, None, ALU.mult), (name, 0))
                    own.link(tt(s[:, 4:6], s[:, 0:2], s[:, 0:2], ALU.mult))
                    own.link(stt(s[:, 6:8], s[:, 2:4], LN_EPS, s[:, 4:6], ALU.add, ALU.subtract))
                else:
                    finish(ts(s[:, 6:8], bank[:, 0:T:P], 1.0 / D, RMS_EPS, ALU.mult, ALU.add), (name, 0))
                nc.vector.reciprocal(s[:, 6:8], s[:, 6:8]).then_inc(sig("rinv"), 1)

            def two(ap):
                return ap.broadcast_to([P, 2, T])

            def low_x(src, c):
                count["x_hi"] += 1
                dve.wait_ge(sig("x_hi"), count["x_hi"])
                minus(xl[:, 2 * c:2 * c + 2, :], src[:, 2 * c:2 * c + 2, :], xh[:, 2 * c:2 * c + 2, :]).then_inc(sig("x_normed"), 1)

            def layer_norm(name, g, b, col, cut_after=True, cuts_meanwhile=None):
                norm_stats(name)
                if cuts_meanwhile:
                    cuts_meanwhile()
                mean = wait_filled(dve, (name, 1))[:, 0:T].rearrange("p (a t) -> p a t", a=1)

                def centre(c):
                    pair = res[:, 2 * c:2 * c + 2, :]
                    ins = tt(pair, pair, two(mean), ALU.subtract)
                    if c == 3:
                        finish(ins, (name, 1))
                    else:
                        own.link(ins)

                centre(0)
                centre(1)
                rstd = wait_filled(dve, (name, 2))[:, 0:T].rearrange("p (a t) -> p a t", a=1)
                for c in range(5):
                    if 0 < c < 3:
                        centre(c + 1)
                    if c < 4:
                        pair = res[:, 2 * c:2 * c + 2, :]
                        ins = tt(pair, pair, two(rstd), ALU.mult)
                        count["scaled"] += c < 3
                        if c < 3:
                            ins.then_inc(sig("scaled"), 1)
                        else:
                            finish(ins, (name, 2))
                        if odd_on_dve(c):
                            dve.wait_ge(sig("scaled"), count["scaled"])
                            d = 2 * c + 1
                            ts(x[:, d, :], res[:, d, :], G(g, col + d), G(b, col + d), ALU.mult, ALU.add).then_inc(sig("x_odd"), 1)
                            count["odd"] += 1
                    if c and cut_after:
                        low_x(x, c - 1)
                if not cut_after:
                    count["squared"] += DC

            def add_squares(c, last=False):
                dve.wait_ge(sig("squared"), count["squared"] + 2 * c + 2)
                first = sqr[:, 0:2, :] if c == 1 else ha[:, :, :]
                ins = tt(ha[:, :, :], first, sqr[:, 2 * c:2 * c + 2, :], ALU.add)
                if last:
                    ins.then_inc(sig("added"), 1)
                else:
                    own.link(ins)
                if c == 3:
                    count["squared"] += DC

            def add_chunk(a, src, c, last=False):
                if a:
                    dve.wait_ge(sig("squared"), count["squared"] + c + 1)
                if c:
                    ins = tt(ha[:, a, :], src[:, 0, :] if c == 1 else ha[:, a, :], src[:, c, :], ALU.add)
                    if last:
                        ins.then_inc(sig("added"), 1)
                    else:
                        own.link(ins)
                if a and c == DC - 1:
                    count["squared"] += DC

            def rms_norm(name, g, cuts_meanwhile=None):
                norm_stats(name, False)
                if cuts_meanwhile:
                    cuts_meanwhile()
                rstd = wait_filled(dve, (name, 1))
                for c in range(5):
                    if c < 4:
                        for d in range(2):
                            last = stt(res[:, 2 * c + d, :], x[:, 2 * c + d, :], G(g, 2 * c + d), rstd[:, 0:T], ALU.mult, ALU.mult)
                        last.then_inc(sig("x_ready"), 1)
                    if c:
                        low_x(res, c - 1)
                dve.wait_ge(sig("x_ready"), count["ready"][name])
                drain(nc.vector.memset(stat[:, 0, 10:11], 0.0), (name, 1))

            for c in range(4):
                dve.wait_ge(sig("x0_hi"), c + 1)
                pair = slice(2 * c, 2 * c + 2)
                minus(xl[:, pair, :], x[:, pair, :], xh[:, pair, :]).then_inc(sig("x_cut"), 1)
                if c == 0:
                    cut(0)
            for n in range(1, AHEAD):
                cut(n)
            dve.wait_ge(sig("par_loaded"), 16)
            own.link(ts(nsink[:, :], par[:, PCOL["sinks"]:PCOL["sinks"] + 16], -1.0, None, ALU.mult))
            bank = wait_filled(dve, ("brow", 0))
            dve.wait_ge(sig("band_loaded"), 32)
            drain(tt(brow, bank[0:16, 0:384], bandt[0:16, 1, :], ALU.add), ("brow", 0))
            dve.wait_ge(sig("con_loaded"), 16)
            for j in range(7):
                cuts("in", j)
                if j < 5:
                    dve.wait_ge(sig("in_sq"), j + 1)
                    drain(nc.vector.tensor_copy(hraw[:, j, :], work[RESULT[("in", j)] % 4][:, 0:T]), ("in", j))
                elif j == 5:
                    bank = wait_filled(dve, ("in", 5))
                    drain(tt(ha[:, 0, :], bank[:, 0:T], C("cos", T), ALU.mult), ("in", 5))
                else:
                    bank = wait_filled(dve, ("in", 6))
                    finish(tt(ha[:, 1, :], bank[:, 0:T], C("sin", T), ALU.mult), ("in", 6))
                    wait_drained(dve, ("in", 5))
                    tt(kr[:, :], ha[:, 0, :], ha[:, 1, :], ALU.add).then_inc(sig("kr_ready"), 1)
                if j == 3:
                    bank = wait_filled(dve, ("memstat", 0))
                    finish(ts(mst[:, :], bank[:, 0:T], 1.0 / D, RMS_EPS, ALU.mult, ALU.add), ("memstat", 0))
                    nc.vector.reciprocal(mst[:, :], mst[:, :]).then_inc(sig("mem_inv"), 1)
                if j >= 4:
                    dve.wait_ge(sig("mem_rstd"), 1)
                    for c in ((0, 1), (2,), (3,))[j - 4]:
                        own.link(stt(memc(2 * c), memc(2 * c), G("mem_g", 2 * c), mst[:, :], ALU.mult, ALU.mult))
                        stt(memc(2 * c + 1), memc(2 * c + 1), G("mem_g", 2 * c + 1), mst[:, :], ALU.mult, ALU.mult)\
                            .then_inc(sig("mem_ready"), 1)
                for c in {5: (0, 1), 6: (2, 3)}.get(j, ()):
                    dve.wait_ge(sig("mem_hi"), c + 1)
                    minus(meml[:, 2 * c:2 * c + 2, :], mem2(c), memh[:, 2 * c:2 * c + 2, :]).then_inc(sig("mem_cut"), 1)
            cuts("memk", 0)
            bank = wait_filled(dve, ("mlastat", 0))
            own.link(ts(stat[:, 0, :], bank[:, 0:T], 1.0 / Q_RANK, RMS_EPS, ALU.mult, ALU.add))
            finish(ts(stat[:, 1, :], bank[:, T:2 * T], 1.0 / KV_RANK, RMS_EPS, ALU.mult, ALU.add), ("mlastat", 0))
            nc.vector.reciprocal(stat[:, 0:2, :], stat[:, 0:2, :]).then_inc(sig("mla_inv"), 1)
            dve.wait_ge(sig("mla_rstd"), 1)
            for j in range(3):
                wait_drained(dve, ("in", j))
                last = stt(hraw[:, j, :], hraw[:, j, :], G("g_q", j), stat[:, 2, :], ALU.mult, ALU.mult)
            last.then_inc(sig("cq_ready"), 1)
            for j in range(2):
                wait_drained(dve, ("in", 3 + j))
                stt(ckv[:, j, :], hraw[:, 3 + j, :], G("g_kv", j), stat[:, 3, :], ALU.mult, ALU.mult).then_inc(sig("ckv_ready"), 1)
            dve.wait_ge(sig("cq_hi"), 1)
            minus(flat(cql), flat(hraw[:, 0:3, :]), flat(cqh)).then_inc(sig("cq_cut"), 1)
            for j in range(1, 4):
                cuts("memk", j)
            for j in range(16):
                for s in range(6):
                    if 3 * j <= 8 * s < 3 * j + 3:
                        cuts("q", s)
                key = ("q", j)
                if j < 8:
                    dve.wait_ge(sig("qn_hi"), j + 1)
                    drain(minus(qnl[:, j, :], work[RESULT[key] % 4][:, 0:T], qnh[:, j, :]), key)
                elif j % 2 == 0:
                    bank = wait_filled(dve, key)
                    finish(tt(ha[:, 0, :], bank[:, 0:T], C("cos", T), ALU.mult), key)
                else:
                    bank = wait_filled(dve, key)
                    finish(tt(ha[:, 1, :], bank[:, 0:T], C("sin", T), ALU.mult), key)
                    tt(qr[:, j // 2 - 4, :], ha[:, 0, :], ha[:, 1, :], ALU.add).then_inc(sig("qr_ready"), 1)
                    dve.wait_ge(sig("qr_ready"), j // 2 - 3)
            dve.wait_ge(sig("brow_stored"), 16)
            for h in range(8):
                if h % 4 == 0:
                    cuts("uk", h // 4)
                if h % 2:
                    bank = wait_filled(dve, ("qlat", h))
                    drain(nc.vector.tensor_copy(qlat[:, h, :], bank[:, :]), ("qlat", h))

            def scores(stage, h, parts, scale, added, sink=None, normed=False):
                p = softmax_set(stage, h)
                bank = wait_filled(dve, (stage, ("s", h)))
                n = len(added)
                for a, (cols, extra) in enumerate(added):
                    if normed:
                        ins = ts(score_buffer(stage, h)[:, cols], bank[:, cols], extra, scale, ALU.mult, ALU.mult)
                    else:
                        ins = stt(score_buffer(stage, h)[:, cols], bank[:, cols], scale, extra, ALU.mult, ALU.add)
                    if a == n - 1:
                        finish(ins, (stage, ("s", h)))
                for b, cols in enumerate(parts):
                    last = nc.vector.tensor_reduce(sm[:, p, b:b + 1], score_buffer(stage, h)[:, cols], AX.X, ALU.max, negate=True)
                    if b and sink is not None:
                        own.link(last)
                if sink is not None:
                    last = ts(sm[:, p, 0:2], sm[:, p, 0:2], sink, None, ALU.min)
                last.then_inc(sig(f"{stage}_max"), 1)

            def normalise(stage, h, parts, sink=False):
                p = softmax_set(stage, h)
                dve.wait_ge(sig(f"{stage}_exp"), h + 1)
                if sink:
                    own.link(tt(sm[:, p, 2:4], sm[:, p, 2:4], sm[:, p, 4:6], ALU.add))
                inverse = nc.vector.reciprocal(sm[:, p, 6:8], sm[:, p, 2:4])
                if sink:
                    inverse.then_inc(sig("swa_inverse"), 1)
                    return
                own.link(inverse)
                for b, cols in enumerate(parts):
                    last = ts(probability_buffer(stage, h)[:, cols], probability_buffer(stage, h)[:, cols], sm[:, p, 6 + b:7 + b], None, ALU.mult)
                last.then_inc(sig(f"{stage}_norm"), 1)

            three = (slice(0, P), slice(P, 3 * P))
            for t in range(MLA_H + 4):
                if t < MLA_H:
                    scores("mla", t, three, (NOPE + ROPE) ** -0.5, [(slice(0, 384), C("causal", 384))])
                if 0 <= t - 1 < MLA_H:
                    normalise("mla", t - 1, three)
                if t >= 4:
                    key = ("mla", ("u", t - 4))
                    dve.wait_ge(sig("oh_hi"), t - 3)
                    drain(minus(ol[:, t - 4, :], work[RESULT[key] % 4][:, 0:T], oh[:, t - 4, :]), key)
                if 0 <= t - 3 < MLA_H:
                    key = ("mla", ("o", t - 3))
                    dve.wait_ge(sig("ol_hi"), t - 2)
                    drain(minus(oll[:, :], work[RESULT[key] % 4][:, :], olh[:, :]), key)
                if t >= 4 and t % 4 == 0:
                    cuts("uv", (t - 4) // 4)

            def residual(stage):
                for j in range(DC):
                    if j < DC - 1:
                        cuts(stage, j)
                    bank = wait_filled(dve, (stage, j))
                    finish(stt(res[:, j, :], x[:, j, :], ALPHA, bank[:, 0:T], ALU.mult, ALU.add), (stage, j))
                    add_chunk(0, res, j)
                    if j:
                        add_chunk(1, sqr, j - 1)
                add_chunk(1, sqr, DC - 1, True)

            def mlp(stage, units_before, name):
                def hidden(f, it=None):
                    done = units_before + f + 1
                    n = RESULT[(stage, f)]
                    dve.wait_ge(sig("relu"), done if it is None else it * 4 + done)
                    tt(hb[:, f % 2, :], ha[:, f % 2, :], ha[:, f % 2, :], ALU.mult).then_inc(sig("h_squared"), 1)
                    dve.wait_ge(sig("h_squared"), done if it is None else it * 4 + done)
                    dve.wait_ge(sig("h_hi"), done if it is None else it * 4 + done)
                    drain(minus(hl[:, f % 2, :], hb[:, f % 2, :], hh[:, f % 2, :]), (stage, f))

                cuts(stage, 0)
                hidden(0)

                def step(f, it=None):
                    cuts(stage, 2 * f + 1, it, 8)
                    hidden(f + 1, it)
                    cuts(stage, 2 * f + 2, it, 8)

                rounds = (FC - 1) // 4
                with dve.Fori(0, rounds) as it:
                    for f in range(4):
                        step(f, it)
                for f in range(4 * rounds, FC - 1):
                    step(f)
                cuts(stage, 2 * FC - 1)
                for b in range(4):
                    dve.wait_ge(sig("acc_full"), 4 * (units_before // FC) + b + 1)
                    stt(res[:, 2 * b:2 * b + 2, :], x[:, 2 * b:2 * b + 2, :], ALPHA, acc[b][:, :].rearrange("p (a t) -> p a t", a=2),
                        ALU.mult, ALU.add).then_inc(sig(f"{name}_sum"), 1)
                dve.wait_ge(sig(f"{name}_sum"), 4)
                for c in range(1, 4):
                    add_squares(c, c == 3)

            residual("wo")
            def cuts_for_ln0():
                cuts("wo", DC - 1)
                cuts("memva", 0)
            layer_norm("ln0", "ln_mix_g", "ln_mix_b", 0, True, cuts_for_ln0)
            cuts("memva", 1)
            mlp("mlp0", 0, "ln1")
            layer_norm("ln1", "ln_mlp_g", "ln_mlp_b", 0, True, lambda: cuts("memvb", 0))
            cuts("memvb", 1)
            for j in range(8):
                cuts("swaq", j)
            for j in range(2):
                cuts("swak", j)
            for j in range(2):
                cuts("swav", j)
            dve.wait_ge(sig("bias_loaded"), 16)
            for t in range(SWA_H + 5):
                if t < SWA_H:
                    h = SWA_ORDER[t]
                    scores("swa", t, three, SWA_D ** -0.5, [(slice(0, P), bias[:, h, P - 1::-1]), (slice(P, 384), bias[:, h, ::-1])],
                           nsink[:, h:h + 1])
                if 0 <= t - 1 < SWA_H:
                    normalise("swa", t - 1, three, True)
                if 0 <= t - 5 and (t - 5) % 2:
                    pair = (t - 5) // 2
                    dve.wait_ge(sig("oh_hi"), 8 + pair + 1)
                    minus(ol[:, pair, :], acc[pair % 4][:, 0:T], oh[:, pair, :]).then_inc(sig("swa_cut"), 1)
            residual("swao")
            layer_norm("ln2", "ln_mix_g", "ln_mix_b", 8, True, lambda: cuts("swao", DC - 1))
            mlp("mlp1", FC, "ln3")
            layer_norm("ln3", "ln_mlp_g", "ln_mlp_b", 8, False)
            dve.wait_ge(sig("x_made"), 16)
            dve.wait_ge(sig("x_odd"), count["odd"])

            rms_norm("rms1", "norm1")
            dve.wait_ge(sig("pb_zero"), 2)
            for j in range(14):
                cuts("rwkv", j)
                dve.wait_ge(sig("pb_full"), j + 1)
                own.link(tt(ha[:, j % 2, :], pb[:, j % 2, 0:T], pb[:, j % 2, 1:T + 1], ALU.subtract))
                drain(stt(projected(j), ha[:, j % 2, :], G("mu", j), pb[:, j % 2, 1:T + 1], ALU.mult, ALU.add), ("rwkv", j))
            for j in range(12):
                wait_drained(dve, ("rwkv", j))
            for c in range(4):
                last = ts(kk[:, c, :], k_[:, c, :], G("k_k", c), None, ALU.mult)
                if c < 3:
                    own.link(last)
            last.then_inc(sig("kk_raw"), 1)
            fill_cut(0)
            for j in range(2):
                wait_drained(dve, ("loraw", j))
            for c in range(8):
                own.link(nc.vector.tensor_tensor_scan(out=cum[:, c, 1:129], data0=ones, data1=em[:, c, :], initial=0.0,
                                                      op0=ALU.mult, op1=ALU.add))
            own.link(ts(mid[:, 0, :], cum[:, :, 64], KAPPA, None, ALU.mult))
            own.link(ts(mid[:, 1, :], cum[:, :, 64], -KAPPA, None, ALU.mult))
            ts(mid[:, 2, :], cum[:, :, 64], 1.0, None, ALU.mult).then_inc(sig("cum_ready"), 1)
            dve.wait_ge(sig("cum_ready"), 1)
            halves = cum[:, :, :].rearrange("p (c a) t -> p c a t", a=2)
            own.link(tt(fac[:, :], halves[:, :, 0, 128], halves[:, :, 0, 64], ALU.subtract))
            tt(fac[:, :], fac[:, :], halves[:, :, 1, 64], ALU.add).then_inc(sig("fac_ready"), 1)
            bank = wait_filled(dve, ("kkstat", 0))
            finish(ts(hst[:, 2, 0:16], bank[:, 0:512:32], 1e-24, None, ALU.max), ("kkstat", 0))
            nc.vector.reciprocal(hst[:, 2, 0:16], hst[:, 2, 0:16]).then_inc(sig("kk_inv"), 1)
            for j in range(2):
                wait_drained(dve, ("loraa", j))
            for c in range(4):
                own.link(ts(sqr[:, 4 + c, :], aa[:, c, :], -1.0, G("k_a", c), ALU.add, ALU.mult))
            own.link(stt(k_[:, :, :], sqr[:, 4:8, :], 1.0, k_[:, :, :], ALU.add, ALU.mult))
            for c in range(4):
                last = stt(sqr[:, 4 + c, :], r_[:, c, :], G("r_k", c), k_[:, c, :], ALU.mult, ALU.mult)
                if c < 3:
                    own.link(last)
            last.then_inc(sig("rk_prod"), 1)
            for j in range(2):
                bank = wait_filled(dve, ("bonus", j))
                drain(tt(bon[:, 2 * j:2 * j + 2, :], v_[:, 2 * j:2 * j + 2, :], bank[:, :].rearrange("p (a t) -> p a t", a=2), ALU.mult), ("bonus", j))
            for j in range(2):
                bank = wait_filled(dve, ("kkspread", j))
                part = kk[:, 2 * j:2 * j + 2, :]
                finish(tt(part, part, bank[:, :].rearrange("p (a t) -> p a t", a=2), ALU.mult), ("kkspread", j))
            dve.wait_ge(sig("exps"), 1)

            def factors(tc):
                fall, rise = ep[:, tc:8:2, :], em[:, tc:8:2, :]
                own.link(tt(aa[:, :, half(tc)], aa[:, :, half(tc)], kk[:, :, half(tc)], ALU.mult))
                tt(kk[:, :, half(tc)], kk[:, :, half(tc)], fall[:, :, 0:128], ALU.mult)
                tt(r_[:, :, half(tc)], r_[:, :, half(tc)], fall[:, :, 1:129], ALU.mult)
                tt(aa[:, :, half(tc)], aa[:, :, half(tc)], rise, ALU.mult)
                tt(k_[:, :, half(tc)], k_[:, :, half(tc)], rise, ALU.mult).then_inc(sig("factors"), 1)

            factors(0)
            fill_cut(1)
            fill_cut(2)
            factors(1)
            dve.wait_ge(sig("fac_exp"), 1)
            dve.wait_ge(sig("factors"), 2)
            fill_cut(3)
            dve.wait_ge(sig("con2_loaded"), 16)
            bank = wait_filled(dve, ("sbqstat", 0))
            finish(ts(hst[:, 0, 0:16], bank[:, 0:512:32], 1.0 / RW_D, RMS_EPS, ALU.mult, ALU.add), ("sbqstat", 0))

            def level_mask(l, g):
                tt(four(sc[:, g, :]), four(at[:, g, :]), mask4(C("level", P, l * P)), ALU.mult).then_inc(sig("inv_mask"), 1)

            for tc in range(2):
                for g in range(2):
                    def masked(m, dst, mask, *_):
                        key = (f"mat{tc}", (m, g))
                        bank = wait_filled(dve, key)
                        finish(tt(four(dst), four(bank[:, :]), mask4(mask), ALU.mult), key)
                    masked("at", at[:, g, :], C("before"))
                    own.link(tt(four(uinv[:, g, :]), four(at[:, g, :]), mask4(C("level")), ALU.mult))
                    own.link(tt(four(uinv[:, g, :]), mask4(C("ident")), four(uinv[:, g, :]), ALU.subtract))
                    masked("a0", tinv[:, g, :], C("level0t"))
                    own.link(tt(four(tinv[:, g, :]), mask4(C("ident")), four(tinv[:, g, :]), ALU.subtract))
                    level_mask(1, g)
                for l in range(1, 7):
                    for g in range(2):
                        if l < 6:
                            wait_drained(dve, (f"inv{tc}", (l, "h", g)))
                            level_mask(l + 1, g)
                    if l < 4:
                        m, dst, mask = (("kk", kkm, "before"), ("rb", rb, "upto"), ("rk", rk, "upto"))[l - 1]
                        for g in range(2):
                            wait_drained(dve, (f"mat{tc}", (m, g)))
                            last = tt(four(dst[:, g, :]), four(dst[:, g, :]), mask4(C(mask)), ALU.mult)
                        last.then_inc(sig("mats_masked"), 1)
                    if tc == 0:
                        fill_cut(3 + l)
                    elif l < 6:
                        fill_cut(10 + l)
                    if (tc, l) == (1, 1):
                        bank = wait_filled(dve, ("sbstat", 0))
                        finish(ts(hst[:, 0, 16:32], bank[:, 0:512:32], 1.0, RMS_EPS * RW_D, ALU.mult, ALU.add), ("sbstat", 0))
                        nc.vector.reciprocal(hst[:, 0, :], hst[:, 0, :]).then_inc(sig("sb_inv"), 1)
                    for g in range(2):
                        if l < 6:
                            key = (f"inv{tc}", (l, "d", g))
                            bank = wait_filled(dve, key)
                            half_ = half_columns(tinv[:, g, :], l, False)
                            finish(tt(half_, half_, half_columns(bank[:, :], l, False), ALU.subtract), key)
                        key = (f"inv{tc}", (l, "dt", g))
                        bank = wait_filled(dve, key)
                        half_ = half_columns(uinv[:, g, :], l, True)
                        finish(tt(half_, half_, half_columns(bank[:, :], l, True), ALU.subtract), key)
                    if (tc, l) == (1, 3):
                        for j in range(2):
                            bank = wait_filled(dve, ("sbspread", j))
                            part = sbq[:, 2 * j:2 * j + 2, :]
                            ins = stt(part, part, G("sbq_g"), bank[:, :].rearrange("p (a t) -> p a t", a=2), ALU.mult, ALU.mult)
                            finish(ins, ("sbspread", j))
                for g in range(2):
                    key = (f"end{tc}", f"rhs{g}")
                    bank = wait_filled(dve, key)
                    drain(ts(rhs[:, g * T:(g + 1) * T], bank[:, 0:T], -1.0, None, ALU.mult), key)
                if tc == 0:
                    fill_cut(10)
                else:
                    bank = wait_filled(dve, ("memstat2", 0))
                    finish(ts(hst[:, 1, 0:16], bank[:, 0:512:32], 1.0 / P, RMS_EPS, ALU.mult, ALU.add), ("memstat2", 0))
                    nc.vector.reciprocal(hst[:, 1, 0:16], hst[:, 1, 0:16]).then_inc(sig("mem_inv2"), 1)
                key = (f"end{tc}", "y")
                bank = wait_filled(dve, key)
                finish(nc.vector.tensor_copy(yy[:, :, half(tc)], four(bank[:, :])), key)
                if tc == 0:
                    key = ("end0", "state")
                    bank = wait_filled(dve, key)
                    for c in range(4):
                        last = ts(st[:, c, :], bank[:, c * 64:c * 64 + 64], fac[:, c:c + 1], None, ALU.mult)
                    drain(last, key)

            def sbz(h):
                wait_drained(dve, ("sbz", h))
                stt(e8[:, h, :], z8[:, h, :], -1.0, z8[:, h, :], ALU.mult, ALU.max).then_inc(sig("sb_abs"), 1)

            for h in range(4):
                sbz(h)
            means, variances, squares = hst[:, 3, 0:16], hst[:, 3, 16:32], stat[:, 3, P:P + 16]
            bank = wait_filled(dve, ("ystat", 0))
            finish(ts(hst[:, 3, :], bank[:, 0:512:16], 1.0 / RW_D, None, ALU.mult), ("ystat", 0))
            own.link(tt(squares, means, means, ALU.mult))
            own.link(tt(variances, variances, squares, ALU.subtract))
            own.link(ts(variances, variances, LNX_EPS, None, ALU.add))
            nc.vector.reciprocal(variances, variances).then_inc(sig("y_inv"), 1)
            fill_cut(16)
            for h in range(4, 8):
                sbz(h)
            for j in range(2):
                bank = wait_filled(dve, ("memspread", j))
                part = km[:, 2 * j:2 * j + 2, :]
                finish(stt(part, part, G("memk_g"), bank[:, :].rearrange("p (a t) -> p a t", a=2), ALU.mult, ALU.mult), ("memspread", j))
            for j in range(4):
                bank = wait_filled(dve, ("yspread", j))
                part = yy[:, j % 2 * 2:j % 2 * 2 + 2, :]
                piece = bank[:, :].rearrange("p (a t) -> p a t", a=2)
                if j < 2:
                    ins = stt(part, piece, -1.0 / RW_D, part, ALU.mult, ALU.add)
                else:
                    ins = tt(part, part, piece, ALU.mult)
                finish(ins, ("yspread", j))
            def diagonals(ap):
                b = ap.rearrange("p (a t) -> p a t", t=P)
                return b[:, 0:3:2, :]

            def masked_diagonals(ap):
                return tt(diagonals(ap), diagonals(ap), C("before").rearrange("p (a t) -> p a t", a=1).broadcast_to([P, 2, P]), ALU.mult)

            def softplus(h):
                dve.wait_ge(sig("sb_ln"), h + 1)
                own.link(stt(spc(h), z8[:, h, :], 0.0, e8[:, h, :], ALU.max, ALU.add))
                stt(z8[:, h, :], z8[:, h, :], 0.0, e8[:, h, :], ALU.min, ALU.subtract)
                masked_diagonals(spc(h)).then_inc(sig("softplus"), 1)

            def weight_outputs(c):
                own.link(ts(yy[:, c, :], yy[:, c, :], G("lnx_g", c), G("lnx_b", c), ALU.mult, ALU.add))

            def finish_outputs(step):
                if step < 2:
                    weight_outputs(2 * step)
                    weight_outputs(2 * step + 1)
                elif step == 2:
                    for j in range(2):
                        wait_drained(dve, ("bonus", j))
                    own.link(tt(yy[:, :, :], yy[:, :, :], bon[:, :, :], ALU.add))
                else:
                    for j in range(2):
                        wait_drained(dve, ("lorag", j))
                    tt(yy[:, :, :], yy[:, :, :], gg[:, :, :], ALU.mult).then_inc(sig("y_done"), 1)

            softplus(0)
            softplus(1)
            fill_cut(17)
            fill_cut(18)
            for t in range(10):
                if t < 8:
                    key = ("sbo", ("b", t))
                    bank = wait_filled(dve, key)
                    finish(tt(z8[:, t, :], z8[:, t, :], bank[:, 0:384], ALU.subtract), key)
                if 0 <= t - 1 < 8:
                    dve.wait_ge(sig("sb_exp"), t)
                    masked_diagonals(z8[:, t - 1, :]).then_inc(sig("sb_attn"), 1)
                if t < 6:
                    softplus(t + 2)
                if t >= 3 and t % 2:
                    key = ("sbo", ("o", t))
                    dve.wait_ge(sig("sbo_hi"), (t - 3) // 2 + 1)
                    c = 4 + (t - 3) // 2
                    drain(minus(yl[:, c, :], work[RESULT[key] % 4][:, 0:T], yh[:, c, :]), key)
                for key, i in SB_FILLS.items():
                    if key[1] == t:
                        fill_cut(i)
                if t >= 6:
                    finish_outputs(t - 6)

            dve.wait_ge(sig("mem_norm_rstd"), 1)
            wide = (slice(0, T), slice(T, 2 * T))
            for t in range(4 + 3):
                if t < 4:
                    scores("mem", t, wide, P ** -0.5, [(wide[b], hst[:, 1, 4 * b + t:4 * b + t + 1]) for b in range(2)], normed=True)
                if 0 <= t - 1 < 4:
                    normalise("mem", t - 1, wide)
                if t >= 3:
                    key = ("mem", ("o", t - 3))
                    dve.wait_ge(sig("memo_hi"), t - 2)
                    drain(minus(yl[:, 8 + t - 3, :], work[RESULT[key] % 4][:, 0:T], yh[:, 8 + t - 3, :]), key)
                if t == 1:
                    dve.wait_ge(sig("y_hi"), 1)
                    minus(yl[:, 0:4, :], yy[:, :, :], yh[:, 0:4, :]).then_inc(sig("y_cut"), 1)
                for i in MEM_TURNS.get(t, []):
                    fill_cut(i)

            for j in range(FILLED_GATES, 24):
                cuts("gate", j)
            dve.wait_ge(sig("gates_sigm"), 1)
            for r in range(4):
                wait_side_drained(dve, ("gate", 20 + r))
            for r in range(25):
                if r > 8:
                    before = r - 1
                    tt(res[:, before % 8, :], res[:, before % 8, :], hb[:, before % 2, :], ALU.add).then_inc(sig("merged"), 1)
                if r == 24:
                    break
                if r % 2 == 0:
                    cuts("branch", r // 2)
                bank, key = wait_filled(dve, ("branch", r)), ("branch", r)
                if r >= 10:
                    dve.wait_ge(sig("merged"), r - 9)
                dst = res[:, r, :] if r < 8 else hb[:, r % 2, :]
                finish(tt(dst, gates[:, r, :], bank[:, 0:T], ALU.mult), key)
                if r >= 18 and r % 2 == 0:
                    low_x(res, (r - 18) // 2)
            low_x(res, 3)
            for j in range(DC):
                if j < DC - 1:
                    cuts("out", j)
                bank = wait_filled(dve, ("out", j))
                finish(tt(x[:, j, :], x[:, j, :], bank[:, 0:T], ALU.add), ("out", j))
                if j:
                    add_chunk(1, sqr, j - 1)
            add_chunk(1, sqr, DC - 1, True)
            rms_norm("rms2", "norm2", lambda: cuts("out", DC - 1))

            dve.wait_ge(sig("cg_zero"), 2)

            def conv(dst, src, it, f, is_value):
                def tap(name):
                    col = PCOL[name] + f + (FC2 if is_value else 0)
                    if it is None:
                        return par[:, col:col + 1]
                    return par[:, bass.ds(it * 4 + col, 1)]
                own.link(stt(dst, src[:, 1:T + 1], tap("conv1"), dst, ALU.mult, ALU.add))
                return stt(dst, src[:, 0:T], tap("conv0"), dst, ALU.mult, ALU.add)

            def upto(n, it, per):
                return n if it is None else it * per + n

            def ffn_gate(f, it=None):
                p = f % 2
                dve.wait_ge(sig("gate_in"), upto(2 * f + 2, it, 8))
                drain(conv(fa[:, p, :], cg[:, p, :], it, f, False), ("ffn", 2 * f))

            def ffn_value(f, it=None):
                p = f % 2
                dve.wait_ge(sig("value_in"), upto(2 * f + 2, it, 8))
                own.link(conv(fb[:, p, :], cv[:, p, :], it, f, True))
                wait_drained(dve, ("ffn", 2 * f), it, 8)
                own.link(tt(fb[:, p, :], fb[:, p, :], fa[:, p, :], ALU.mult))
                dve.wait_ge(sig("sigm"), upto(f + 1, it, 4))
                tt(hb[:, p, :], fb[:, p, :], fs[:, p, :], ALU.mult).then_inc(sig("ffn_prod"), 1)
                dve.wait_ge(sig("ffn_hi"), upto(f + 1, it, 4))
                drain(minus(hl[:, p, :], hb[:, p, :], hh[:, p, :]), ("ffn", 2 * f + 1))

            cuts("ffn", 0)
            ffn_gate(0)
            ffn_value(0)
            cuts("ffn", 1)

            def ffn_step(f, it=None):
                cuts("ffn", 3 * f + 2, it, 12)
                ffn_gate(f + 1, it)
                cuts("ffn", 3 * f + 3, it, 12)
                ffn_value(f + 1, it)
                cuts("ffn", 3 * f + 4, it, 12)

            rounds = (FC2 - 1) // 4
            with dve.Fori(0, rounds) as it:
                own.enter(it, 4 * 4)
                for f in range(4):
                    ffn_step(f, it)
                own.leave(rounds)
            for f in range(4 * rounds, FC2 - 1):
                ffn_step(f)
            for b in range(4):
                dve.wait_ge(sig("acc_full"), 8 + b + 1)
                tt(res[:, 2 * b:2 * b + 2, :], x[:, 2 * b:2 * b + 2, :], acc[b][:, :].rearrange("p (a t) -> p a t", a=2), ALU.add)\
                    .then_inc(sig("final"), 1)


def _tiles(m):
    return m.reshape(m.shape[0] // P, P, m.shape[1] // P, P)


def _columns(m):
    t = _tiles(m).transpose(2, 1, 0, 3)
    return t.reshape(-1, P, 1024)


def _rows(m):
    t = m.reshape(m.shape[0] // P, P, m.shape[1]).transpose(1, 0, 2).reshape(P, -1, 1024)
    return t.transpose(1, 0, 2)


def _packed(tiles):
    t = np.stack(tiles).reshape(-1, 8, P, P).transpose(0, 2, 1, 3)
    return t.reshape(-1, P, 1024)


def _stream(i):
    swap = np.r_[32:64, 0:32]
    w_in = i["mla_w_in"][0]
    kr = w_in[:, Q_RANK + KV_RANK:]
    parts = {"in": _columns(np.concatenate([w_in[:, :Q_RANK + KV_RANK], kr, kr, kr[:, swap], kr[:, swap]], 1))}
    mem = i["w_mem_kv_2"][0]
    parts["memk"] = _columns(mem[:, :512])
    parts["memva"], parts["memvb"] = _rows(mem[:, 512:768]), _rows(mem[:, 768:])
    uq = i["mla_w_uq"][0]
    nope = [uq[:, h, :NOPE] for h in range(MLA_H)]
    rope = uq[:, :, NOPE:]
    pairs = []
    for c in range(4):
        for r in (rope, rope[:, :, swap]):
            pairs.append(r[:, 2 * c:2 * c + 2].reshape(Q_RANK, P))
    parts["q"] = _packed([m[k * P:(k + 1) * P] for m in nope + pairs for k in range(3)])
    uk = i["mla_w_uk"][0].transpose(1, 2, 0)
    parts["uk"] = _packed([uk[h, :, c * P:(c + 1) * P] for h in range(MLA_H) for c in range(2)])
    uv = i["mla_w_uv"][0]
    parts["uv"] = _packed([uv[c * P:(c + 1) * P, h, :] for h in range(MLA_H) for c in range(2)])
    parts["wo"] = _columns(i["mla_w_o"][0])
    for l in range(2):
        up, down = _columns(i["mlp_w_up"][l]), _rows(i["mlp_w_down"][l])
        order = [up[0]]
        for f in range(FC - 1):
            order += [up[f + 1], down[f]]
        parts[f"mlp{l}"] = np.stack(order + [down[-1]])
    q = i["swa_w_q"][0].reshape(D, SWA_H, SWA_D)[:, SWA_ORDER].reshape(D, D)
    parts["swaq"] = _columns(q)
    parts["swak"] = _columns(i["kv_w_shared"][:, :256])
    parts["swav"] = _rows(i["kv_w_shared"][:, 256:])
    parts["swao"] = _columns(i["swa_w_o"][0].reshape(SWA_H, SWA_D, D)[SWA_ORDER].reshape(D, D))
    w = i["w_in_2"][0]
    cols = [w[:, 512:1024], w[:, 0:512], w[:, 1024:1792]]
    parts["rwkv"] = _columns(np.concatenate(cols, 1))
    parts["sbqk"] = _columns(w[:, 1792:2816])
    parts["sbv"] = _rows(w[:, 2816:3328])
    parts["memq"] = _columns(w[:, 3328:3840])
    parts["gate"] = _columns(w[:, 3840:])[GATE_ORDER]
    br = i["w_branch_2"][0]
    parts["branch"] = _packed([br[n, k * P:(k + 1) * P, c * P:(c + 1) * P] for n in range(3) for c in range(DC) for k in range(4)])
    parts["out"] = _columns(i["w_out_2"][0])
    up, down = _columns(i["w_up_2"][0]), _rows(i["w_down_2"][0])
    order = [up[0], up[FC2]]
    for f in range(FC2 - 1):
        order += [up[f + 1], up[FC2 + f + 1], down[f]]
    parts["ffn"] = np.stack(order + [down[-1]])
    for name, n in STREAM:
        assert parts[name].shape[0] == n, name
    return np.ascontiguousarray(np.concatenate([parts[name] for name, _ in STREAM]))


def _params(i):
    mu = i["shift_mu_2"][0]
    mu = np.concatenate([mu[512:1024], mu[0:512], mu[1024:]])
    conv = i["conv_w_2"][0]
    rows = {"g_q": i["mla_g_q"], "g_kv": i["mla_g_kv"], "ln_mix_g": i["ln_mix_g"], "ln_mix_b": i["ln_mix_b"],
            "ln_mlp_g": i["ln_mlp_g"], "ln_mlp_b": i["ln_mlp_b"], "norm1": i["norm1_g_2"], "mu": mu,
            "w0": i["decay_w0_2"], "a0": i["iclr_a0_2"], "k_k": i["k_k_2"], "k_a": i["k_a_2"], "r_k": i["r_k_2"],
            "lnx_g": i["lnx_g_2"], "lnx_b": i["lnx_b_2"], "sbq_g": np.tile(i["sb_q_norm_g_2"], (1, 2)),
            "sbk_g": np.tile(i["sb_k_norm_g_2"], (1, 2)), "mem_g": i["mem_norm_g_2"], "memq_g": i["mem_q_norm_g_2"],
            "memk_g": i["mem_k_norm_g_2"], "norm2": i["norm2_g_2"], "conv0": conv[0], "conv1": conv[1],
            "conv2": conv[2], "conv_b": i["conv_b_2"]}
    cols = [rows[name].reshape(-1, P).T if name in rows else np.tile(i["swa_sinks"][0], (P, 1)) for name, _ in PARAMS]
    return np.ascontiguousarray(np.concatenate(cols, 1))


def kernel(**inputs):
    import concourse.bacc as bacc
    from concourse.bass_utils import run_bass_kernel_spmd

    i = {name: np.asarray(a) for name, a in inputs.items()}

    def feature_major(a):
        return np.ascontiguousarray(a.reshape(T, DC, P).transpose(2, 1, 0))

    table, band = constants()
    arrays = {
        "weights": _stream(i),
        "x_t": feature_major(i["x"][0]),
        "mem_t": feature_major(i["mem_2"][0]).reshape(P, DC * T),
        "table": table,
        "band_rows": band,
        "params": _params(i),
        "lora_w": np.ascontiguousarray(np.concatenate([i["decay_w2_2"][0], i["iclr_a2_2"][0]], 0)),
        "gate_w": np.ascontiguousarray(i["gate_g2_2"][0]),
        "rel_bias_w": np.ascontiguousarray(i["rel_bias"]),
    }
    nc = bacc.Bacc("TRN2", target_bir_lowering=False, num_devices=1)
    args = [nc.dram_tensor(name, a.shape, F32, kind="ExternalInput").ap() for name, a in arrays.items()]
    out = nc.dram_tensor("out_t", (P, DC, T), F32, kind="ExternalOutput").ap()
    build(nc, *args, out)
    result = run_bass_kernel_spmd(nc, [arrays], core_ids=[0]).results[0]["out_t"]
    return np.ascontiguousarray(np.asarray(result).transpose(2, 1, 0).reshape(1, T, D))
```
